# Optimizing a Trainium2 kernel written in Bass

```python
import math
import jax, jax.numpy as jnp
from jax import lax
import numpy as np

D_MODEL = 1024
BATCH = 1
SEQ = 1024
DEPTH = 2
DEC_BATCH = 1
DEC_SEQ = 64
PAST_LEN = 256

CHUNK = 64
N_EVEN = (DEPTH + 1) // 2
N_ODD = DEPTH // 2
ROPE_THETA = 10000.0
EPS = 1e-5
A_HEADS = 4
A_DH = 64
A_WIDTH = A_HEADS * 2 * A_DH
Q_BLOCK = 128
POOL_WINDOWS = (2, 4, 8, 16)
POOL_GROUPS = len(POOL_WINDOWS)
B_WIDTH = D_MODEL - A_WIDTH
POOL_CH = B_WIDTH // POOL_GROUPS
POOL_HIST = max(POOL_WINDOWS) - 1
EVEN_IN = 3 * A_WIDTH + B_WIDTH
C_HEADS = 16
C_KV = 2
C_DH = D_MODEL // C_HEADS
C_GROUP = C_HEADS // C_KV
WINDOW = 128
WIN_CHUNKS = WINDOW // CHUNK
C_CACHE = min(WINDOW, PAST_LEN)
ODD_IN = C_HEADS * C_DH + 2 * C_KV * C_DH
D_FF = 2816
CONV_W = 3

kernel_name = 'hybrid_stream_encoder_step'

def rmsnorm(x, g):
    xf = x.astype(jnp.float32)
    y = xf * lax.rsqrt(jnp.mean(xf * xf, axis=-1, keepdims=True) + EPS)
    return (y * g.astype(jnp.float32)).astype(x.dtype)

def rope(x, pos):
    d = x.shape[-1]
    inv = ROPE_THETA ** (-jnp.arange(0, d, 2, dtype=jnp.float32) / d)
    ang = pos.astype(jnp.float32)[:, None] * inv[None, :]
    shape = (ang.shape[0],) + (1,) * (x.ndim - 3) + (d // 2,)
    cos = jnp.cos(ang).reshape(shape)
    sin = jnp.sin(ang).reshape(shape)
    xf = x.astype(jnp.float32)
    x1, x2 = xf[..., :d // 2], xf[..., d // 2:]
    return jnp.concatenate([x1 * cos - x2 * sin, x2 * cos + x1 * sin], axis=-1).astype(x.dtype)

def diff_core(q, k, v, lam, mask):
    s = jnp.einsum('bqhmd,bkhmd->bhmqk', q, k).astype(jnp.float32) * (A_DH ** -0.5)
    if mask is not None:
        s = jnp.where(mask, s, -jnp.inf)
    p = jax.nn.softmax(s, axis=-1)
    a = p[:, :, 0] - lam * p[:, :, 1]
    return jnp.einsum('bhqk,bkhe->bqhe', a.astype(v.dtype), v)

def diff_attn_prompt(q, k, v, lam):
    B, S = q.shape[:2]
    nb = S // Q_BLOCK
    qb = q.reshape(B, nb, Q_BLOCK, A_HEADS, 2, A_DH).swapaxes(0, 1)
    k_chunk = jnp.arange(S) // CHUNK

    def one(args):
        q_blk, bi = args
        q_chunk = (bi * Q_BLOCK + jnp.arange(Q_BLOCK)) // CHUNK
        mask = k_chunk[None, :] <= q_chunk[:, None]
        return diff_core(q_blk, k, v, lam, mask)

    out = lax.map(one, (qb, jnp.arange(nb)))
    return out.swapaxes(0, 1).reshape(B, S, A_HEADS, 2 * A_DH)

def pool_mix(u, hist, n_hist, w, scale):
    B, S, _ = u.shape
    ext = jnp.concatenate([hist, u], axis=1).astype(jnp.float32)
    cs = jnp.concatenate([jnp.zeros_like(ext[:, :1]), jnp.cumsum(ext, axis=1)], axis=1)
    end = cs[:, POOL_HIST + 1:]
    t = jnp.arange(S, dtype=jnp.float32)
    outs = []
    for g, win in enumerate(POOL_WINDOWS):
        sl = slice(g * POOL_CH, (g + 1) * POOL_CH)
        start = cs[:, POOL_HIST + 1 - win: POOL_HIST + 1 - win + S, sl]
        cnt = jnp.minimum(float(win), t + 1.0 + n_hist)[None, :, None]
        outs.append((end[..., sl] - start) / cnt)
    pooled = (jnp.concatenate(outs, axis=-1) - u.astype(jnp.float32)).astype(u.dtype)
    y = jnp.einsum('bsgc,gcd->bsgd', pooled.reshape(B, S, POOL_GROUPS, POOL_CH), w)
    return y.reshape(B, S, B_WIDTH) * scale, ext[:, -POOL_HIST:].astype(u.dtype)

def even_mixer(h, pos, k_cache, v_cache, pool_hist, n_hist, w_in, w_out, lam_p, subln, pool_w, pool_scale, li):
    B, S, _ = h.shape
    z = h @ w_in
    q, k, v, u = jnp.split(z, [A_WIDTH, 2 * A_WIDTH, 3 * A_WIDTH], axis=-1)
    q = rope(q.reshape(B, S, A_HEADS, 2, A_DH), pos)
    k = rope(k.reshape(B, S, A_HEADS, 2, A_DH), pos)
    v = v.reshape(B, S, A_HEADS, 2 * A_DH)
    lam_init = 0.8 - 0.6 * math.exp(-0.3 * li)
    lp = lam_p.astype(jnp.float32)
    lam = jnp.exp(jnp.sum(lp[0] * lp[1])) - jnp.exp(jnp.sum(lp[2] * lp[3])) + lam_init
    if k_cache is None:
        a = diff_attn_prompt(q, k, v, lam)
    else:
        k_all = jnp.concatenate([k_cache, k], axis=1)
        v_all = jnp.concatenate([v_cache, v], axis=1)
        a = diff_core(q, k_all, v_all, lam, None)
    a = (rmsnorm(a, subln) * (1.0 - lam_init)).reshape(B, S, A_WIDTH)
    p, new_pool = pool_mix(u, pool_hist, n_hist, pool_w, pool_scale)
    out = jnp.concatenate([a, p], axis=-1) @ w_out
    return out, k, v, new_pool

def sink_attend(q, k, v, sink, mask):
    s = jnp.einsum('...qkgd,...jkd->...kgqj', q, k).astype(jnp.float32) * (C_DH ** -0.5)
    if mask is not None:
        s = jnp.where(mask, s, -jnp.inf)
    sk = jnp.broadcast_to(sink.astype(jnp.float32)[:, :, None, None], s.shape[:-1] + (1,))
    p = jax.nn.softmax(jnp.concatenate([s, sk], axis=-1), axis=-1)[..., :-1]
    return jnp.einsum('...kgqj,...jkd->...qkgd', p.astype(v.dtype), v)

def swa_prompt(q, k, v, sink):
    B, S = q.shape[:2]
    nC = S // CHUNK
    qc = q.reshape(B, nC, CHUNK, C_KV, C_GROUP, C_DH)
    pad = WIN_CHUNKS * CHUNK

    def band(t):
        tp = jnp.pad(t, ((0, 0), (pad, 0), (0, 0), (0, 0))).reshape(B, nC + WIN_CHUNKS, CHUNK, C_KV, C_DH)
        return jnp.concatenate([tp[:, i:i + nC] for i in range(WIN_CHUNKS + 1)], axis=2)

    kb, vb = band(k), band(v)
    key_pos = (jnp.arange(nC)[:, None] - WIN_CHUNKS) * CHUNK + jnp.arange((WIN_CHUNKS + 1) * CHUNK)[None, :]
    mask = (key_pos >= 0)[:, None, None, None, :]
    out = sink_attend(qc, kb, vb, sink, mask)
    return out.reshape(B, S, C_HEADS * C_DH)

def odd_mixer(h, pos, k_cache, v_cache, w_in, b_in, w_out, sink):
    B, S, _ = h.shape
    z = h @ w_in + b_in
    q, k, v = jnp.split(z, [C_HEADS * C_DH, C_HEADS * C_DH + C_KV * C_DH], axis=-1)
    q = rope(q.reshape(B, S, C_KV, C_GROUP, C_DH), pos)
    k = rope(k.reshape(B, S, C_KV, C_DH), pos)
    v = v.reshape(B, S, C_KV, C_DH)
    sink = sink.reshape(C_KV, C_GROUP)
    if k_cache is None:
        o = swa_prompt(q, k, v, sink)
        k_all, v_all = k, v
    else:
        k_all = jnp.concatenate([k_cache, k], axis=1)
        v_all = jnp.concatenate([v_cache, v], axis=1)
        o = sink_attend(q, k_all, v_all, sink, None).reshape(B, S, C_HEADS * C_DH)
    return o @ w_out, k_all[:, -C_CACHE:], v_all[:, -C_CACHE:]

def conv_ffn(x, hist, w_up, conv_w, conv_b, w_down):
    S = x.shape[1]
    up = x @ w_up
    ext = jnp.concatenate([hist, up], axis=1)
    c = conv_b + ext[:, 0:S] * conv_w[0]
    for j in range(1, CONV_W):
        c = c + ext[:, j:j + S] * conv_w[j]
    gate, val = jnp.split(c, 2, axis=-1)
    return (jax.nn.silu(gate) * val) @ w_down, ext[:, -(CONV_W - 1):]

def setup_inputs(seed: int = 0) -> dict:
    key = jax.random.key(seed)
    ks = jax.random.split(key, 26)
    D = D_MODEL

    def nrm(k, shape, s=1.0):
        return s * jax.random.normal(k, shape, jnp.float32)

    return {
        'x_prompt': nrm(ks[0], (BATCH, SEQ, D)),
        'x_sample': nrm(ks[1], (DEC_BATCH, DEC_SEQ, D)),
        'cache_diff_k': nrm(ks[2], (N_EVEN, DEC_BATCH, PAST_LEN, A_HEADS, 2, A_DH)),
        'cache_diff_v': nrm(ks[3], (N_EVEN, DEC_BATCH, PAST_LEN, A_HEADS, 2 * A_DH)),
        'state_pool': nrm(ks[4], (N_EVEN, DEC_BATCH, POOL_HIST, B_WIDTH)),
        'cache_swa_k': nrm(ks[5], (N_ODD, DEC_BATCH, C_CACHE, C_KV, C_DH)),
        'cache_swa_v': nrm(ks[6], (N_ODD, DEC_BATCH, C_CACHE, C_KV, C_DH)),
        'state_ffn_conv': nrm(ks[7], (DEPTH, DEC_BATCH, CONV_W - 1, 2 * D_FF)),
        'norm_attn': 1.0 + nrm(ks[8], (DEPTH, D), 0.05),
        'norm_ffn': 1.0 + nrm(ks[9], (DEPTH, D), 0.05),
        'norm_final': 1.0 + nrm(ks[10], (D,), 0.05),
        'w_in_even': nrm(ks[11], (N_EVEN, D, EVEN_IN), D ** -0.5),
        'w_out_even': nrm(ks[12], (N_EVEN, A_WIDTH + B_WIDTH, D), (A_WIDTH + B_WIDTH) ** -0.5),
        'diff_lambda': nrm(ks[13], (N_EVEN, 4, A_DH), 0.1),
        'diff_subln': 1.0 + nrm(ks[14], (N_EVEN, 2 * A_DH), 0.05),
        'pool_w': nrm(ks[15], (N_EVEN, POOL_GROUPS, POOL_CH, POOL_CH), POOL_CH ** -0.5),
        'pool_scale': 1.0 + nrm(ks[16], (N_EVEN, B_WIDTH), 0.1),
        'w_in_odd': nrm(ks[17], (N_ODD, D, ODD_IN), D ** -0.5),
        'b_in_odd': nrm(ks[18], (N_ODD, ODD_IN), 0.02),
        'w_out_odd': nrm(ks[19], (N_ODD, C_HEADS * C_DH, D), (C_HEADS * C_DH) ** -0.5),
        'sinks': nrm(ks[20], (N_ODD, C_HEADS), 0.5),
        'w_up': nrm(ks[21], (DEPTH, D, 2 * D_FF), D ** -0.5),
        'conv_w': nrm(ks[22], (DEPTH, CONV_W, 2 * D_FF), CONV_W ** -0.5),
        'conv_b': nrm(ks[23], (DEPTH, 2 * D_FF), 0.02),
        'w_down': nrm(ks[24], (DEPTH, D_FF, D), D_FF ** -0.5),
    }

def reference(x_prompt, x_sample, cache_diff_k, cache_diff_v, state_pool, cache_swa_k, cache_swa_v, state_ffn_conv,
              norm_attn, norm_ffn, norm_final, w_in_even, w_out_even, diff_lambda, diff_subln, pool_w, pool_scale,
              w_in_odd, b_in_odd, w_out_odd, sinks, w_up, conv_w, conv_b, w_down):
    hp, hs = x_prompt, x_sample
    bp, sp = x_prompt.shape[:2]
    pos_p = jnp.arange(sp, dtype=jnp.int32)
    pos_s = PAST_LEN + jnp.arange(x_sample.shape[1], dtype=jnp.int32)
    dkp, dvp, plp, skp, svp, fcp = [], [], [], [], [], []
    dks, dvs, pls, sks, svs, fcs = [], [], [], [], [], []
    for i in range(DEPTH):
        j = i // 2
        hn_p = rmsnorm(hp, norm_attn[i])
        hn_s = rmsnorm(hs, norm_attn[i])
        if i % 2 == 0:
            ew = (w_in_even[j], w_out_even[j], diff_lambda[j], diff_subln[j], pool_w[j], pool_scale[j], i)
            zero_pool = jnp.zeros((bp, POOL_HIST, B_WIDTH), hp.dtype)
            mp, kp, vp, pp = even_mixer(hn_p, pos_p, None, None, zero_pool, 0, *ew)
            ms, k_s, v_s, ps = even_mixer(hn_s, pos_s, cache_diff_k[j], cache_diff_v[j], state_pool[j], POOL_HIST, *ew)
            dkp.append(kp); dvp.append(vp); plp.append(pp)
            dks.append(k_s); dvs.append(v_s); pls.append(ps)
        else:
            ow = (w_in_odd[j], b_in_odd[j], w_out_odd[j], sinks[j])
            mp, kp, vp = odd_mixer(hn_p, pos_p, None, None, *ow)
            ms, k_s, v_s = odd_mixer(hn_s, pos_s, cache_swa_k[j], cache_swa_v[j], *ow)
            skp.append(kp); svp.append(vp)
            sks.append(k_s); svs.append(v_s)
        hp = hp + mp
        hs = hs + ms
        fw = (w_up[i], conv_w[i], conv_b[i], w_down[i])
        zero_conv = jnp.zeros((bp, CONV_W - 1, 2 * D_FF), hp.dtype)
        fp, cp = conv_ffn(rmsnorm(hp, norm_ffn[i]), zero_conv, *fw)
        f_s, c_s = conv_ffn(rmsnorm(hs, norm_ffn[i]), state_ffn_conv[i], *fw)
        hp = hp + fp
        hs = hs + f_s
        fcp.append(cp); fcs.append(c_s)
    y_prompt = rmsnorm(hp, norm_final)
    y_sample = rmsnorm(hs, norm_final)
    diff_k_prompt = jnp.stack(dkp)
    diff_v_prompt = jnp.stack(dvp)
    pool_prompt = jnp.stack(plp)
    swa_k_prompt = jnp.stack(skp)
    swa_v_prompt = jnp.stack(svp)
    ffn_conv_prompt = jnp.stack(fcp)
    diff_k_sample = jnp.stack(dks)
    diff_v_sample = jnp.stack(dvs)
    pool_sample = jnp.stack(pls)
    swa_k_sample = jnp.stack(sks)
    swa_v_sample = jnp.stack(svs)
    ffn_conv_sample = jnp.stack(fcs)
    return (y_prompt, y_sample, diff_k_prompt, diff_v_prompt, pool_prompt, swa_k_prompt, swa_v_prompt, ffn_conv_prompt,
            diff_k_sample, diff_v_sample, pool_sample, swa_k_sample, swa_v_sample, ffn_conv_sample)


_drawn_inputs = setup_inputs


def setup_inputs(seed=0):
    import zlib

    import numpy as np

    out = dict(_drawn_inputs(seed))
    spreads = {}
    factors = {'diff_lambda': 6.579, 'b_in_odd': 2.743, 'sinks': 8.0, 'conv_b': 3.282}
    for name, (base, spread) in spreads.items():
        noise = np.random.default_rng([zlib.crc32(name.encode()), seed]).standard_normal(out[name].shape)
        drawn = base * np.exp(spread * noise) if base else spread * noise
        out[name] = __import__('jax').numpy.asarray(drawn.astype(out[name].dtype))
    for name, factor in factors.items():
        out[name] = (out[name] * factor).astype(out[name].dtype)
    return out
```

```python
import math
from contextlib import ExitStack

import numpy as np
import concourse.bass as bass
from concourse import mybir

F32 = mybir.dt.float32
F32R = mybir.dt.float32r
BF16 = mybir.dt.bfloat16
ALU = mybir.AluOpType
ACT = mybir.ActivationFunctionType
AX_X = mybir.AxisListType.X

P = 128
D = 1024
KT = D // P
SEQ, DEC = 1024, 64
R = SEQ + DEC
PAST = 256
A_H, A_DH = 4, 64
A_W = A_H * 2 * A_DH
WINDOWS = (2, 4, 8, 16)
HIST = 15
C_H, C_KV, C_DH, C_CACHE = 16, 2, 64, 128
FF = 2816
FT = FF // P
NB = FT // 2
EPS = 1e-5
LAM_INIT = 0.8 - 0.6 * math.exp(-0.3 * 0)
BIG = -1e30
RT = 9
ROWS = [P] * 8 + [DEC]
CHUNKS = [(0, 364), (364, 364), (728, 360)]
EXT = SEQ + DEC + 4
UEXT = HIST + SEQ + HIST + DEC
U_S = HIST + SEQ + HIST

P_TILES = 7
P_NA0, P_NA1, P_NF0, P_NF1, P_NFIN, P_BIN, P_PS, P_SUB, P_ROWS6 = 0, 8, 16, 24, 32, 40, 50, 54, 55


def build(nc, io):
    ctx = ExitStack()
    with ctx:

        base = (nc.sbuf_base + 31) // 32 * 32
        RA = base
        RSZ = 71936
        R0 = RA + KT * R * 4
        R1 = R0 + RSZ
        RW = R1 + RSZ
        RK = RW + 26624
        RM = RK + 5120

        def at(name, off, shape, dt=F32):
            return nc.alloc_sbuf_tensor_at(name, shape, dt, offset=off)

        H = at("resid", RA, [P, KT, R])
        cos_e = at("cos_e", RA, [P, R])
        sin_e = at("sin_e", RA + 4352, [P, R])
        z_e = at("z_e", RA + 2 * 4352, [P, R])
        zs_e = at("zs_e", RA + 3 * 4352, [P, R])
        vz_e = at("vz_e", RA + 4 * 4352, [P, R])
        sumB = at("sumB", RA + 5 * 4352, [P, UEXT])
        sumA = at("sumA", RA + 5 * 4352 + 4480, [P, UEXT])

        def region_x(tag, off):
            return at(f"xhi{tag}", off, [P, KT, R], F32R), at(f"xlo{tag}", off + KT * R * 4, [P, KT, R], F32R)

        xn0, xn1 = region_x("0", R0), region_x("1", R1)
        xnat = at("xnat", R1, [P, RT, D])
        junk = at("junk", R1 + 36864, [P, D])
        pnat = at("pnat", R1 + 36864 + 4096, [P, P_TILES, P])
        hnat = at("hnat", R1 + 36864 + 4096 + 3584, [HIST, A_W])
        qT = at("qT", R1, [P, A_H, R])
        kT = at("kT", R1 + 17408, [P, A_H, R])
        vN = at("vN", R1 + 34816, [P, RT, A_W])
        uT = at("uT", R1 + 53248, [P, 4, UEXT])
        phi = at("phi", R0, [P, 2, R], F32R)
        plo = at("plo", R0 + 34816, [P, 2, R], F32R)
        E = at("E", R0, [P, 2, 2, 1024])
        comb = at("comb", R0 + 34816, [P, 2, 1024])
        AT = at("AT", R0 + 34816 + 8192, [P, 2, 1024])
        oN = at("oN", RW + 8192, [P, RT, A_H, P])
        kcn = at("kcn", RW, [P, 2, A_W])
        vcn = at("vcn", RW + 4096, [P, 2, A_W])
        kNat = at("kNat", RK, [P, RT, P])
        kAll = at("kAll", RK, [P, A_H, PAST + DEC])
        acc = at("acc", RK, [P, RT * P])
        kc2n = at("kc2n", RK, [P, P])
        wraw = at("wraw", RW, [P, 2, KT, P])
        whi = at("whi", RW + 8192, [P, 2, KT, P], F32R)
        wlo = at("wlo", RW + 8192 + 8192, [P, 2, KT, P], F32R)
        graw = at("graw", RW, [P, KT, 2 * P])
        vraw = at("vraw", RW + 8192, [P, KT, 2 * P])
        draw = at("draw", RW + 16384, [P, 2, D])

        class FfnBuffers:
            def __init__(self, tag, off):
                self.hhi = at(f"hhi{tag}", off, [P, 2, R], F32R)
                self.hlo = at(f"hlo{tag}", off + 8704, [P, 2, R], F32R)
                o = off + 17408
                self.uphi = at(f"uphi{tag}", o, [P, 2, KT, P], F32R)
                self.uplo = at(f"uplo{tag}", o + 8192, [P, 2, KT, P], F32R)
                o += 16384
                self.dhi = at(f"dhi{tag}", o, [P, 2, D], F32R)
                self.dlo = at(f"dlo{tag}", o + 8192, [P, 2, D], F32R)
                o += 16384
                self.ext = at(f"ext{tag}", o, [P, 2, EXT])
                o += 2 * EXT * 4
                self.c = at(f"c{tag}", o, [P, 2, EXT - 2])
        ffn_buf = [FfnBuffers("_f0", R0), FfnBuffers("_f1", R1)]
        q2T = at("q2T", R0, [P, KT, R])
        kd = at("kd", R0 + 34816, [P, C_KV, R])
        v2N = at("v2N", R0 + 43520, [P, RT, P])
        o = R0 + 48128
        cos_o, sin_o = at("cos_o", o, [P, R]), at("sin_o", o + 4352, [P, R])
        z_o, zs_o = at("z_o", o + 8704, [P, R]), at("zs_o", o + 13056, [P, R])
        vz_o = at("vz_o", o + 17408, [P, R])
        E2 = at("E2", o, [P, 2, 4, 256])
        PT2 = at("PT2", o + 8192, [P, 2, 2, 4, P])
        oN2 = at("oN2", o + 16384, [P, D])
        o += 21760
        kds = at("kds", o, [P, C_KV, C_CACHE + DEC])
        vc2 = at("vc2", o + 1536, [P, P])
        yN = at("yN", R0, [P, RT, D])

        o = RM
        def small(name, shape, dt=F32):
            nonlocal o
            size = int(np.prod(shape[1:])) * (2 if dt == BF16 else 4)
            t = at(name, o, shape, dt)
            o += (size + 31) // 32 * 32
            return t
        dg_off = o
        dg = small("dg", [P, RT, P])
        rB = at("rB", dg_off, [P, R])
        ident = small("ident", [P, P])
        ones = small("ones", [P, P])
        par = small("par", [P, P_TILES, 88])
        s_off = o
        pwraw = small("pwraw", [P, 4, P])
        pwhi = small("pwhi", [P, 4, P], F32R)
        pwlo = small("pwlo", [P, 4, P], F32R)
        sq = at("sq", s_off, [P, R])
        ojunk = at("ojunk", s_off + 4352, [P, P])
        kn2 = at("kn2", s_off + 4352, [P, 2, P])
        maskL = small("maskL", [P, P], BF16)
        maskR = small("maskR", [P, 2, 256], BF16)
        epsT = small("epsT", [P, 1])
        ss = small("ss", [P, RT])
        std = small("std", [P, RT])
        rs = small("rs", [P, RT])
        lamp = at("lamp", R1 + 48640, [P, 4, A_DH])
        lam2 = small("lam2", [P, 4])
        neglam = small("neglam", [P, 1])
        subg = small("subg", [P, 1])
        sinkb = small("sinkb", [P, C_H])
        e_off = o
        edge = at("edge", e_off, [P, 2, 2, 2 * FT])
        rct = small("rct", [P, 4, HIST])
        ue = small("ue", [P, 4, 2, HIST])
        fix = small("fix", [P, HIST])
        nm = small("nm", [P, 2, 2])
        sums = small("sums", [P, 2, 2])
        rsum = small("rsum", [P, 4, 2])
        cc = small("cc", [P, 2])
        sso = small("sso", [P, RT, A_H])
        rso = small("rso", [P, RT, A_H])
        m2 = small("m2", [P, 2, 4]); nm2 = small("nm2", [P, 2, 4]); snk2 = small("snk2", [P, 2, 4])
        es2 = small("es2", [P, 2, 4]); sum2 = small("sum2", [P, 2, 4]); den2 = small("den2", [P, 2, 4])
        rd2 = small("rd2", [P, 2, 4])
        uout = at("uout", s_off, [HIST, 2, A_W])
        edgeN = at("edgeN", s_off + 4352, [4 * FT, 2, P])
        assert o <= nc.sbuf_usable_end, (o, nc.sbuf_usable_end)

        PS = ctx.enter_context(nc.psum_tensor("PS", [P, 8, 512], F32))

        def pieces(s, t, off=0):
            a = CHUNKS[2][0]
            return [(PS[:, 3 * s:3 * s + 2, 0:364], t[:, off:off + a].rearrange("p (c n) -> p c n", c=2)),
                    (PS[:, 3 * s + 2, 0:360], t[:, off + a:off + R])]

        def rows_of(t):
            return slice(P * t, P * t + ROWS[t])

        def param(tile, row):
            return par[:, tile, row:row + 1]

        def products(s, k, nk, wh, wl, xh, xl):
            for n, (w, x) in enumerate(((wh, xh), (wh, xl), (wl, xh))):
                for c, (a, width) in enumerate(CHUNKS):
                    last = nc.tensor.matmul(PS[:, 3 * s + c, 0:width], w, x[:, a:a + width],
                                            start=(k == 0 and n == 0), stop=(k == nk - 1 and n == 2))
            return last

        made = {}

        def S(name):
            if name not in made:
                made[name] = ctx.enter_context(nc.semaphore(name))
            return made[name]

        LAYER_COUNT = {"in_raw0": 128, "in_raw1": 128, "in_hi": 16, "in_lo": 16, "in_mm": 16, "in_ev": 16,
                       "in_rope": 8, "in_rz": 8, "in_sw": 8, "op_raw0": 64, "op_raw1": 64, "op_hi": 8, "op_lo": 8, "op_mm": 8,
                       "ff_graw": 16 * NB, "ff_vraw": 16 * NB, "ff_draw": 16 * NB,
                       "ff_uphi": 4 * NB, "ff_uplo": 4 * NB, "ff_upmm": 4 * NB,
                       "ff_dhi": NB, "ff_dlo": NB, "ff_dnmm": KT * NB, "ff_dnev": KT * (NB - 1)}
        for name in ("gext", "vext", "gtap", "vtap", "gmid", "vmid", "gconv", "vconv", "silu", "h", "hhi", "hlo"):
            LAYER_COUNT["ff_" + name] = FT

        C_IDENT, C_SMALL, C_ALL = 2, 7, 17
        X_IN = [f"x_in{n}" for n in (0, 2, 2, 4, 4, 6, 6, 7, 8)]

        def reached(eng, l, name, count):
            eng.wait_ge(S(name), count + l * LAYER_COUNT[name])

        def norm_pe_stats(pe, n):
            pe.wait_ge(S("acc_done"), 8 * n)
            for t in range(RT):
                last = nc.tensor.matmul(PS[:, 6, t:t + 1], acc[:, t * P:(t + 1) * P], ones[:, 0:1],
                                        start=True, stop=True)
            last.then_inc(S("n_stat"), 1)

        def norm_pe_bcast(pe, n):
            pe.wait_ge(S("n_diag"), n + 1)
            flat = dg[:, :, :].rearrange("p t c -> p (t c)")
            for c, (a, width) in enumerate(CHUNKS):
                last = nc.tensor.matmul(PS[:, 3 + c, 0:width], ones[:, :], flat[:, a:a + width],
                                        start=True, stop=True)
            last.then_inc(S("n_bc"), 1)

        def norm_act(act, n, src):
            nc.scalar.activation(std[:, :], src, ACT.Sqrt, scale=1.0 / D,
                                 bias=epsT[:, 0:1]).then_inc(S("n_sqrt"), 1)

        def norm_dve_diag(dve, n):
            dve.wait_ge(S("n_sqrt"), n + 1)
            nc.vector.reciprocal(rs[:, :], std[:, :]).then_inc(S("n_rec"), 1)
            if n < 4:
                dve.wait_ge(S("n_rec"), n + 1)
                nc.vector.tensor_tensor(dg[:, :, :], ident[:, :].unsqueeze(1).to_broadcast([P, RT, P]),
                                        rs[:, :].unsqueeze(2).to_broadcast([P, RT, P]),
                                        ALU.mult).then_inc(S("n_diag"), 1)

        def norm_dve_rb(dve, n):
            dve.wait_ge(S("n_bc"), n + 1)
            for src, dst in pieces(1, rB):
                last = nc.vector.tensor_copy(dst, src)
            last.then_inc(S("n_rb"), 1)

        def scaled_by_row(s, dst, off=0):
            for (src, d), (_, r) in zip(pieces(s, dst, off), pieces(s, rB)):
                last = nc.vector.tensor_tensor(d, src, r, ALU.mult)
            return last

        PAIRS = [(t, h) for t in range(RT) for h in range(A_H)]
        KEYS = [(t + 1) * P for t in range(8)] + [PAST + DEC]
        BLOCKS = [[(b * P, min(P, KEYS[t] - b * P)) for b in range((KEYS[t] + P - 1) // P)] for t in range(RT)]
        FILLS = [[(f, min(4, len(BLOCKS[t]) - f)) for f in range(0, len(BLOCKS[t]), 4)] for t in range(RT)]
        FIRST_FILL = [sum(len(FILLS[t]) for t, _ in PAIRS[:p]) for p in range(len(PAIRS) + 1)]
        NP_ = len(PAIRS)
        BATCHES = [(t, b) for t in range(RT) for b in range(4)]
        WIN = [(P, 256)] + [(0, 256)] * 7 + [(0, C_CACHE + DEC)]
        NQ = len(BATCHES)

        def key_tiles(t):
            return [kt for kt in range(2) if WIN[t][0] < (kt + 1) * P]
        OFILL = [sum(len(key_tiles(t)) for t, _ in BATCHES[:q]) for q in range(NQ + 1)]

        OUTP = [dict(x=xn0, y=xn1, w=io["w_out_even"][0], gain=P_NF0, n=1, l=0, tag="op", ks=[4, 5, 6, 7, 0, 1, 2, 3]),
                dict(x=xn1, y=xn0, w=io["w_out_odd"][0], gain=P_NF1, n=3, l=1, tag="op", ks=list(range(8)))]
        FFN = [dict(x=xn1, y=xn1, gain=P_NA1, n=1, tag="ff", b=ffn_buf[0], l=0),
               dict(x=xn0, y=None, gain=P_NFIN, n=3, tag="ff", b=ffn_buf[1], l=1)]

        def pool_hi(act, identity, g):
            act.wait_ge(S("pm_mm"), g + 1)
            for src, dst in pieces(g % 2, xn0[0][:, 4 + g, :]):
                last = identity(dst, src, scale=param(6, P_PS + g))
            last.then_inc(S("pm_hi"), 1)

        def finish_tile(act, identity, k, x, gain):
            h = H[:, bass.ds(k, 1), :]
            if x:
                identity(x[0][:, bass.ds(k, 1), :], h, scale=par[:, 6, bass.ds(k + gain, 1)]).then_inc(S("fin_hi"), 1)
            nc.scalar.activation(sq[:, :].unsqueeze(1), h, ACT.Square).then_inc(S("fin_sq"), 1)

        def odd_rows_hi(act, t):
            nr = ROWS[t]
            for j in range(2):
                act.wait_ge(S("om_tr"), 2 * t + j + 1)
                nc.scalar.copy(xn1[0][:, 4 * j:4 * j + 4, P * t:P * t + nr],
                               PS[:, 4 + j, :].rearrange("p (k r) -> p k r", k=4)[:, :, 0:nr]).then_inc(S("om_hi"), 1)

        block = ctx.enter_context(nc.Block())


        @block.sync
        def _(sp):
            def x_tile(t):
                if t == 8:
                    sp.dma_start(xnat[0:DEC, t, :], io["x_sample"][0]).then_inc(S("x_in8"), 16)
                else:
                    t0 = max(t - 1, 0)
                    sp.dma_start(xnat[:, t0:t + 1, :], io["x_prompt"][0].rearrange("(t p) d -> p t d", p=P)[:, t0:t + 1, :]) \
                        .then_inc(S(f"x_in{t}"), 16)

            def par_rows(tile, row, src):
                n = src.shape[0]
                sp.dma_start(pnat[row:row + n, tile, :], src).then_inc(S("par_in"), 16)

            x_tile(0)
            for l in range(2):
                par_rows(3 * l, 0, io["conv_w"][l, 0:2].rearrange("i (t c) -> (i t) c", c=P))
                par_rows(3 * l + 1, 0, io["conv_w"][l, 2:3].rearrange("i (t c) -> (i t) c", c=P))
                par_rows(3 * l + 1, 44, io["conv_b"][l:l + 1].rearrange("i (t c) -> (i t) c", c=P))
                par_rows(3 * l + 2, 0, io["state_ffn_conv"][l, 0].rearrange("i (t c) -> (i t) c", c=P))
            par_rows(6, P_NA0, io["norm_attn"].rearrange("i (t c) -> (i t) c", c=P))
            par_rows(6, P_NF0, io["norm_ffn"].rearrange("i (t c) -> (i t) c", c=P))
            par_rows(6, P_NFIN, io["norm_final"].rearrange("(t c) -> t c", c=P))
            par_rows(6, P_BIN, io["b_in_odd"][0].rearrange("(t c) -> t c", c=P))
            par_rows(6, P_PS, io["pool_scale"][0].rearrange("(t c) -> t c", c=P))
            par_rows(6, P_SUB, io["diff_subln"])
            sp.dma_start(hnat[:, :], io["state_pool"][0, 0]).then_inc(S("par_in"), 16)
            x_tile(2)
            x_tile(4)

            def even_in_weight(u):
                col = (u % 4) * A_W + (u // 4) * P
                if u >= 2:
                    reached(sp, 0, "in_lo", u - 1)
                sp.dma_start(wraw[:, u % 2], io["w_in_even"][0].rearrange("(k p) n -> p k n", p=P)[:, :, col:col + P]) \
                    .then_inc(S(f"in_raw{u % 2}"), 16)
            even_in_weight(0)
            even_in_weight(1)
            x_tile(6)
            sp.dma_start(xnat[:, 7, :], io["x_prompt"][0, 7 * P:8 * P, :]).then_inc(S("x_in7"), 16)
            x_tile(8)
            for c in range(4):
                sp.dma_start(cos_e[32 * c:32 * c + 32, :], io["cos_t"]).then_inc(S("tab_in"), 16)
            for c in range(2):
                sp.dma_start(sin_e[64 * c:64 * c + 64, :], io["sin_t"]).then_inc(S("tab_in"), 16)
            sp.dma_start(pwraw[:, :, :], io["pool_w"][0].rearrange("g c d -> c g d")).then_inc(S("pw_in"), 16)
            sp.dma_start(rct[:, :, :].rearrange("p g t -> p (g t)"), io["rcnt_t"].partition_broadcast(P)).then_inc(S("bc_in"), 16)
            sp.dma_start(lamp[:, :, :].rearrange("p a b -> p (a b)"),
                         io["diff_lambda"][0].rearrange("a b -> (a b)").partition_broadcast(P)).then_inc(S("bc_in"), 16)
            sp.dma_start(sinkb[:, :], io["sinks"][0].partition_broadcast(P)).then_inc(S("bc_in"), 16)
            for u in range(2, 16):
                even_in_weight(u)
            reached(sp, 0, "in_lo", 16)
            sp.dma_start(kcn[:, :, :], io["cache_diff_k"][0, 0].rearrange("(b p) h m d -> p b (h m d)", p=P)).then_inc(S("kc_in"), 16)
            sp.dma_start(vcn[:, :, :], io["cache_diff_v"][0, 0].rearrange("(b p) h e -> p b (h e)", p=P)).then_inc(S("vc_in"), 16)
            sp.wait_ge(S("ei_tev"), 24)
            sp.dma_start(io["diff_v_prompt"][0, 0].rearrange("(t p) h e -> p t (h e)", p=P), vN[:, 0:8, :]).then_inc(S("st_v"), 16)
            sp.dma_start(io["diff_v_sample"][0, 0].rearrange("s h e -> s (h e)"), vN[0:DEC, 8, :]).then_inc(S("st_v"), 16)
            sp.dma_start(io["swa_k_sample"][0, 0, 0:64], io["cache_swa_k"][0, 0, 64:128]).then_inc(S("st_y"), 16)
            sp.dma_start(io["swa_v_sample"][0, 0, 0:64], io["cache_swa_v"][0, 0, 64:128]).then_inc(S("st_y"), 16)

            def out_weights(o):
                t, l = o["tag"], o["l"]
                src = o["w"].rearrange("(k p) n -> p k n", p=P)
                for u in range(2):
                    if l == 0:
                        sp.wait_ge(S("kc_ev") if u == 0 else S("at_pv"), 3 if u == 0 else NP_)
                    else:
                        reached(sp, 1, "in_lo", 9 + u)
                    sp.dma_start(wraw[:, u], src[:, :, u * P:(u + 1) * P]).then_inc(S(f"{t}_raw{u}"), 16)
                with sp.Fori(1, 4) as j:
                    for s in range(2):
                        col = sp.snap(j * 256 + s * P)
                        reached(sp, l, f"{t}_lo", 2 * j + s - 1)
                        sp.dma_start(wraw[:, s], src[:, :, bass.ds(col, P)]).then_inc(S(f"{t}_raw{s}"), 16)

            def ffn_weights(f):
                t, l, b = f["tag"], f["l"], f["b"]
                up = io["w_up"][l].rearrange("(k p) n -> p k n", p=P)
                down = io["w_down"][l].rearrange("(f p) n -> p f n", p=P)
                reached(sp, l, "op_lo", 8)
                sp.dma_start(graw[:, :, :], up[:, :, 0:256]).then_inc(S(f"{t}_graw"), 16)
                reached(sp, l, "op_mm", 8)
                sp.dma_start(vraw[:, :, :], up[:, :, FF:FF + 256]).then_inc(S(f"{t}_vraw"), 16)
                sp.dma_start(draw[:, :, :], down[:, 0:2, :]).then_inc(S(f"{t}_draw"), 16)
                with sp.Fori(1, NB) as i:
                    g_col = sp.snap(i * 256)
                    v_col = sp.snap(i * 256 + FF)
                    d_tile = sp.snap(i * 2)
                    reached(sp, l, f"{t}_uplo", 4 * i - 1)
                    sp.dma_start(graw[:, :, :], up[:, :, bass.ds(g_col, 256)]).then_inc(S(f"{t}_graw"), 16)
                    reached(sp, l, f"{t}_dlo", i)
                    sp.dma_start(draw[:, :, :], down[:, bass.ds(d_tile, 2), :]).then_inc(S(f"{t}_draw"), 16)
                    reached(sp, l, f"{t}_uplo", 4 * i)
                    sp.dma_start(vraw[:, :, :], up[:, :, bass.ds(v_col, 256)]).then_inc(S(f"{t}_vraw"), 16)

            out_weights(OUTP[0])
            ffn_weights(FFN[0])

            src = io["w_in_odd"][0].rearrange("(k p) n -> p k n", p=P)
            for u in range(2):
                sp.wait_ge(S("ff_uplo"), 4 * NB)
                sp.dma_start(wraw[:, u], src[:, :, u * P:(u + 1) * P]).then_inc(S(f"in_raw{u}"), 16)
            sp.wait_ge(S("fin_h"), 16)
            for c in range(4):
                sp.dma_start(cos_o[32 * c:32 * c + 32, :], io["cos_t"]).then_inc(S("tab_in"), 16)
            for c in range(2):
                sp.dma_start(sin_o[64 * c:64 * c + 64, :], io["sin_t"]).then_inc(S("tab_in"), 16)
            sp.dma_start(vc2[:, :], io["cache_swa_v"][0, 0].rearrange("s g d -> s (g d)")).then_inc(S("vc_in"), 16)
            with sp.Fori(1, 5) as j:
                for s in range(2):
                    col = sp.snap(j * 256 + s * P)
                    reached(sp, 1, "in_lo", 2 * j + s - 1)
                    sp.dma_start(wraw[:, s], src[:, :, bass.ds(col, P)]).then_inc(S(f"in_raw{s}"), 16)
            sp.wait_ge(S("n_stat"), 2)
            sp.dma_start(kc2n[:, :], io["cache_swa_k"][0, 0].rearrange("s g d -> s (g d)")).then_inc(S("kc_in"), 16)
            sp.wait_ge(S("oi_kn"), 2)
            sp.dma_start(io["swa_k_prompt"][0, 0].rearrange("s g d -> s (g d)"), kn2[:, 0, :]).then_inc(S("st_k2"), 16)
            sp.dma_start(io["swa_k_sample"][0, 0, 64:128].rearrange("s g d -> s (g d)"), kn2[0:DEC, 1, :]).then_inc(S("st_k2"), 16)
            sp.wait_ge(S("oi_vn"), 3)
            sp.dma_start(io["swa_v_prompt"][0, 0].rearrange("s g d -> s (g d)"), v2N[:, 7, :]).then_inc(S("st_v2"), 16)
            sp.dma_start(io["swa_v_sample"][0, 0, 64:128].rearrange("s g d -> s (g d)"), v2N[0:DEC, 8, :]).then_inc(S("st_v2"), 16)

            out_weights(OUTP[1])
            ffn_weights(FFN[1])

            for t in range(RT):
                sp.wait_ge(S("y_act"), t + 1)
                sp.wait_ge(S("y_dve"), t + 1)
                dst = io["y_prompt"][0, t * P:(t + 1) * P, :] if t < 8 else io["y_sample"][0]
                sp.dma_start(dst, yN[0:ROWS[t], t, :]).then_inc(S("st_y"), 16)
            for name, n in (("st_v", 2), ("st_k2", 2), ("st_v2", 2), ("st_y", RT + 2),
                            ("st_k", 8), ("st_u", 2), ("st_e", 4)):
                sp.wait_ge(S(name), 16 * n)

        @block.gpsimd
        def _(pool):
            made_ = [0]

            def constant(ins):
                made_[0] += 1
                ins.then_inc(S("c_set"), 1)
                pool.wait_ge(S("c_set"), made_[0])

            constant(nc.gpsimd.memset(ident[:, :], 0.0))
            constant(nc.gpsimd.affine_select(out=ident[:, :], in_=ident[:, :], compare_op=ALU.not_equal, fill=1.0,
                                             base=0, pattern=[[-1, P]], channel_multiplier=1))
            for tile, value in ((ones[:, :], 1.0), (epsT[:, :], EPS), (ss[:, :], 0.0), (sso[:, :, :], 0.0),
                                (uT[:, :, 0:HIST], 0.0), (maskL[:, :], 0.0), (maskR[:, :, :], 0.0)):
                constant(nc.gpsimd.memset(tile, value))
            for half in (0, 64):
                constant(nc.gpsimd.memset(maskL[half:half + 1, 0:64], 1.0))
                constant(nc.gpsimd.memset(maskL[half + 32:half + 33, 64:128], 1.0))
                constant(nc.gpsimd.memset(maskR[half:half + 1, :, 192:256], BIG))
                constant(nc.gpsimd.memset(maskR[half + 32:half + 33, :, 0:64], BIG))

            gain = par[:, 6, P_NA0:P_NA0 + KT].unsqueeze(2).to_broadcast([P, KT, P])

            def even_gain(u):
                reached(pool, 0, f"in_raw{u % 2}", 16 * (u // 2 + 1))
                if u == 0:
                    pool.wait_ge(S("par_ev"), 3)
                w = wraw[:, u % 2]
                nc.gpsimd.tensor_tensor(w, w, gain, ALU.mult).then_inc(S("ei_gam"), 1)
                pool.wait_ge(S("ei_gam"), u + 1)

            chain = [0]

            def step(ins):
                chain[0] += 1
                ins.then_inc(S("pl"), 1)
                pool.wait_ge(S("pl"), chain[0])

            def window_mean(g):
                pool.wait_ge(S("ei_ue"), g + 1)
                u, bufs = uT[:, g, :], [sumA, sumB]
                cur = u
                for l in range(g + 1):
                    sh, st, dst = 1 << l, (2 << l) - 1, bufs[l % 2]
                    step(nc.gpsimd.tensor_tensor(dst[:, st:UEXT], cur[:, st:UEXT], cur[:, st - sh:UEXT - sh], ALU.add))
                    cur = dst
                if g == 0:
                    pool.wait_ge(S("bc_in"), 48)
                step(nc.gpsimd.tensor_tensor(fix[:, :], cur[:, HIST:2 * HIST], rct[:, g, :], ALU.mult))
                step(nc.gpsimd.tensor_scalar(cur[:, HIST:UEXT], cur[:, HIST:UEXT], 1.0 / WINDOWS[g], None, ALU.mult))
                step(nc.gpsimd.tensor_copy(cur[:, HIST:2 * HIST], fix[:, :]))
                nc.gpsimd.tensor_tensor(u[:, HIST:UEXT], cur[:, HIST:UEXT], u[:, HIST:UEXT], ALU.subtract).then_inc(S("pooled"), 1)
                pool.wait_ge(S("pooled"), g + 1)

            even_gain(0)
            even_gain(1)
            for u in range(2, 16):
                even_gain(u)
                if u % 4 == 1 and u > 4:
                    window_mean(u // 4 - 1)
            window_mean(3)
            pool.wait_ge(S("pooled"), 4)
            for k in range(5, KT):
                nc.gpsimd.tensor_tensor(H[:, k, :], xn0[0][:, k, :].bitcast(F32), xn0[1][:, k, :].bitcast(F32),
                                        ALU.add).then_inc(S("h_pool"), 1)
                pool.wait_ge(S("h_pool"), k - 4)
            pool.wait_ge(S("at_pv"), NP_)
            nc.gpsimd.memset(acc[:, :], 0.0).then_inc(S("acc_zero"), 1)
            for n in (2, 3, 4):
                pool.wait_ge(S("n_stat"), n - 1)
                if n == 3:
                    pool.wait_ge(S("kc2_tr"), 1)
                nc.gpsimd.memset(acc[:, :], 0.0).then_inc(S("acc_zero"), 1)

        @block.scalar
        def _(act):
            def identity(dst, src, scale=1.0, bias=0.0):
                return nc.scalar.activation(dst, src, ACT.Identity, scale=scale, bias=bias)

            act.wait_ge(S("c_set"), C_SMALL)

            def even_hi(u):
                act.wait_ge(S("ei_gam"), u + 1)
                if u >= 2:
                    reached(act, 0, "in_mm", u - 1)
                nc.scalar.copy(whi[:, u % 2], wraw[:, u % 2]).then_inc(S("in_hi"), 1)

            def params_out():
                act.wait_ge(S("par_tr"), 1)
                nc.scalar.copy(par[:, 0:4, :], PS[:, 6, 0:352].rearrange("p (a b) -> p a b", b=88)).then_inc(S("par_ev"), 1)
                act.wait_ge(S("par_tr"), 2)
                nc.scalar.copy(par[:, 4:6, :], PS[:, 7, 0:176].rearrange("p (a b) -> p a b", b=88)).then_inc(S("par_ev"), 1)
                nc.scalar.copy(par[:, 6, 0:P_ROWS6], PS[:, 7, 176:176 + P_ROWS6]).then_inc(S("par_ev"), 1)
                nc.scalar.copy(uT[:, :, HIST + SEQ:U_S], PS[:, 7, 240:300].rearrange("p (g r) -> p g r", r=HIST)) \
                    .then_inc(S("par_ev"), 1)

            for t in range(RT):
                nr = ROWS[t]
                act.wait_ge(S(X_IN[t]), 16)
                if t >= 1:
                    act.wait_ge(S("x_sq"), t)
                nc.scalar.activation(junk[0:nr, :], xnat[0:nr, t, :], ACT.Square,
                                     accum_out=ss[0:nr, t:t + 1]).then_inc(S("x_sq"), 1)
                for j in range(2):
                    f = 2 * t + j
                    act.wait_ge(S("x_tr"), f + 1)
                    nc.scalar.copy(xn0[0][:, 4 * j:4 * j + 4, P * t:P * t + nr],
                                   PS[:, f % 6, :].rearrange("p (k r) -> p k r", k=4)[:, :, 0:nr]).then_inc(S("x_hi"), 1)
                if t == 2:
                    params_out()
            even_hi(0)
            even_hi(1)
            act.wait_ge(S("pw_in"), 16)
            nc.scalar.copy(pwhi[:, :, :], pwraw[:, :, :]).then_inc(S("pw_hi"), 1)
            act.wait_ge(S("x_sq"), RT)
            norm_act(act, 0, ss[:, :])

            def natural(g, f, src, dst):
                for j, (a, n, nr) in enumerate(((0, 4, P), (4, 4, P), (8, 1, DEC))):
                    act.wait_ge(S("ei_tr"), f + j + 1)
                    last = nc.scalar.copy(dst[0:nr, a:a + n, :],
                                          PS[0:nr, 6 + (f + j) % 2, 0:n * P].rearrange("p (t c) -> p t c", c=P)) \
                        .then_inc(S("ei_tev"), 1)

            ropes = 0
            for u in range(16):
                g, kind = u // 4, u % 4
                if u + 2 < 16:
                    even_hi(u + 2)
                reached(act, 0, "in_ev", u + 1)
                if kind < 2:
                    if ropes:
                        reached(act, 0, "in_rope", ropes)
                    for c in range(4):
                        last = nc.scalar.copy(zs_e[32 * c:32 * c + 32, :], z_e[32 * (c ^ 1):32 * (c ^ 1) + 32, :])
                    last.then_inc(S("in_sw"), 1)
                    ropes += 1
                if kind == 3:
                    nc.scalar.copy(ue[:, g, 0, :], uT[:, g, SEQ:SEQ + HIST])
                    nc.scalar.copy(ue[:, g, 1, :], uT[:, g, UEXT - HIST:UEXT]).then_inc(S("ei_ue"), 1)
                    if g >= 1:
                        act.wait_ge(S("st_k"), 32 * g)
                    natural(g, 6 * g, kT, kNat)
                    natural(g, 6 * g + 3, vz_e, vN[:, :, g * P:(g + 1) * P])
                    act.wait_ge(S("ei_tev"), 6 * g + 3)
                    act.dma_start(io["diff_k_prompt"][0, 0].rearrange("(t p) h m d -> p t h (m d)", p=P)[:, :, g, :],
                                  kNat[:, 0:8, :]).then_inc(S("st_k"), 16)
                    act.dma_start(io["diff_k_sample"][0, 0].rearrange("s h m d -> s h (m d)")[:, g, :],
                                  kNat[0:DEC, 8, :]).then_inc(S("st_k"), 16)

            act.wait_ge(S("lam"), 2)
            nc.scalar.activation(lam2[:, 2:4], lam2[:, 0:2], ACT.Exp).then_inc(S("lam_exp"), 1)

            for g in range(4):
                act.wait_ge(S("pooled"), g + 1)
                if g == 0:
                    act.wait_ge(S("h_dve"), 1)
                    act.wait_ge(S("h_pool"), 3)
                if g >= 2:
                    act.wait_ge(S("pm_mm"), g - 1)
                nc.scalar.copy(phi[:, g % 2, 0:SEQ], uT[:, g, HIST:HIST + SEQ])
                nc.scalar.copy(phi[:, g % 2, SEQ:R], uT[:, g, U_S:UEXT]).then_inc(S("pm_phi"), 1)
                if g >= 1:
                    pool_hi(act, identity, g - 1)
            pool_hi(act, identity, 3)
            act.wait_ge(S("ue_tr"), 1)
            for st in range(2):
                last = nc.scalar.copy(uout[:, st, :], PS[0:HIST, 6 + st, :])
            last.then_inc(S("ue_ev"), 1)
            act.wait_ge(S("ue_ev"), 1)
            act.dma_start(io["pool_prompt"][0, 0], uout[:, 0, :]).then_inc(S("st_u"), 16)
            act.dma_start(io["pool_sample"][0, 0], uout[:, 1, :]).then_inc(S("st_u"), 16)
            act.wait_ge(S("st_k"), 128)
            for b in range(2):
                act.wait_ge(S("kc_tr"), b + 1)
                nc.scalar.copy(kAll[:, :, b * P:(b + 1) * P],
                               PS[:, 4 + b, :].rearrange("p (h r) -> p h r", h=4)).then_inc(S("kc_ev"), 1)
            nc.scalar.copy(kAll[:, :, PAST:PAST + DEC], kT[:, :, SEQ:R]).then_inc(S("kc_ev"), 1)

            def exps(p):
                t, h = PAIRS[p]
                nq, L = ROWS[t], KEYS[t]
                if p >= 2:
                    act.wait_ge(S("at_comb"), p - 1)
                for m in range(2):
                    act.wait_ge(S(f"at_max{m}"), p + 1)
                    nc.scalar.activation(E[0:nq, p % 2, m, 0:L],
                                         PS[0:nq, 2 * m:2 * m + 2, :].rearrange("p b n -> p (b n)")[:, 0:L],
                                         ACT.Exp, bias=nm[0:nq, p % 2, m:m + 1],
                                         accum_out=sums[0:nq, p % 2, m:m + 1]).then_inc(S(f"at_exp{m}"), 1)

            def probs_out(p):
                t, h = PAIRS[p]
                nq = ROWS[t]
                if p >= 2:
                    act.wait_ge(S("at_pv"), p - 1)
                for j, (f, n) in enumerate(FILLS[t]):
                    F = FIRST_FILL[p] + j
                    act.wait_ge(S("at_tr"), F + 1)
                    src = PS[:, 4 + F % 2, :].rearrange("p (b q) -> p b q", q=P)
                    dst = AT[:, p % 2, :].rearrange("p (b q) -> p b q", q=P)
                    if t < 8:
                        last = nc.scalar.copy(dst[:, f:f + n, :], src[:, 0:n, :])
                    else:
                        nc.scalar.copy(dst[:, 0:2, 0:nq], src[:, 0:2, 0:nq])
                        last = nc.scalar.copy(dst[0:DEC, 2, 0:nq], src[0:DEC, 2, 0:nq])
                    last.then_inc(S("at_tev"), 1)

            def head_out(p):
                t, h = PAIRS[p]
                nq = ROWS[t]
                act.wait_ge(S("at_pv"), p + 1)
                identity(oN[0:nq, t, h, :], PS[0:nq, 6 + p % 2, 0:P], scale=rsum[0:nq, p % 4, 0:1]).then_inc(S("at_o"), 1)
                act.wait_ge(S("at_o"), p + 1)
                if p >= 1:
                    act.wait_ge(S("at_ss"), p)
                nc.scalar.activation(ojunk[0:nq, :], oN[0:nq, t, h, :], ACT.Square,
                                     accum_out=sso[0:nq, t, h:h + 1]).then_inc(S("at_ss"), 1)

            for p in range(NP_ + 2):
                if p < NP_:
                    exps(p)
                if 1 <= p <= NP_:
                    probs_out(p - 1)
                if p >= 2:
                    head_out(p - 2)
            act.wait_ge(S("at_ss"), NP_)
            nc.scalar.activation(rso[:, :, :], sso[:, :, :], ACT.Sqrt, scale=1.0 / P,
                                 bias=epsT[:, 0:1]).then_inc(S("so_sqrt"), 1)
            for t in range(RT):
                nr = ROWS[t]
                act.wait_ge(S("so_tr"), t + 1)
                identity(xn0[0][:, 0:4, P * t:P * t + nr],
                         PS[:, 4 + t % 2, :].rearrange("p (h r) -> p h r", h=4)[:, :, 0:nr],
                         scale=subg[:, 0:1]).then_inc(S("so_hi"), 1)

            def out_projection(o):
                t, l, x = o["tag"], o["l"], o["y"]

                def w_hi(u, s):
                    reached(act, l, f"{t}_raw{s}", (u - s) * 8 + 16)
                    nc.scalar.copy(whi[:, s], wraw[:, s]).then_inc(S(f"{t}_hi"), 1)

                def step(k, s, more):
                    c = 8 * (o["n"] - 1) + k
                    if more:
                        reached(act, l, f"{t}_mm", k + 1)
                        w_hi(k + 2, s)
                    act.wait_ge(S("fin_h"), c + 1)
                    if not isinstance(k, int) or k > 0 or o["n"] > 1:
                        act.wait_ge(S("acc_done"), c)
                    finish_tile(act, identity, k, x, o["gain"])

                if l == 0:
                    act.wait_ge(S("so_tr"), RT)
                    act.wait_ge(S("st_v"), 32)
                    act.wait_ge(S("st_u"), 32)
                else:
                    act.wait_ge(S("st_v2"), 32)
                for s in range(2):
                    w_hi(s, s)
                for s in range(2):
                    step(s, s, True)
                with act.Fori(1, 3) as j:
                    for s in range(2):
                        step(2 * j + s, s, True)
                for s in range(2):
                    step(6 + s, s, False)

            def ffn(f):
                t, b, l = f["tag"], f["b"], f["l"]

                def w_hi(s, half, raw, count, freed):
                    reached(act, l, f"{t}_{'gv'[s]}raw", count)
                    if freed is not None:
                        reached(act, l, f"{t}_upmm", freed)
                    nc.scalar.copy(b.uphi[:, s], raw[:, :, half * P:(half + 1) * P]).then_inc(S(f"{t}_uphi"), 1)

                def tap(s, T):
                    k = "gv"[s]
                    col = T + FT * s
                    reached(act, l, f"{t}_{k}ext", T + 1)
                    nc.scalar.copy(edge[:, :, :, bass.ds(col, 1)],
                                   b.ext[:, s, 960:EXT].rearrange("p (a c) -> p a c", c=66)[:, :, 64:66].unsqueeze(3))
                    identity(b.c[:, s, :], b.ext[:, s, 0:EXT - 2], scale=par[:, 3 * l, bass.ds(col, 1)],
                             bias=par[:, 3 * l + 1, bass.ds(col + 44, 1)]).then_inc(S(f"{t}_{k}tap"), 1)

                def silu(T):
                    reached(act, l, f"{t}_gconv", T + 1)
                    nc.scalar.activation(b.c[:, 0, :], b.c[:, 0, :], ACT.Silu).then_inc(S(f"{t}_silu"), 1)

                def h_hi(T, s):
                    reached(act, l, f"{t}_h", T + 1)
                    nc.scalar.copy(b.hhi[:, s, :], b.ext[:, 1, 4:EXT]).then_inc(S(f"{t}_hhi"), 1)

                def d_hi(i, first):
                    reached(act, l, f"{t}_draw", 16 * i + 16)
                    if not first:
                        reached(act, l, f"{t}_dnmm", 8 * i)
                    nc.scalar.copy(b.dhi[:, :, :], draw[:, :, :]).then_inc(S(f"{t}_dhi"), 1)

                def block_(i, first, last):
                    if not first:
                        tap(1, 2 * i - 1)
                        h_hi(2 * i - 1, 1)
                    w_hi(1, 0, vraw, 16 * i + 16, None if first else 4 * i)
                    tap(0, 2 * i)
                    silu(2 * i)
                    w_hi(0, 1, graw, 16 * i + 16, 4 * i + 1)
                    d_hi(i, first)
                    tap(1, 2 * i)
                    w_hi(1, 1, vraw, 16 * i + 16, 4 * i + 2)
                    h_hi(2 * i, 0)
                    tap(0, 2 * i + 1)
                    silu(2 * i + 1)
                    if not last:
                        w_hi(0, 0, graw, 16 * i + 32, 4 * i + 3)

                reached(act, l, "op_mm", 8)
                w_hi(0, 0, graw, 16, None)
                act.wait_ge(S("n_stat"), f["n"])
                norm_act(act, f["n"], PS[:, 6, 0:RT])
                block_(0, True, False)
                with act.Fori(1, NB - 1) as i:
                    block_(i, False, False)
                block_(NB - 1, False, True)
                tap(1, 2 * NB - 1)
                h_hi(2 * NB - 1, 1)
                for k in range(KT):
                    c = 8 * f["n"] + k
                    act.wait_ge(S("fin_h"), c + 1)
                    act.wait_ge(S("acc_done"), c)
                    if k == 0 and f["y"]:
                        reached(act, l, f"{t}_upmm", 4 * NB)
                    finish_tile(act, identity, k, f["y"], f["gain"])
                act.wait_ge(S("ed_tr"), l + 1)
                if l == 1:
                    act.wait_ge(S("st_k2"), 32)
                nc.scalar.copy(edgeN[:, :, :], PS[0:2 * 2 * FT, 7, 0:256].rearrange("p (a c) -> p a c", a=2)).then_inc(S("ed_ev"), 1)
                act.wait_ge(S("ed_ev"), l + 1)
                for a, name in enumerate(("ffn_conv_prompt", "ffn_conv_sample")):
                    act.dma_start(io[name][l, 0].rearrange("i (t c) -> (i t) c", c=P), edgeN[:, a, :]).then_inc(S("st_e"), 16)

            out_projection(OUTP[0])
            ffn(FFN[0])

            def odd_hi(u, s):
                reached(act, 1, f"in_raw{s}", (u - s) * 8 + 16)
                if not isinstance(u, int) or u >= 2:
                    reached(act, 1, "in_mm", u - 1)
                nc.scalar.copy(whi[:, s], wraw[:, s]).then_inc(S("in_hi"), 1)

            def swap_bias(u):
                reached(act, 1, "in_ev", u + 1)
                if not isinstance(u, int) or u >= 1:
                    reached(act, 1, "in_rope", u)
                for c in range(4):
                    a = 32 * (c ^ 1)
                    last = identity(zs_o[32 * c:32 * c + 32, :], z_o[a:a + 32, :], bias=par[a:a + 32, 6, bass.ds(u + P_BIN, 1)])
                last.then_inc(S("in_sw"), 1)

            act.wait_ge(S("ff_vtap"), FT)
            for s in range(2):
                odd_hi(s, s)
            act.wait_ge(S("n_stat"), 2)
            norm_act(act, 2, PS[:, 6, 0:RT])
            for s in range(2):
                odd_hi(s + 2, s)
                swap_bias(s)
            with act.Fori(1, 4) as j:
                for s in range(2):
                    odd_hi(2 * j + s + 2, s)
                    swap_bias(2 * j + s)
            swap_bias(8)
            reached(act, 1, "in_rope", 9)
            for g in range(C_KV):
                for half in (0, 64):
                    last = nc.scalar.copy(kd[half:half + 64, g, :], z_o[64 * g:64 * g + 64, :])
            last.then_inc(S("oi_kd"), 1)
            act.wait_ge(S("oi_ktr"), 1)
            act.wait_ge(S("st_e"), 32)
            nc.scalar.copy(kn2[:, 0, :], PS[:, 6, 0:P]).then_inc(S("oi_kn"), 1)
            nc.scalar.copy(kn2[0:DEC, 1, :], PS[0:DEC, 6, P:2 * P]).then_inc(S("oi_kn"), 1)
            act.wait_ge(S("kc2_tr"), 1)
            for g in range(C_KV):
                for half in (0, 64):
                    nc.scalar.copy(kds[half:half + 64, g, 0:P], PS[64 * g:64 * g + 64, 7, 0:P])
            act.wait_ge(S("oi_kd"), 1)
            nc.scalar.copy(kds[:, :, P:P + DEC], kd[:, :, SEQ:R]).then_inc(S("oi_kds"), 1)
            for j, (a, n, nr) in enumerate(((0, 4, P), (4, 4, P), (8, 1, DEC))):
                act.wait_ge(S("oi_vtr"), j + 1)
                nc.scalar.copy(v2N[0:nr, a:a + n, :], PS[0:nr, 3 + j, 0:n * P].rearrange("p (t c) -> p t c", c=P)) \
                    .then_inc(S("oi_vn"), 1)

            def odd_exps(q):
                t, b = BATCHES[q]
                nq, (c0, c1), v = ROWS[t], WIN[t], q % 2
                act.wait_ge(S("o_nm"), q + 1)
                if q >= 2:
                    act.wait_ge(S("o_tr"), OFILL[q - 1])
                for i in range(4):
                    last = nc.scalar.activation(E2[0:nq, v, i, c0:c1],
                                                PS[0:nq, 2 * v + i // 2, (i % 2) * 256 + c0:(i % 2) * 256 + c1],
                                                ACT.Exp, bias=nm2[0:nq, v, i:i + 1], scale=C_DH ** -0.5,
                                                accum_out=sum2[0:nq, v, i:i + 1])
                last.then_inc(S("o_exp"), 1)
                nc.scalar.activation(es2[0:nq, v, :], snk2[0:nq, v, :], ACT.Exp).then_inc(S("o_es"), 1)

            for q in range(NQ + 2):
                if q < NQ:
                    odd_exps(q)
                if q >= 5 and q % 4 == 1:
                    odd_rows_hi(act, (q - 5) // 4)

            out_projection(OUTP[1])
            ffn(FFN[1])

            act.wait_ge(S("n_stat"), 4)
            norm_act(act, 4, PS[:, 6, 0:RT])
            act.wait_ge(S("n_rec"), 5)
            for t in range(RT):
                act.wait_ge(S("y_tr"), 2 * t + 1)
                identity(yN[0:ROWS[t], t, 0:512], PS[0:ROWS[t], 2 * t % 6, :], scale=rs[0:ROWS[t], t:t + 1]).then_inc(S("y_act"), 1)

        @block.vector
        def _(dve):
            tt = nc.vector.tensor_tensor

            def split_lo(dst, src, hi, scale=None):
                if scale is None:
                    return tt(dst, src, hi.bitcast(F32), ALU.subtract)
                return nc.vector.scalar_tensor_tensor(out=dst, in0=src, scalar=scale, in1=hi.bitcast(F32),
                                                      op0=ALU.mult, op1=ALU.subtract)

            def even_lo(u):
                reached(dve, 0, "in_hi", u + 1)
                split_lo(wlo[:, u % 2], wraw[:, u % 2], whi[:, u % 2]).then_inc(S("in_lo"), 1)

            for f in range(2 * RT):
                t, j = f // 2, f % 2
                nr = ROWS[t]
                dve.wait_ge(S("x_hi"), f + 1)
                cols = slice(P * t, P * t + nr)
                split_lo(xn0[1][:, 4 * j:4 * j + 4, cols], PS[:, f % 6, :].rearrange("p (k r) -> p k r", k=4)[:, :, 0:nr],
                         xn0[0][:, 4 * j:4 * j + 4, cols]).then_inc(S("x_lo"), 1)
            even_lo(0)
            even_lo(1)
            dve.wait_ge(S("pw_hi"), 1)
            split_lo(pwlo[:, :, :], pwraw[:, :, :], pwhi[:, :, :]).then_inc(S("pw_lo"), 1)
            dve.wait_ge(S("c_set"), C_IDENT)
            norm_dve_diag(dve, 0)
            dve.wait_ge(S("bc_in"), 48)
            tt(lamp[:, 0:4:2, :], lamp[:, 0:4:2, :], lamp[:, 1:4:2, :], ALU.mult).then_inc(S("lam"), 1)
            dve.wait_ge(S("lam"), 1)
            nc.vector.tensor_reduce(lam2[:, 0:2], lamp[:, 0:4:2, :], AX_X, ALU.add).then_inc(S("lam"), 1)
            nc.vector.tensor_scalar(subg[:, :], param(6, P_SUB), 1.0 - LAM_INIT, None, ALU.mult).then_inc(S("lam"), 1)
            norm_dve_rb(dve, 0)

            dve.wait_ge(S("n_rb"), 1)
            ropes = 0
            for u in range(16):
                g, kind, s = u // 4, u % 4, u % 2
                reached(dve, 0, "in_mm", u + 1)
                if kind < 2:
                    if ropes:
                        reached(dve, 0, "in_rope", ropes)
                    last = scaled_by_row(s, z_e)
                elif kind == 2:
                    if g >= 1:
                        dve.wait_ge(S("ei_tr"), 6 * g)
                    last = scaled_by_row(s, vz_e)
                else:
                    tt(uT[:, g, HIST:HIST + 728].rearrange("p (c n) -> p c n", c=2), PS[:, 3 * s:3 * s + 2, 0:364],
                       rB[:, 0:728].rearrange("p (c n) -> p c n", c=2), ALU.mult)
                    tt(uT[:, g, HIST + 728:HIST + SEQ], PS[:, 3 * s + 2, 0:SEQ - 728], rB[:, 728:SEQ], ALU.mult)
                    last = tt(uT[:, g, U_S:UEXT], PS[:, 3 * s + 2, SEQ - 728:360], rB[:, SEQ:R], ALU.mult)
                last.then_inc(S("in_ev"), 1)
                if u + 2 < 16:
                    even_lo(u + 2)
                if kind < 2:
                    if ropes == 0:
                        dve.wait_ge(S("tab_in"), 96)
                    ropes += 1
                    by = 1.0 if kind else A_DH ** -0.5
                    reached(dve, 0, "in_sw", ropes)
                    nc.vector.scalar_tensor_tensor(out=z_e[:, :], in0=z_e[:, :], scalar=by, in1=cos_e[:, :],
                                                   op0=ALU.mult, op1=ALU.mult)
                    nc.vector.scalar_tensor_tensor(out=zs_e[:, :], in0=zs_e[:, :], scalar=by, in1=sin_e[:, :],
                                                   op0=ALU.mult, op1=ALU.mult).then_inc(S("in_rz"), 1)
                    reached(dve, 0, "in_rz", ropes)
                    tt((kT if kind else qT)[:, g, :], z_e[:, :], zs_e[:, :], ALU.add).then_inc(S("in_rope"), 1)
            dve.wait_ge(S("ei_tr"), 24)
            for k in range(5):
                last = tt(H[:, k, :], xn0[0][:, k, :].bitcast(F32), xn0[1][:, k, :].bitcast(F32), ALU.add)
            last.then_inc(S("h_dve"), 1)
            dve.wait_ge(S("lam_exp"), 1)
            nc.vector.scalar_tensor_tensor(out=neglam[:, :], in0=lam2[:, 3:4], scalar=-LAM_INIT, in1=lam2[:, 2:3],
                                           op0=ALU.add, op1=ALU.subtract).then_inc(S("lam"), 1)

            def pool_lo(g):
                dve.wait_ge(S("pm_hi"), g + 1)
                for (src, dst), (_, hi) in zip(pieces(g % 2, xn0[1][:, 4 + g, :]), pieces(g % 2, xn0[0][:, 4 + g, :])):
                    last = split_lo(dst, src, hi, param(6, P_PS + g))
                last.then_inc(S("pm_ev"), 1)

            for g in range(4):
                dve.wait_ge(S("pm_phi"), g + 1)
                split_lo(plo[:, g % 2, 0:SEQ], uT[:, g, HIST:HIST + SEQ], phi[:, g % 2, 0:SEQ])
                split_lo(plo[:, g % 2, SEQ:R], uT[:, g, U_S:UEXT], phi[:, g % 2, SEQ:R]).then_inc(S("pm_plo"), 1)
                if g >= 1:
                    pool_lo(g - 1)
            pool_lo(3)

            def maxes(p):
                t, h = PAIRS[p]
                nq, L = ROWS[t], KEYS[t]
                for m in range(2):
                    dve.wait_ge(S(f"at_s{m}"), p + 1)
                    nc.vector.tensor_reduce(nm[0:nq, p % 2, m:m + 1],
                                            PS[0:nq, 2 * m:2 * m + 2, :].rearrange("p b n -> p (b n)")[:, 0:L],
                                            AX_X, ALU.max, negate=True).then_inc(S(f"at_max{m}"), 1)

            def combine(p):
                t, h = PAIRS[p]
                nq, L = ROWS[t], KEYS[t]
                for m in range(2):
                    dve.wait_ge(S(f"at_exp{m}"), p + 1)
                if p >= 4:
                    dve.wait_ge(S("at_o"), p - 3)
                nc.vector.reciprocal(rsum[0:nq, p % 4, :], sums[0:nq, p % 2, :]).then_inc(S("at_r"), 1)
                dve.wait_ge(S("at_r"), 2 * p + 1)
                nc.vector.tensor_scalar(cc[0:nq, p % 2:p % 2 + 1], sums[0:nq, p % 2, 0:1], rsum[0:nq, p % 4, 1:2],
                                        neglam[0:nq, :], ALU.mult, ALU.mult).then_inc(S("at_r"), 1)
                dve.wait_ge(S("at_r"), 2 * p + 2)
                if p >= 2:
                    dve.wait_ge(S("at_tr"), FIRST_FILL[p - 1])
                nc.vector.scalar_tensor_tensor(out=comb[0:nq, p % 2, 0:L], in0=E[0:nq, p % 2, 1, 0:L],
                                               scalar=cc[0:nq, p % 2:p % 2 + 1], in1=E[0:nq, p % 2, 0, 0:L],
                                               op0=ALU.mult, op1=ALU.add).then_inc(S("at_comb"), 1)

            dve.wait_ge(S("lam"), 4)
            for p in range(NP_ + 1):
                if p >= 1:
                    combine(p - 1)
                if p < NP_:
                    maxes(p)
            dve.wait_ge(S("so_sqrt"), 1)
            nc.vector.reciprocal(rso[:, :, :], rso[:, :, :]).then_inc(S("so_rec"), 1)
            dve.wait_ge(S("so_rec"), 1)
            for t in range(RT + 1):
                if t < RT:
                    nr = ROWS[t]
                    tt(oN[0:nr, t], oN[0:nr, t], rso[0:nr, t, :].unsqueeze(2).to_broadcast([nr, A_H, P]), ALU.mult) \
                        .then_inc(S("so_n"), 1)
                if t >= 1:
                    nr, cols = ROWS[t - 1], slice(P * (t - 1), P * (t - 1) + ROWS[t - 1])
                    dve.wait_ge(S("so_hi"), t)
                    split_lo(xn0[1][:, 0:4, cols], PS[:, 4 + (t - 1) % 2, :].rearrange("p (h r) -> p h r", h=4)[:, :, 0:nr],
                             xn0[0][:, 0:4, cols], subg[:, 0:1]).then_inc(S("so_lo"), 1)

            def add_residual(s, k):
                for (src, dst) in pieces(s, H[:, bass.ds(k, 1), :].rearrange("p k r -> p (k r)")):
                    last = tt(dst, src, dst, ALU.add)
                last.then_inc(S("fin_h"), 1)

            def finish_lo(k, c, x, gain):
                if x:
                    dve.wait_ge(S("fin_hi"), c + 1)
                    split_lo(x[1][:, bass.ds(k, 1), :], H[:, bass.ds(k, 1), :], x[0][:, bass.ds(k, 1), :],
                             par[:, 6, bass.ds(k + gain, 1)]).then_inc(S("fin_lo"), 1)
                dve.wait_ge(S("fin_sq"), c + 1)
                if not isinstance(c, int) or c > 0:
                    dve.wait_ge(S("acc_done"), c)
                tt(acc[:, 0:R], acc[:, 0:R], sq[:, :], ALU.add).then_inc(S("acc_done"), 1)

            def out_projection(o):
                t, l = o["tag"], o["l"]

                def w_lo(u, s):
                    reached(dve, l, f"{t}_hi", u + 1)
                    split_lo(wlo[:, s], wraw[:, s], whi[:, s]).then_inc(S(f"{t}_lo"), 1)

                def step(k, s, more):
                    reached(dve, l, f"{t}_mm", k + 1)
                    add_residual(s, k)
                    if more:
                        w_lo(k + 2, s)
                    finish_lo(k, 8 * (o["n"] - 1) + k, o["y"], o["gain"])

                for s in range(2):
                    w_lo(s, s)
                dve.wait_ge(S("acc_zero"), o["n"])
                for s in range(2):
                    step(s, s, True)
                with dve.Fori(1, 3) as j:
                    for s in range(2):
                        step(2 * j + s, s, True)
                for s in range(2):
                    step(6 + s, s, False)

            def ffn(f):
                t, b, l = f["tag"], f["b"], f["l"]

                def w_lo(s, half, raw, count):
                    reached(dve, l, f"{t}_uphi", count)
                    split_lo(b.uplo[:, s], raw[:, :, half * P:(half + 1) * P], b.uphi[:, s]).then_inc(S(f"{t}_uplo"), 1)

                def extend(s, T, count, ps):
                    e = b.ext[:, s, :]
                    reached(dve, l, f"{t}_upmm", count)
                    nc.vector.tensor_copy(e[:, 2 + SEQ:4 + SEQ].unsqueeze(2),
                                          par[:, 3 * l + 2, :].rearrange("p (i t) -> p i t", i=2)[:, :, bass.ds(T + FT * s, 1)])
                    tt(e[:, 2:730].rearrange("p (c n) -> p c n", c=2), PS[:, 3 * ps:3 * ps + 2, 0:364],
                       rB[:, 0:728].rearrange("p (c n) -> p c n", c=2), ALU.mult)
                    tt(e[:, 730:2 + SEQ], PS[:, 3 * ps + 2, 0:SEQ - 728], rB[:, 728:SEQ], ALU.mult)
                    tt(e[:, 4 + SEQ:EXT], PS[:, 3 * ps + 2, SEQ - 728:360], rB[:, SEQ:R], ALU.mult) \
                        .then_inc(S(f"{t}_{'gv'[s]}ext"), 1)

                def taps(s, T):
                    k, col = "gv"[s], T + FT * s
                    e, c = b.ext[:, s, :], b.c[:, s, :]
                    reached(dve, l, f"{t}_{k}tap", T + 1)
                    nc.vector.scalar_tensor_tensor(out=c, in0=e[:, 1:EXT - 1], scalar=par[:, 3 * l, bass.ds(col + 44, 1)],
                                                   in1=c, op0=ALU.mult, op1=ALU.add).then_inc(S(f"{t}_{k}mid"), 1)
                    reached(dve, l, f"{t}_{k}mid", T + 1)
                    nc.vector.scalar_tensor_tensor(out=c, in0=e[:, 2:EXT], scalar=par[:, 3 * l + 1, bass.ds(col, 1)],
                                                   in1=c, op0=ALU.mult, op1=ALU.add).then_inc(S(f"{t}_{k}conv"), 1)

                def gate(T, s):
                    reached(dve, l, f"{t}_silu", T + 1)
                    reached(dve, l, f"{t}_vconv", T + 1)
                    h = b.ext[:, 1, 4:EXT]
                    tt(h[:, 0:SEQ], b.c[:, 0, 0:SEQ], b.c[:, 1, 0:SEQ], ALU.mult)
                    tt(h[:, SEQ:R], b.c[:, 0, SEQ + 2:EXT - 2], b.c[:, 1, SEQ + 2:EXT - 2], ALU.mult).then_inc(S(f"{t}_h"), 1)
                    reached(dve, l, f"{t}_hhi", T + 1)
                    split_lo(b.hlo[:, s, :], h, b.hhi[:, s, :]).then_inc(S(f"{t}_hlo"), 1)

                def down(i):
                    for k in range(KT):
                        reached(dve, l, f"{t}_dnmm", 8 * i - 7 + k)
                        for src, dst in pieces((k + 1) % 2, H[:, k, :]):
                            last = tt(dst, src, dst, ALU.add)
                        last.then_inc(S(f"{t}_dnev"), 1)

                def block_(i, first, last):
                    if not first:
                        extend(1, 2 * i - 1, 4 * i, 1)
                        taps(1, 2 * i - 1)
                        gate(2 * i - 1, 1)
                    w_lo(1, 0, vraw, 4 * i + 2)
                    if first:
                        norm_dve_rb(dve, f["n"])
                        dve.wait_ge(S("n_rb"), f["n"] + 1)
                    extend(0, 2 * i, 4 * i + 1, 0)
                    taps(0, 2 * i)
                    w_lo(0, 1, graw, 4 * i + 3)
                    if not first:
                        down(i)
                    reached(dve, l, f"{t}_dhi", i + 1)
                    split_lo(b.dlo[:, :, :], draw[:, :, :], b.dhi[:, :, :]).then_inc(S(f"{t}_dlo"), 1)
                    extend(1, 2 * i, 4 * i + 2, 1)
                    taps(1, 2 * i)
                    w_lo(1, 1, vraw, 4 * i + 4)
                    gate(2 * i, 0)
                    extend(0, 2 * i + 1, 4 * i + 3, 0)
                    taps(0, 2 * i + 1)
                    if not last:
                        w_lo(0, 0, graw, 4 * i + 5)

                reached(dve, l, "op_mm", 8)
                for s in range(2):
                    last = nc.vector.memset(b.ext[:, s, 0:2], 0.0)
                w_lo(0, 0, graw, 1)
                norm_dve_diag(dve, f["n"])
                block_(0, True, False)
                with dve.Fori(1, NB - 1) as i:
                    block_(i, False, False)
                block_(NB - 1, False, True)
                extend(1, 2 * NB - 1, 4 * NB, 1)
                taps(1, 2 * NB - 1)
                gate(2 * NB - 1, 1)
                dve.wait_ge(S("acc_zero"), f["n"] + 1)
                for k in range(KT + 1):
                    c = 8 * f["n"] + k
                    if k < KT:
                        reached(dve, l, f"{t}_dnmm", 8 * NB - 7 + k)
                        add_residual((k + 1) % 2, k)
                    if k >= 1:
                        finish_lo(k - 1, c - 1, f["y"], f["gain"])
                        if f["y"] is None:
                            nc.vector.tensor_scalar(H[:, k - 1, :], H[:, k - 1, :], param(6, P_NFIN + k - 1), None,
                                                    ALU.mult).then_inc(S("fin_g"), 1)

            out_projection(OUTP[0])
            ffn(FFN[0])

            def odd_lo(u, s):
                reached(dve, 1, "in_hi", u + 1)
                split_lo(wlo[:, s], wraw[:, s], whi[:, s]).then_inc(S("in_lo"), 1)

            def odd_rope(u, out):
                b = par[:, 6, bass.ds(u + P_BIN, 1)]
                reached(dve, 1, "in_sw", u + 1)
                nc.vector.scalar_tensor_tensor(out=z_o[:, :], in0=z_o[:, :], scalar=b, in1=cos_o[:, :],
                                               op0=ALU.add, op1=ALU.mult)
                tt(zs_o[:, :], zs_o[:, :], sin_o[:, :], ALU.mult).then_inc(S("in_rz"), 1)
                reached(dve, 1, "in_rz", u + 1)
                tt(out, z_o[:, :].unsqueeze(1), zs_o[:, :].unsqueeze(1), ALU.add).then_inc(S("in_rope"), 1)

            def odd_unit(u, s, more, out):
                reached(dve, 1, "in_mm", u + 1)
                if not isinstance(u, int) or u:
                    reached(dve, 1, "in_rope", u)
                scaled_by_row(s, z_o).then_inc(S("in_ev"), 1)
                if more:
                    odd_lo(u + 2, s)
                odd_rope(u, out)

            for s in range(2):
                odd_lo(s, s)
            norm_dve_diag(dve, 2)
            norm_dve_rb(dve, 2)
            dve.wait_ge(S("n_rb"), 3)
            dve.wait_ge(S("tab_in"), 192)
            for s in range(2):
                odd_unit(s, s, True, q2T[:, s:s + 1, :])
            with dve.Fori(1, 4) as j:
                for s in range(2):
                    odd_unit(2 * j + s, s, True, q2T[:, bass.ds(2 * j + s, 1), :])
            odd_unit(8, 0, False, z_o[:, :].unsqueeze(1))
            reached(dve, 1, "in_mm", 10)
            scaled_by_row(1, vz_o).then_inc(S("in_ev"), 1)
            reached(dve, 1, "in_ev", 10)
            nc.vector.tensor_scalar(vz_o[:, :], vz_o[:, :], param(6, P_BIN + 9), None, ALU.add).then_inc(S("oi_vz"), 1)

            def by_head(x):
                return x.rearrange("p (j a) -> p a j", a=2)

            def quad(x):
                return x.rearrange("p (a j) -> p a j", a=2)

            def odd_max(q):
                t, b = BATCHES[q]
                nq, (c0, c1), v = ROWS[t], WIN[t], q % 2
                dve.wait_ge(S("o_s"), q + 1)
                if q >= 2:
                    dve.wait_ge(S("o_es"), q - 1)
                nc.vector.tensor_reduce(m2[0:nq, v, :],
                                        PS[0:nq, 2 * v:2 * v + 2, :].rearrange("p b (j c) -> p (b j) c", j=2)[:, :, c0:c1],
                                        AX_X, ALU.max).then_inc(S("o_m"), 1)
                dve.wait_ge(S("o_m"), 2 * q + 1)
                sink = by_head(sinkb[0:nq, 4 * b:4 * b + 4])
                nc.vector.scalar_tensor_tensor(out=quad(m2[0:nq, v, :]), in0=quad(m2[0:nq, v, :]), scalar=C_DH ** -0.5,
                                               in1=sink, op0=ALU.mult, op1=ALU.max).then_inc(S("o_m"), 1)
                dve.wait_ge(S("o_m"), 2 * q + 2)
                tt(quad(snk2[0:nq, v, :]), sink, quad(m2[0:nq, v, :]), ALU.subtract)
                nc.vector.tensor_scalar(nm2[0:nq, v, :], m2[0:nq, v, :], -1.0, None, ALU.mult).then_inc(S("o_nm"), 1)

            def odd_den(q):
                nq, v = ROWS[BATCHES[q][0]], q % 2
                dve.wait_ge(S("o_es"), q + 1)
                dve.wait_ge(S("o_exp"), q + 1)
                tt(den2[0:nq, v, :], sum2[0:nq, v, :], es2[0:nq, v, :], ALU.add).then_inc(S("o_rd"), 1)
                dve.wait_ge(S("o_rd"), 2 * q + 1)
                nc.vector.reciprocal(rd2[0:nq, v, :], den2[0:nq, v, :]).then_inc(S("o_rd"), 1)

            def odd_out(q):
                t, b = BATCHES[q]
                nq, v = ROWS[t], q % 2
                dve.wait_ge(S("o_pv"), q + 1)
                dve.wait_ge(S("o_rd"), 2 * q + 2)
                if b == 0 and t >= 1:
                    dve.wait_ge(S("om_tr"), 2 * t)
                tt(oN2[0:nq, 256 * b:256 * b + 256].rearrange("p (j a d) -> p a j d", j=2, a=2),
                   PS[0:nq, 6 + v, 0:256].rearrange("p (a j d) -> p a j d", a=2, j=2),
                   quad(rd2[0:nq, v, :]).unsqueeze(3).to_broadcast([nq, 2, 2, C_DH]), ALU.mult).then_inc(S("o_o"), 1)

            def odd_probs(q):
                t, b = BATCHES[q]
                nq, v = ROWS[t], q % 2
                if q >= 2:
                    dve.wait_ge(S("o_pv"), q - 1)
                for n, kt in enumerate(key_tiles(t)):
                    bs = DEC if (t == 8 and kt == 1) else P
                    dve.wait_ge(S("o_tr"), OFILL[q] + n + 1)
                    nc.vector.tensor_copy(PT2[0:bs, v, kt, :, 0:nq],
                                          PS[0:bs, 4 + kt, :].rearrange("p (i q) -> p i q", i=4)[:, :, 0:nq]).then_inc(S("o_tev"), 1)

            def odd_rows_lo(t):
                nr = ROWS[t]
                for j in range(2):
                    dve.wait_ge(S("om_hi"), 2 * t + j + 1)
                    split_lo(xn1[1][:, 4 * j:4 * j + 4, P * t:P * t + nr],
                             PS[:, 4 + j, :].rearrange("p (k r) -> p k r", k=4)[:, :, 0:nr],
                             xn1[0][:, 4 * j:4 * j + 4, P * t:P * t + nr]).then_inc(S("om_lo"), 1)

            for q in range(NQ + 2):
                if q < NQ:
                    odd_max(q)
                if 1 <= q <= NQ:
                    odd_den(q - 1)
                if q >= 2:
                    odd_out(q - 2)
                if q >= 5 and q % 4 == 1:
                    odd_rows_lo((q - 5) // 4)
                if 1 <= q <= NQ:
                    odd_probs(q - 1)

            out_projection(OUTP[1])
            ffn(FFN[1])

            norm_dve_diag(dve, 4)
            dve.wait_ge(S("n_rec"), 5)
            for t in range(RT):
                dve.wait_ge(S("y_tr"), 2 * t + 2)
                nc.vector.tensor_scalar(yN[0:ROWS[t], t, 512:1024], PS[0:ROWS[t], (2 * t + 1) % 6, :],
                                        rs[0:ROWS[t], t:t + 1], None, ALU.mult).then_inc(S("y_dve"), 1)

        @block.tensor
        def _(pe):
            pe.wait_ge(S("c_set"), C_IDENT)

            def params_in():
                pe.wait_ge(S("par_in"), 16 * 15)
                for n in range(P_TILES):
                    nr = P_ROWS6 if n == 6 else 88
                    col = 88 * (n % 4)
                    last = nc.tensor.transpose(PS[:, 6 + n // 4, col:col + nr], pnat[0:nr, n, :], ident[0:nr, 0:nr])
                    if n == 3:
                        last.then_inc(S("par_tr"), 1)
                for g in range(4):
                    last = nc.tensor.transpose(PS[:, 7, 240 + HIST * g:240 + HIST * (g + 1)], hnat[:, g * P:(g + 1) * P],
                                               ident[0:HIST, 0:HIST])
                last.then_inc(S("par_tr"), 1)

            for t in range(RT):
                nr = ROWS[t]
                pe.wait_ge(S(X_IN[t]), 16)
                for j in range(2):
                    f = 2 * t + j
                    if f >= 6:
                        pe.wait_ge(S("x_lo"), f - 5)
                    for i in range(4):
                        k = 4 * j + i
                        last = nc.tensor.transpose(PS[:, f % 6, i * P:i * P + nr], xnat[0:nr, t, k * P:(k + 1) * P],
                                                   ident[0:nr, 0:nr])
                    last.then_inc(S("x_tr"), 1)
                if t == 2:
                    params_in()

            def to_rows(src, f):
                for j, (a, n) in enumerate(((0, 4), (4, 4), (8, 1))):
                    if f + j >= 2:
                        pe.wait_ge(S("ei_tev"), f + j - 1)
                    for i in range(n):
                        t = a + i
                        last = nc.tensor.transpose(PS[0:ROWS[t], 6 + (f + j) % 2, i * P:(i + 1) * P], src[:, rows_of(t)], ident[:, :])
                    last.then_inc(S("ei_tr"), 1)

            pe.wait_ge(S("x_lo"), 2 * RT)
            for u in range(16):
                g, s = u // 4, u % 2
                reached(pe, 0, "in_lo", u + 1)
                if u == 1:
                    pe.wait_ge(S("n_rb"), 1)
                if u >= 2:
                    reached(pe, 0, "in_ev", u - 1)
                for k in range(KT):
                    last = products(s, k, KT, whi[:, s, k, :], wlo[:, s, k, :], xn0[0][:, k, :], xn0[1][:, k, :])
                last.then_inc(S("in_mm"), 1)
                if u == 0:
                    norm_pe_bcast(pe, 0)
                if u % 4 == 3:
                    reached(pe, 0, "in_rope", 2 * g + 2)
                    to_rows(kT[:, g, :], 6 * g)
                    reached(pe, 0, "in_ev", 4 * g + 3)
                    to_rows(vz_e, 6 * g + 3)

            pe.wait_ge(S("pw_lo"), 1)
            reached(pe, 0, "in_ev", 16)
            for g in range(4):
                pe.wait_ge(S("pm_plo"), g + 1)
                if g >= 2:
                    pe.wait_ge(S("pm_ev"), g - 1)
                products(g % 2, 0, 1, pwhi[:, g, :], pwlo[:, g, :], phi[:, g % 2, :], plo[:, g % 2, :]).then_inc(S("pm_mm"), 1)
            pe.wait_ge(S("ei_tev"), 24)
            pe.wait_ge(S("ei_ue"), 4)
            for st in range(2):
                for g in range(4):
                    last = nc.tensor.transpose(PS[0:HIST, 6 + st, g * P:(g + 1) * P], ue[:, g, st, :], ident[:, :])
            last.then_inc(S("ue_tr"), 1)
            pe.wait_ge(S("kc_in"), 16)
            pe.wait_ge(S("pm_ev"), 4)
            for b in range(2):
                for h in range(A_H):
                    last = nc.tensor.transpose(PS[:, 4 + b, h * P:(h + 1) * P], kcn[:, b, h * P:(h + 1) * P], ident[:, :])
                last.then_inc(S("kc_tr"), 1)

            def scores(p):
                t, h = PAIRS[p]
                nq, L = ROWS[t], KEYS[t]
                for m in range(2):
                    if p >= 1:
                        pe.wait_ge(S(f"at_exp{m}"), p)
                for a in range(0, L, 512):
                    w = min(512, L - a)
                    masked = t < 8 and a + w == L
                    for m in range(2):
                        half = slice(64 * m, 64 * m + 64)
                        keys = kT[half, h, a:a + w] if t < 8 else kAll[half, h, a:a + w]
                        last = nc.tensor.matmul(PS[0:nq, 2 * m + a // 512, 0:w], qT[half, h, rows_of(t)], keys,
                                                start=True, stop=not masked)
                        if masked:
                            last = nc.tensor.matmul(PS[0:nq, 2 * m + a // 512, w - 64:w], maskL[half, :], maskR[half, 0, 192:256],
                                                    start=False, stop=True)
                        if a + w == L:
                            last.then_inc(S(f"at_s{m}"), 1)

            def probs(p):
                t, h = PAIRS[p]
                nq = ROWS[t]
                pe.wait_ge(S("at_comb"), p + 1)
                for j, (f, n) in enumerate(FILLS[t]):
                    F = FIRST_FILL[p] + j
                    if F >= 2:
                        pe.wait_ge(S("at_tev"), F - 1)
                    for i in range(n):
                        a, w = BLOCKS[t][f + i]
                        last = nc.tensor.transpose(PS[0:w, 4 + F % 2, i * P:i * P + nq], comb[0:nq, p % 2, a:a + w], ident[0:nq, 0:nq])
                    last.then_inc(S("at_tr"), 1)

            def values(p):
                t, h = PAIRS[p]
                nq = ROWS[t]
                pe.wait_ge(S("at_tev"), FIRST_FILL[p + 1])
                if p >= 2:
                    pe.wait_ge(S("at_o"), p - 1)
                n = len(BLOCKS[t])
                for b, (a, w) in enumerate(BLOCKS[t]):
                    if t < 8:
                        v = vN[0:w, b, h * P:(h + 1) * P]
                    else:
                        v = vcn[:, b, h * P:(h + 1) * P] if b < 2 else vN[0:DEC, 8, h * P:(h + 1) * P]
                    last = nc.tensor.matmul(PS[0:nq, 6 + p % 2, 0:P], AT[0:w, p % 2, b * P:b * P + nq], v,
                                            start=b == 0, stop=b == n - 1)
                last.then_inc(S("at_pv"), 1)

            pe.wait_ge(S("kc_ev"), 3)
            pe.wait_ge(S("vc_in"), 16)
            pe.wait_ge(S("ue_ev"), 1)
            pe.wait_ge(S("c_set"), C_ALL)
            for p in range(NP_ + 1):
                if p < NP_:
                    scores(p)
                if p >= 1:
                    probs(p - 1)
                    values(p - 1)
            for t in range(RT):
                nr = ROWS[t]
                pe.wait_ge(S("so_n"), t + 1)
                if t >= 2:
                    pe.wait_ge(S("so_lo"), t - 1)
                for h in range(A_H):
                    last = nc.tensor.transpose(PS[:, 4 + t % 2, h * P:h * P + nr], oN[0:nr, t, h, :], ident[0:nr, 0:nr])
                last.then_inc(S("so_tr"), 1)

            def out_projection(o):
                t, l, x = o["tag"], o["l"], o["x"]
                c0 = 8 * (o["n"] - 1)

                def unit(u, s, free):
                    reached(pe, l, f"{t}_lo", u + 1)
                    if free is not None:
                        pe.wait_ge(S("fin_h"), free)
                    for n, k in enumerate(o["ks"]):
                        last = products(s, n, KT, whi[:, s, k, :], wlo[:, s, k, :], x[0][:, k, :], x[1][:, k, :])
                    last.then_inc(S(f"{t}_mm"), 1)

                for s in range(2):
                    unit(s, s, None)
                with pe.Fori(1, 4) as j:
                    for s in range(2):
                        unit(2 * j + s, s, c0 + 2 * j + s - 1)

            def ffn(f):
                t, b, l, x = f["tag"], f["b"], f["l"], f["x"]

                def up(s, ps, count):
                    reached(pe, l, f"{t}_uplo", count)
                    for k in range(KT):
                        last = products(ps, k, KT, b.uphi[:, s, k, :], b.uplo[:, s, k, :], x[0][:, k, :], x[1][:, k, :])
                    last.then_inc(S(f"{t}_upmm"), 1)

                def first_gate():
                    reached(pe, l, f"{t}_uplo", 1)
                    for k in range(KT):
                        pe.wait_ge(S("fin_lo"), 8 * f["l"] * 2 + k + 1)
                        last = products(0, k, KT, b.uphi[:, 0, k, :], b.uplo[:, 0, k, :], x[0][:, k, :], x[1][:, k, :])
                    last.then_inc(S(f"{t}_upmm"), 1)

                def down(i, final):
                    reached(pe, l, f"{t}_dlo", i)
                    reached(pe, l, f"{t}_hlo", 2 * i)
                    for k in range(KT):
                        if k == 0:
                            reached(pe, l, f"{t}_vext", 2 * i)
                        elif k == 1:
                            reached(pe, l, f"{t}_gext", 2 * i if final else 2 * i + 1)
                        elif final:
                            pe.wait_ge(S("fin_h"), 8 * f["n"] + k - 1)
                        else:
                            reached(pe, l, f"{t}_dnev", 8 * i - 8 + k - 1)
                        for n in range(2):
                            c = slice(k * P, (k + 1) * P)
                            last = products((k + 1) % 2, n, 2, b.dhi[:, n, c], b.dlo[:, n, c], b.hhi[:, n, :], b.hlo[:, n, :])
                        last.then_inc(S(f"{t}_dnmm"), 1)

                def rest(i, first):
                    if not first:
                        reached(pe, l, f"{t}_dnev", 8 * i - 1)
                    up(1, 1, 4 * i + 2)
                    if first:
                        reached(pe, l, f"{t}_gext", 1)
                    else:
                        reached(pe, l, f"{t}_dnev", 8 * i)
                    up(0, 0, 4 * i + 3)
                    reached(pe, l, f"{t}_vext", 2 * i + 1)
                    up(1, 1, 4 * i + 4)

                c0 = 8 * f["n"]
                pe.wait_ge(S("fin_h"), c0 - 1)
                first_gate()
                norm_pe_stats(pe, f["n"])
                pe.wait_ge(S("fin_h"), c0)
                norm_pe_bcast(pe, f["n"])
                pe.wait_ge(S("n_rb"), f["n"] + 1)
                rest(0, True)
                with pe.Fori(1, NB) as i:
                    reached(pe, l, f"{t}_gext", 2 * i)
                    up(0, 0, 4 * i + 1)
                    down(i, False)
                    rest(i, False)
                down(NB, True)
                reached(pe, l, f"{t}_vtap", FT)
                for a in range(2):
                    last = nc.tensor.transpose(PS[0:4 * FT, 7, a * P:(a + 1) * P],
                                               edge[:, a, :, :].rearrange("p i t -> p (i t)"), ident[:, :])
                last.then_inc(S("ed_tr"), 1)

            out_projection(OUTP[0])
            ffn(FFN[0])

            def odd_unit(u, s, free):
                reached(pe, 1, "in_lo", u + 1)
                if free is not None:
                    reached(pe, 1, "in_ev", free)
                for k in range(KT):
                    if free is None:
                        pe.wait_ge(S("fin_lo"), 8 + k + 1)
                    last = products(s, k, KT, whi[:, s, k, :], wlo[:, s, k, :], xn1[0][:, k, :], xn1[1][:, k, :])
                last.then_inc(S("in_mm"), 1)

            pe.wait_ge(S("fin_h"), 16)
            odd_unit(0, 0, None)
            norm_pe_stats(pe, 2)
            norm_pe_bcast(pe, 2)
            pe.wait_ge(S("n_rb"), 3)
            odd_unit(1, 1, None)
            with pe.Fori(1, 5) as j:
                for s in range(2):
                    odd_unit(2 * j + s, s, 2 * j + s - 1)
            reached(pe, 1, "in_rope", 9)
            pe.wait_ge(S("ed_ev"), 1)
            nc.tensor.transpose(PS[:, 6, 0:P], z_o[:, 7 * P:8 * P], ident[:, :])
            nc.tensor.transpose(PS[0:DEC, 6, P:2 * P], z_o[:, SEQ:R], ident[:, :]).then_inc(S("oi_ktr"), 1)
            pe.wait_ge(S("kc_in"), 32)
            nc.tensor.transpose(PS[:, 7, 0:P], kc2n[:, :], ident[:, :]).then_inc(S("kc2_tr"), 1)
            pe.wait_ge(S("oi_vz"), 1)
            for j, (a, n) in enumerate(((0, 4), (4, 4), (8, 1))):
                for i in range(n):
                    t = a + i
                    last = nc.tensor.transpose(PS[0:ROWS[t], 3 + j, i * P:(i + 1) * P], vz_o[:, rows_of(t)], ident[:, :])
                last.then_inc(S("oi_vtr"), 1)

            def odd_scores(q):
                t, b = BATCHES[q]
                nq, (c0, c1), v = ROWS[t], WIN[t], q % 2
                if q >= 2:
                    pe.wait_ge(S("o_exp"), q - 1)
                for jj in range(2):
                    for par_ in range(2):
                        half = slice(64 * par_, 64 * par_ + 64)
                        if t < 8:
                            keys = kd[half, b // 2, (t - 1) * P + c0:(t - 1) * P + c1]
                        else:
                            keys = kds[half, b // 2, 0:c1]
                        last = nc.tensor.matmul(PS[0:nq, 2 * v + par_, jj * 256 + c0:jj * 256 + c1], q2T[half, 2 * b + jj, rows_of(t)],
                                                keys, start=jj == 0, stop=t == 8 and jj == 1, skip_group_check=True)
                if t < 8:
                    for par_ in range(2):
                        half = slice(64 * par_, 64 * par_ + 64)
                        last = nc.tensor.matmul(PS[0:nq, 2 * v + par_, :].rearrange("p (j c) -> p j c", j=2)[:, :, c0:c1],
                                                maskL[half, :], maskR[half, :, c0:c1], start=False, stop=True,
                                                skip_group_check=True)
                last.then_inc(S("o_s"), 1)

            def odd_probs(q):
                t, b = BATCHES[q]
                nq, v = ROWS[t], q % 2
                pe.wait_ge(S("o_exp"), q + 1)
                if q >= 1:
                    pe.wait_ge(S("o_tev"), OFILL[q])
                if q % 4 == 0 and q >= 4:
                    pe.wait_ge(S("om_lo"), q // 2)
                for kt in key_tiles(t):
                    bs = DEC if (t == 8 and kt == 1) else P
                    for i in range(4):
                        last = nc.tensor.transpose(PS[0:bs, 4 + kt, i * P:i * P + nq], E2[0:nq, v, i, kt * P:kt * P + bs], ident[0:nq, 0:nq])
                    last.then_inc(S("o_tr"), 1)

            def odd_values(q):
                t, b = BATCHES[q]
                nq, v, g = ROWS[t], q % 2, b // 2
                pe.wait_ge(S("o_tev"), OFILL[q + 1])
                if q >= 2:
                    pe.wait_ge(S("o_o"), q - 1)
                kts = key_tiles(t)
                for i in range(4):
                    for kt in kts:
                        bs = DEC if (t == 8 and kt == 1) else P
                        if t < 8:
                            vals = v2N[:, t - 1 + kt, g * C_DH:(g + 1) * C_DH]
                        else:
                            vals = (v2N[0:DEC, 8] if kt else vc2[:, :])[:, g * C_DH:(g + 1) * C_DH]
                        last = nc.tensor.matmul(PS[0:nq, 6 + v, i * C_DH:(i + 1) * C_DH], PT2[0:bs, v, kt, i, 0:nq], vals,
                                                start=kt == kts[0], stop=kt == 1)
                last.then_inc(S("o_pv"), 1)

            def odd_rows(t):
                nr = ROWS[t]
                pe.wait_ge(S("o_o"), 4 * t + 4)
                pe.wait_ge(S("o_tev"), OFILL[4 * t + 4])
                for j in range(2):
                    for i in range(4):
                        k = 4 * j + i
                        last = nc.tensor.transpose(PS[:, 4 + j, i * P:i * P + nr], oN2[0:nr, k * P:(k + 1) * P], ident[0:nr, 0:nr])
                    last.then_inc(S("om_tr"), 1)

            pe.wait_ge(S("oi_kds"), 1)
            pe.wait_ge(S("oi_vn"), 3)
            pe.wait_ge(S("vc_in"), 32)
            for q in range(NQ + 2):
                if q < NQ:
                    odd_scores(q)
                if q >= 5 and q % 4 == 1:
                    odd_rows((q - 5) // 4)
                if 1 <= q <= NQ:
                    odd_probs(q - 1)
                    odd_values(q - 1)

            pe.wait_ge(S("om_lo"), 2 * RT)
            out_projection(OUTP[1])
            ffn(FFN[1])

            norm_pe_stats(pe, 4)
            pe.wait_ge(S("fin_g"), KT)
            for t in range(RT):
                nr = ROWS[t]
                for j in range(2):
                    f = 2 * t + j
                    if f >= 6:
                        pe.wait_ge(S("y_dve") if j else S("y_act"), t - 2)
                    for i in range(4):
                        last = nc.tensor.transpose(PS[0:nr, f % 6, i * P:(i + 1) * P], H[:, 4 * j + i, rows_of(t)], ident[:, :])
                    last.then_inc(S("y_tr"), 1)


_INS = ["x_prompt", "x_sample", "cache_diff_k", "cache_diff_v", "state_pool", "cache_swa_k", "cache_swa_v",
        "state_ffn_conv", "norm_attn", "norm_ffn", "norm_final", "w_in_even", "w_out_even", "diff_lambda",
        "diff_subln", "pool_w", "pool_scale", "w_in_odd", "b_in_odd", "w_out_odd", "sinks", "w_up", "conv_w",
        "conv_b", "w_down"]
_OUTS = [("y_prompt", (1, SEQ, D)), ("y_sample", (1, DEC, D)),
         ("diff_k_prompt", (1, 1, SEQ, A_H, 2, A_DH)), ("diff_v_prompt", (1, 1, SEQ, A_H, 2 * A_DH)),
         ("pool_prompt", (1, 1, HIST, A_W)),
         ("swa_k_prompt", (1, 1, C_CACHE, C_KV, C_DH)), ("swa_v_prompt", (1, 1, C_CACHE, C_KV, C_DH)),
         ("ffn_conv_prompt", (2, 1, 2, 2 * FF)),
         ("diff_k_sample", (1, 1, DEC, A_H, 2, A_DH)), ("diff_v_sample", (1, 1, DEC, A_H, 2 * A_DH)),
         ("pool_sample", (1, 1, HIST, A_W)),
         ("swa_k_sample", (1, 1, C_CACHE, C_KV, C_DH)), ("swa_v_sample", (1, 1, C_CACHE, C_KV, C_DH)),
         ("ffn_conv_sample", (2, 1, 2, 2 * FF))]


def tables():
    inv = np.float32(10000.0) ** (-np.arange(0, A_DH, 2, dtype=np.float32) / np.float32(A_DH))
    pos = np.concatenate([np.arange(SEQ), PAST + np.arange(DEC)]).astype(np.float32)
    ang = inv[:, None] * pos[None, :]
    cos, sin = np.cos(ang).astype(np.float32), np.sin(ang).astype(np.float32)
    counts = [[1.0 / min(w, t + 1) for t in range(HIST)] for w in WINDOWS]
    return {"cos_t": cos, "sin_t": np.concatenate([-sin, sin]),
            "rcnt_t": np.array(counts, np.float32).reshape(-1)}


def kernel(**inputs):
    import concourse.bacc as bacc
    from concourse.bass_utils import run_bass_kernel_spmd

    nc = bacc.Bacc("TRN2", target_bir_lowering=False, num_devices=1, dynamic_dma_scratch_size=1024)
    arrays, io = {}, {}
    for name in _INS:
        arrays[f"in_{name}"] = np.ascontiguousarray(inputs[name])
    for name, table in tables().items():
        arrays[f"in_{name}"] = table
    for name, a in arrays.items():
        io[name[3:]] = nc.dram_tensor(name, a.shape, mybir.dt.from_np(a.dtype), kind="ExternalInput").ap()
    for name, shape in _OUTS:
        io[name] = nc.dram_tensor(f"out_{name}", shape, F32, kind="ExternalOutput").ap()
    build(nc, io)
    r = run_bass_kernel_spmd(nc, [arrays], core_ids=[0])
    return tuple(r.results[0][f"out_{name}"] for name, _ in _OUTS)
```

```python
import math
from contextlib import ExitStack

import numpy as np
import concourse.bass as bass
from concourse import mybir

F32 = mybir.dt.float32
F32R = mybir.dt.float32r
BF16 = mybir.dt.bfloat16
ALU = mybir.AluOpType
ACT = mybir.ActivationFunctionType
AX_X = mybir.AxisListType.X

P = 128
D = 1024
KT = D // P
SEQ, DEC = 1024, 64
R = SEQ + DEC
PAST = 256
A_H, A_DH = 4, 64
A_W = A_H * 2 * A_DH
WINDOWS = (2, 4, 8, 16)
HIST = 15
C_H, C_KV, C_DH, C_CACHE = 16, 2, 64, 128
FF = 2816
FT = FF // P
NB = FT // 2
EPS = 1e-5
LAM_INIT = 0.8 - 0.6 * math.exp(-0.3 * 0)
BIG = -1e30
RT = 9
ROWS = [P] * 8 + [DEC]
CHUNKS = [(0, 364), (364, 364), (728, 360)]
EXT = SEQ + DEC + 4
UEXT = HIST + SEQ + HIST + DEC
U_S = HIST + SEQ + HIST

P_TILES = 7
P_NA0, P_NA1, P_NF0, P_NF1, P_NFIN, P_BIN, P_PS, P_SUB, P_ROWS6 = 0, 8, 16, 24, 32, 40, 50, 54, 55


def build(nc, io):
    ctx = ExitStack()
    with ctx:

        base = (nc.sbuf_base + 31) // 32 * 32
        RA = base
        RSZ = 71936
        R0 = RA + KT * R * 4
        R1 = R0 + RSZ
        RW = R1 + RSZ
        RK = RW + 26624
        RM = RK + 5120

        def at(name, off, shape, dt=F32):
            return nc.alloc_sbuf_tensor_at(name, shape, dt, offset=off)

        H = at("resid", RA, [P, KT, R])
        cos_e = at("cos_e", RA, [P, R])
        sin_e = at("sin_e", RA + 4352, [P, R])
        z_e = at("z_e", RA + 2 * 4352, [P, R])
        zs_e = at("zs_e", RA + 3 * 4352, [P, R])
        vz_e = at("vz_e", RA + 4 * 4352, [P, R])
        sumB = at("sumB", RA + 5 * 4352, [P, UEXT])
        sumA = at("sumA", RA + 5 * 4352 + 4480, [P, UEXT])

        def region_x(tag, off):
            return at(f"xhi{tag}", off, [P, KT, R], F32R), at(f"xlo{tag}", off + KT * R * 4, [P, KT, R], F32R)

        xn0, xn1 = region_x("0", R0), region_x("1", R1)
        xnat = at("xnat", R1, [P, RT, D])
        junk = at("junk", R1 + 36864, [P, D])
        pnat = at("pnat", R1 + 36864 + 4096, [P, P_TILES, P])
        hnat = at("hnat", R1 + 36864 + 4096 + 3584, [HIST, A_W])
        qT = at("qT", R1, [P, A_H, R])
        kT = at("kT", R1 + 17408, [P, A_H, R])
        vN = at("vN", R1 + 34816, [P, RT, A_W])
        uT = at("uT", R1 + 53248, [P, 4, UEXT])
        E = at("E", R0, [P, 2, 2, 1024])
        comb = at("comb", R0 + 34816, [P, 2, 1024])
        AT = at("AT", R0 + 34816 + 8192, [P, 2, 1024])
        oN = at("oN", RW + 8192, [P, RT, A_H, P])
        kcn = at("kcn", RW, [P, 2, A_W])
        vcn = at("vcn", RW + 4096, [P, 2, A_W])
        kNat = at("kNat", RK, [P, RT, P])
        kAll = at("kAll", RK, [P, A_H, PAST + DEC])
        acc = at("acc", RK, [P, R])
        kc2n = at("kc2n", RK, [P, P])
        wraw = at("wraw", RW, [P, 2, KT, P])
        whi = at("whi", RW + 8192, [P, 2, KT, P], F32R)
        wlo = at("wlo", RW + 8192 + 8192, [P, 2, KT, P], F32R)
        whi_op = [at("whi_op0", R1 + 53248, [P, 2, KT, P], F32R), at("whi_op1", R0 + 48128, [P, 2, KT, P], F32R)]
        wlo_op = [at("wlo_op0", R1 + 61440, [P, 2, KT, P], F32R), at("wlo_op1", R0 + 56320, [P, 2, KT, P], F32R)]
        graw = at("graw", RW, [P, KT, 2 * P])
        vraw = at("vraw", RW + 8192, [P, KT, 2 * P])
        draw = at("draw", RW + 16384, [P, 2, D])

        class FfnBuffers:
            def __init__(self, tag, off):
                self.hhi = at(f"hhi{tag}", off, [P, 2, R], F32R)
                self.hlo = at(f"hlo{tag}", off + 8704, [P, 2, R], F32R)
                o = off + 17408
                self.uphi = at(f"uphi{tag}", o, [P, 2, KT, P], F32R)
                self.uplo = at(f"uplo{tag}", o + 8192, [P, 2, KT, P], F32R)
                o += 16384
                self.dhi = at(f"dhi{tag}", o, [P, 2, D], F32R)
                self.dlo = at(f"dlo{tag}", o + 8192, [P, 2, D], F32R)
                o += 16384
                self.ext = at(f"ext{tag}", o, [P, 2, EXT])
                o += 2 * EXT * 4
                self.c = at(f"c{tag}", o, [P, 2, EXT - 2])
        ffn_buf = [FfnBuffers("_f0", R0), FfnBuffers("_f1", R1)]
        q2T = at("q2T", R0, [P, KT, R])
        kd = at("kd", R0 + 34816, [P, C_KV, R])
        v2N = at("v2N", R0 + 43520, [P, RT, P])
        o = R0 + 48128
        cos_o, sin_o = at("cos_o", o, [P, R]), at("sin_o", o + 4352, [P, R])
        z_o, zs_o = at("z_o", o + 8704, [P, R]), at("zs_o", o + 13056, [P, R])
        vz_o = at("vz_o", o + 17408, [P, R])
        E2 = at("E2", RW + 8192, [P, 2, 4, 256])
        PT2 = at("PT2", RW + 16384, [P, 2, 2, 4, P])
        oN2 = at("oN2", o + 16384, [P, D])
        o += 21760
        kds = at("kds", o, [P, C_KV, C_CACHE + DEC])
        vc2 = at("vc2", o + 1536, [P, P])
        yN = at("yN", R0, [P, RT, D])

        o = RM
        def small(name, shape, dt=F32):
            nonlocal o
            size = int(np.prod(shape[1:])) * (2 if dt == BF16 else 4)
            t = at(name, o, shape, dt)
            o += (size + 31) // 32 * 32
            return t
        dg_off = o
        dg = small("dg", [P, RT, P])
        rB = at("rB", dg_off, [P, R])
        ident = small("ident", [P, P])
        ones = small("ones", [P, P])
        par = small("par", [P, P_TILES, 88])
        s_off = o
        pwraw = small("pwraw", [P, 4, P])
        pwhi = small("pwhi", [P, 4, P], F32R)
        pwlo = small("pwlo", [P, 4, P], F32R)
        sq = at("sq", s_off, [P, R])
        ojunk = at("ojunk", s_off + 4352, [P, P])
        kn2 = at("kn2", s_off + 4352, [P, 2, P])
        maskL = small("maskL", [P, P], BF16)
        maskR = small("maskR", [P, 2, 256], BF16)
        epsT = small("epsT", [P, 1])
        ss = small("ss", [P, RT])
        std = small("std", [P, RT])
        rs = small("rs", [P, RT])
        lamp = at("lamp", R1 + 48640, [P, 4, A_DH])
        lam2 = small("lam2", [P, 4])
        neglam = small("neglam", [P, 1])
        subg = small("subg", [P, 1])
        sinkb = small("sinkb", [P, C_H])
        e_off = o
        edge = at("edge", e_off, [P, 2, 2, 2 * FT])
        rct = small("rct", [P, 4, HIST])
        ue = small("ue", [P, 4, 2, HIST])
        fix = small("fix", [P, HIST])
        nm = small("nm", [P, 2, 2])
        sums = small("sums", [P, 2, 2])
        rsum = small("rsum", [P, 4, 2])
        cc = small("cc", [P, 2])
        sso = small("sso", [P, RT, A_H])
        rso = small("rso", [P, RT, A_H])
        m2 = small("m2", [P, 2, 4]); nm2 = small("nm2", [P, 2, 4]); snk2 = small("snk2", [P, 2, 4])
        es2 = small("es2", [P, 2, 4]); sum2 = small("sum2", [P, 2, 4]); den2 = small("den2", [P, 2, 4])
        rd2 = small("rd2", [P, 2, 4])
        uout = at("uout", s_off, [HIST, 2, A_W])
        edgeN = at("edgeN", s_off + 4352, [4 * FT, 2, P])
        assert o <= nc.sbuf_usable_end, (o, nc.sbuf_usable_end)

        PS = ctx.enter_context(nc.psum_tensor("PS", [P, 8, 512], F32))

        def pieces(s, t, off=0):
            a = CHUNKS[2][0]
            return [(PS[:, 3 * s:3 * s + 2, 0:364], t[:, off:off + a].rearrange("p (c n) -> p c n", c=2)),
                    (PS[:, 3 * s + 2, 0:360], t[:, off + a:off + R])]

        def rows_of(t):
            return slice(P * t, P * t + ROWS[t])

        def param(tile, row):
            return par[:, tile, row:row + 1]

        def products(s, k, nk, wh, wl, xh, xl):
            for n, (w, x) in enumerate(((wh, xh), (wh, xl), (wl, xh))):
                for c, (a, width) in enumerate(CHUNKS):
                    last = nc.tensor.matmul(PS[:, 3 * s + c, 0:width], w, x[:, a:a + width],
                                            start=(k == 0 and n == 0), stop=(k == nk - 1 and n == 2))
            return last

        made = {}

        def S(name):
            if name not in made:
                made[name] = ctx.enter_context(nc.semaphore(name))
            return made[name]

        LAYER_COUNT = {"in_raw0": 128, "in_raw1": 128, "in_hi": 16, "in_lo": 16, "in_mm": 16, "in_ev": 16,
                       "in_rope": 8, "in_rz": 8, "in_sw": 8, "op_raw0": 64, "op_raw1": 64, "op_hi": 8, "op_lo": 8, "op_mm": 8,
                       "ff_graw": 16 * NB, "ff_vraw": 16 * NB, "ff_draw": 16 * NB,
                       "ff_uphi": 4 * NB, "ff_uplo": 4 * NB, "ff_upmm": 4 * NB,
                       "ff_dhi": NB, "ff_dlo": NB, "ff_dnmm": KT * NB, "ff_dnev": KT * (NB - 1)}
        for name in ("gext", "vext", "gtap", "vtap", "gmid", "vmid", "gconv", "vconv", "silu", "h", "hhi", "hlo"):
            LAYER_COUNT["ff_" + name] = FT

        C_IDENT, C_SMALL, C_ALL = 2, 7, 17
        X_IN = [f"x_in{n}" for n in (0, 2, 2, 4, 4, 6, 6, 7, 8)]

        def reached(eng, l, name, count):
            eng.wait_ge(S(name), count + l * LAYER_COUNT[name])

        def norm_pe_stats(pe, n):
            pe.wait_ge(S("acc_done"), 7 * n)
            pe.wait_ge(S("fin_sq"), 8 * n)
            for t in range(RT):
                nr = ROWS[t]
                nc.tensor.matmul(PS[0:nr, 6, t:t + 1], acc[:, rows_of(t)], ones[:, 0:1], start=True, stop=False)
                last = nc.tensor.matmul(PS[0:nr, 6, t:t + 1], sq[:, rows_of(t)], ones[:, 0:1], start=False, stop=True)
            last.then_inc(S("n_stat"), 1)

        BC_BANK = (7, 6, 7)

        def norm_pe_bcast(pe, n, c):
            pe.wait_ge(S("n_diag"), n + 1)
            if n == 0:
                pe.wait_ge(S("par_ev"), 4)
            if c == 2:
                pe.wait_ge(S("n_rb"), 3 * n + 1)
            flat = dg[:, :, :].rearrange("p t c -> p (t c)")
            a, width = CHUNKS[c]
            nc.tensor.matmul(PS[:, BC_BANK[c], 0:width], ones[:, :], flat[:, a:a + width],
                             start=True, stop=True).then_inc(S("n_bc"), 1)

        def norm_bcast_after(pe, n):
            def after(k):
                if k == 3:
                    norm_pe_bcast(pe, n, 0)
                    norm_pe_bcast(pe, n, 1)
                if k == 5:
                    norm_pe_bcast(pe, n, 2)
            return after

        def norm_act(act, n, src):
            nc.scalar.activation(std[:, 0:8], src[:, 0:8], ACT.Sqrt, scale=1.0 / D, bias=epsT[:, 0:1])
            nc.scalar.activation(std[0:DEC, 8:9], src[0:DEC, 8:9], ACT.Sqrt, scale=1.0 / D,
                                 bias=epsT[0:DEC, 0:1]).then_inc(S("n_sqrt"), 1)

        def norm_dve_diag(dve, n):
            dve.wait_ge(S("n_sqrt"), n + 1)
            nc.vector.reciprocal(rs[:, :], std[:, :]).then_inc(S("n_rec"), 1)
            if n < 4:
                dve.wait_ge(S("n_rec"), n + 1)
                nc.vector.tensor_tensor(dg[:, :, :], ident[:, :].unsqueeze(1).to_broadcast([P, RT, P]),
                                        rs[:, :].unsqueeze(2).to_broadcast([P, RT, P]),
                                        ALU.mult).then_inc(S("n_diag"), 1)

        def norm_dve_rb(dve, n):
            for c, (a, width) in enumerate(CHUNKS):
                dve.wait_ge(S("n_bc"), 3 * n + c + 1)
                nc.vector.tensor_copy(rB[:, a:a + width], PS[:, BC_BANK[c], 0:width]).then_inc(S("n_rb"), 1)

        def scaled_by_row(s, dst, off=0):
            for (src, d), (_, r) in zip(pieces(s, dst, off), pieces(s, rB)):
                last = nc.vector.tensor_tensor(d, src, r, ALU.mult)
            return last

        PAIRS = [(t, h) for t in (7, 6, 5, 4, 8, 3, 2, 1, 0) for h in range(A_H)]
        SAMPLE_DONE = 20
        KEYS = [(t + 1) * P for t in range(8)] + [PAST + DEC]
        BLOCKS = [[(b * P, min(P, KEYS[t] - b * P)) for b in range((KEYS[t] + P - 1) // P)] for t in range(RT)]
        FILLS = [[(f, min(4, len(BLOCKS[t]) - f)) for f in range(0, len(BLOCKS[t]), 4)] for t in range(RT)]
        FIRST_FILL = [sum(len(FILLS[t]) for t, _ in PAIRS[:p]) for p in range(len(PAIRS) + 1)]
        NP_ = len(PAIRS)

        def two_banks(p):
            return KEYS[PAIRS[p][0]] > 512

        def score_banks(p, m):
            nq, L = ROWS[PAIRS[p][0]], KEYS[PAIRS[p][0]]
            if two_banks(p):
                return PS[0:nq, 2 * m:2 * m + 2, :].rearrange("p b n -> p (b n)")[:, 0:L]
            return PS[0:nq, 2 * m + p % 2, 0:L]

        BATCHES = [(t, b) for t in range(RT) for b in range(4)]
        WIN = [(P, 256)] + [(0, 256)] * 7 + [(0, C_CACHE + DEC)]
        NQ = len(BATCHES)

        def key_tiles(t):
            return [kt for kt in range(2) if WIN[t][0] < (kt + 1) * P]
        OFILL = [sum(len(key_tiles(t)) for t, _ in BATCHES[:q]) for q in range(NQ + 1)]

        OUTP = [dict(x=xn0, y=xn1, w=io["w_out_even"][0], gain=P_NF0, n=1, l=0, tag="op", ks=[4, 5, 6, 7, 0, 1, 2, 3]),
                dict(x=xn1, y=xn0, w=io["w_out_odd"][0], gain=P_NF1, n=3, l=1, tag="op", ks=list(range(8)))]
        FFN = [dict(x=xn1, y=xn1, gain=P_NA1, n=1, tag="ff", b=ffn_buf[0], l=0),
               dict(x=xn0, y=None, gain=P_NFIN, n=3, tag="ff", b=ffn_buf[1], l=1)]

        POOL_ORDER = (1, 2, 3, 0)

        def pool_hi(act, identity, n):
            g = POOL_ORDER[n]
            act.wait_ge(S("pm_mm"), n + 1)
            for src, dst in pieces(n % 2, xn0[0][:, 4 + g, :]):
                last = identity(dst, src, scale=param(6, P_PS + g))
            last.then_inc(S("pm_hi"), 1)

        def row_fill(f):
            j = f % 3
            return f // 6, f % 6 >= 3, 4 * j, 1 if j == 2 else 4

        def row_fills_after(u):
            g, kind = u // 4, u % 4
            if kind == 3:
                return (6 * g, 6 * g + 1)
            return (6 * g - 4 + 2 * kind, 6 * g - 3 + 2 * kind) if g >= 1 and kind < 2 else ()

        def ffn_sq(f, k):
            return sq[:, :] if k % 2 else f["b"].c[:, 0, 0:R]

        def finish_tile(act, identity, k, x, gain, sq_at):
            h = H[:, bass.ds(k, 1), :]
            if x:
                identity(x[0][:, bass.ds(k, 1), :], h, scale=par[:, 6, bass.ds(k + gain, 1)]).then_inc(S("fin_hi"), 1)
            nc.scalar.activation(sq_at.unsqueeze(1), h, ACT.Square).then_inc(S("fin_sq"), 1)

        def odd_rows_hi(act, f):
            t, j = f // 2, f % 2
            nr = ROWS[t]
            act.wait_ge(S("om_tr"), f + 1)
            nc.scalar.copy(xn1[0][:, 4 * j:4 * j + 4, P * t:P * t + nr],
                           PS[:, 7, :].rearrange("p (k r) -> p k r", k=4)[:, :, 0:nr]).then_inc(S("om_hi"), 1)

        STEPS = NQ + 4

        def rows_step(q):
            return (q - 4) // 2 if q >= 4 and q % 2 == 0 and (q - 4) // 2 < 2 * RT else None

        block = ctx.enter_context(nc.Block())


        @block.sync
        def _(sp):
            def x_tile(t):
                if t == 8:
                    sp.dma_start(xnat[0:DEC, t, :], io["x_sample"][0]).then_inc(S("x_in8"), 16)
                else:
                    t0 = max(t - 1, 0)
                    sp.dma_start(xnat[:, t0:t + 1, :], io["x_prompt"][0].rearrange("(t p) d -> p t d", p=P)[:, t0:t + 1, :]) \
                        .then_inc(S(f"x_in{t}"), 16)

            def par_rows(tile, row, src):
                n = src.shape[0]
                sp.dma_start(pnat[row:row + n, tile, :], src).then_inc(S("gain_in" if tile == 6 else "par_in"), 16)

            x_tile(0)
            x_tile(2)

            def even_in_weight(u):
                col = (u + 3) % 4 * A_W + (u // 4) * P
                if u >= 2:
                    reached(sp, 0, "in_lo", u - 1)
                sp.dma_start(wraw[:, u % 2], io["w_in_even"][0].rearrange("(k p) n -> p k n", p=P)[:, :, col:col + P]) \
                    .then_inc(S(f"in_raw{u % 2}"), 16)
            even_in_weight(0)
            par_rows(6, P_NA0, io["norm_attn"].rearrange("i (t c) -> (i t) c", c=P))
            par_rows(6, P_NF0, io["norm_ffn"].rearrange("i (t c) -> (i t) c", c=P))
            par_rows(6, P_NFIN, io["norm_final"].rearrange("(t c) -> t c", c=P))
            par_rows(6, P_BIN, io["b_in_odd"][0].rearrange("(t c) -> t c", c=P))
            par_rows(6, P_PS, io["pool_scale"][0].rearrange("(t c) -> t c", c=P))
            par_rows(6, P_SUB, io["diff_subln"])
            sp.dma_start(hnat[:, :], io["state_pool"][0, 0]).then_inc(S("gain_in"), 16)
            x_tile(4)
            x_tile(6)
            sp.dma_start(xnat[:, 7, :], io["x_prompt"][0, 7 * P:8 * P, :]).then_inc(S("x_in7"), 16)
            x_tile(8)
            even_in_weight(1)
            for l in range(2):
                par_rows(3 * l, 0, io["conv_w"][l, 0:2].rearrange("i (t c) -> (i t) c", c=P))
                par_rows(3 * l + 1, 0, io["conv_w"][l, 2:3].rearrange("i (t c) -> (i t) c", c=P))
                par_rows(3 * l + 1, 44, io["conv_b"][l:l + 1].rearrange("i (t c) -> (i t) c", c=P))
                par_rows(3 * l + 2, 0, io["state_ffn_conv"][l, 0].rearrange("i (t c) -> (i t) c", c=P))
            for c in range(4):
                sp.dma_start(cos_e[32 * c:32 * c + 32, :], io["cos_t"]).then_inc(S("tab_in"), 16)
            for c in range(2):
                sp.dma_start(sin_e[64 * c:64 * c + 64, :], io["sin_t"]).then_inc(S("tab_in"), 16)
            sp.dma_start(pwraw[:, :, :], io["pool_w"][0].rearrange("g c d -> c g d")).then_inc(S("pw_in"), 16)
            sp.dma_start(rct[:, :, :].rearrange("p g t -> p (g t)"), io["rcnt_t"].partition_broadcast(P)).then_inc(S("bc_in"), 16)
            sp.dma_start(lamp[:, :, :].rearrange("p a b -> p (a b)"),
                         io["diff_lambda"][0].rearrange("a b -> (a b)").partition_broadcast(P)).then_inc(S("bc_in"), 16)
            sp.dma_start(sinkb[:, :], io["sinks"][0].partition_broadcast(P)).then_inc(S("bc_in"), 16)
            for u in range(2, 16):
                even_in_weight(u)
            reached(sp, 0, "in_lo", 16)
            sp.dma_start(kcn[:, :, :], io["cache_diff_k"][0, 0].rearrange("(b p) h m d -> p b (h m d)", p=P)).then_inc(S("kc_in"), 16)
            sp.dma_start(vcn[:, :, :], io["cache_diff_v"][0, 0].rearrange("(b p) h e -> p b (h e)", p=P)).then_inc(S("vc_in"), 16)
            sp.wait_ge(S("ei_tev"), 24)
            sp.dma_start(io["diff_v_prompt"][0, 0].rearrange("(t p) h e -> p t (h e)", p=P), vN[:, 0:8, :]).then_inc(S("st_v"), 16)
            sp.dma_start(io["diff_v_sample"][0, 0].rearrange("s h e -> s (h e)"), vN[0:DEC, 8, :]).then_inc(S("st_v"), 16)
            sp.dma_start(io["swa_k_sample"][0, 0, 0:64], io["cache_swa_k"][0, 0, 64:128]).then_inc(S("st_y"), 16)
            sp.dma_start(io["swa_v_sample"][0, 0, 0:64], io["cache_swa_v"][0, 0, 64:128]).then_inc(S("st_y"), 16)

            def out_weights(o):
                t, l = o["tag"], o["l"]
                src = o["w"].rearrange("(k p) n -> p k n", p=P)
                for u in range(2):
                    if l == 0:
                        sp.wait_ge(S("kc_ev") if u == 0 else S("at_pv"), 3 if u == 0 else SAMPLE_DONE)
                    else:
                        reached(sp, 1, "in_lo", 9 + u)
                    sp.dma_start(wraw[:, u], src[:, :, u * P:(u + 1) * P]).then_inc(S(f"{t}_raw{u}"), 16)
                with sp.Fori(1, 4) as j:
                    for s in range(2):
                        col = sp.snap(j * 256 + s * P)
                        reached(sp, l, f"{t}_lo", 2 * j + s - 1)
                        sp.dma_start(wraw[:, s], src[:, :, bass.ds(col, P)]).then_inc(S(f"{t}_raw{s}"), 16)

            def ffn_weights(f):
                t, l, b = f["tag"], f["l"], f["b"]
                up = io["w_up"][l].rearrange("(k p) n -> p k n", p=P)
                down = io["w_down"][l].rearrange("(f p) n -> p f n", p=P)
                reached(sp, l, "op_lo", 8)
                sp.dma_start(graw[:, :, :], up[:, :, 0:256]).then_inc(S(f"{t}_graw"), 16)
                reached(sp, l, "op_mm", 8)
                sp.dma_start(vraw[:, :, :], up[:, :, FF:FF + 256]).then_inc(S(f"{t}_vraw"), 16)
                sp.dma_start(draw[:, :, :], down[:, 0:2, :]).then_inc(S(f"{t}_draw"), 16)
                with sp.Fori(1, NB) as i:
                    g_col = sp.snap(i * 256)
                    v_col = sp.snap(i * 256 + FF)
                    d_tile = sp.snap(i * 2)
                    reached(sp, l, f"{t}_uplo", 4 * i - 1)
                    sp.dma_start(graw[:, :, :], up[:, :, bass.ds(g_col, 256)]).then_inc(S(f"{t}_graw"), 16)
                    reached(sp, l, f"{t}_dlo", i)
                    sp.dma_start(draw[:, :, :], down[:, bass.ds(d_tile, 2), :]).then_inc(S(f"{t}_draw"), 16)
                    reached(sp, l, f"{t}_uplo", 4 * i)
                    sp.dma_start(vraw[:, :, :], up[:, :, bass.ds(v_col, 256)]).then_inc(S(f"{t}_vraw"), 16)

            out_weights(OUTP[0])
            ffn_weights(FFN[0])

            src = io["w_in_odd"][0].rearrange("(k p) n -> p k n", p=P)
            for u in range(2):
                sp.wait_ge(S("ff_uplo"), 4 * NB - 1)
                sp.dma_start(wraw[:, u], src[:, :, u * P:(u + 1) * P]).then_inc(S(f"in_raw{u}"), 16)
            sp.wait_ge(S("fin_h"), 16)
            sp.wait_ge(S("acc_done"), 14)
            for c in range(4):
                sp.dma_start(cos_o[32 * c:32 * c + 32, :], io["cos_t"]).then_inc(S("tab_in"), 16)
            for c in range(2):
                sp.dma_start(sin_o[64 * c:64 * c + 64, :], io["sin_t"]).then_inc(S("tab_in"), 16)
            sp.dma_start(vc2[:, :], io["cache_swa_v"][0, 0].rearrange("s g d -> s (g d)")).then_inc(S("vc_in"), 16)
            with sp.Fori(1, 5) as j:
                for s in range(2):
                    col = sp.snap(j * 256 + s * P)
                    reached(sp, 1, "in_lo", 2 * j + s - 1)
                    sp.dma_start(wraw[:, s], src[:, :, bass.ds(col, P)]).then_inc(S(f"in_raw{s}"), 16)
            sp.wait_ge(S("n_stat"), 2)
            sp.dma_start(kc2n[:, :], io["cache_swa_k"][0, 0].rearrange("s g d -> s (g d)")).then_inc(S("kc_in"), 16)
            sp.wait_ge(S("oi_kn"), 2)
            sp.dma_start(io["swa_k_prompt"][0, 0].rearrange("s g d -> s (g d)"), kn2[:, 0, :]).then_inc(S("st_k2"), 16)
            sp.dma_start(io["swa_k_sample"][0, 0, 64:128].rearrange("s g d -> s (g d)"), kn2[0:DEC, 1, :]).then_inc(S("st_k2"), 16)
            sp.wait_ge(S("oi_vn"), 3)
            sp.dma_start(io["swa_v_prompt"][0, 0].rearrange("s g d -> s (g d)"), v2N[:, 7, :]).then_inc(S("st_v2"), 16)
            sp.dma_start(io["swa_v_sample"][0, 0, 64:128].rearrange("s g d -> s (g d)"), v2N[0:DEC, 8, :]).then_inc(S("st_v2"), 16)

            out_weights(OUTP[1])
            ffn_weights(FFN[1])

            for t in range(RT):
                sp.wait_ge(S("y_act"), t + 1)
                sp.wait_ge(S("y_dve"), t + 1)
                dst = io["y_prompt"][0, t * P:(t + 1) * P, :] if t < 8 else io["y_sample"][0]
                sp.dma_start(dst, yN[0:ROWS[t], t, :]).then_inc(S("st_y"), 16)
            for name, n in (("st_v", 2), ("st_k2", 2), ("st_v2", 2), ("st_y", RT + 2),
                            ("st_k", 8), ("st_u", 2), ("st_e", 4)):
                sp.wait_ge(S(name), 16 * n)

        @block.gpsimd
        def _(pool):
            made_ = [0]

            def constant(ins):
                made_[0] += 1
                ins.then_inc(S("c_set"), 1)
                pool.wait_ge(S("c_set"), made_[0])

            constant(nc.gpsimd.memset(ident[:, :], 0.0))
            constant(nc.gpsimd.affine_select(out=ident[:, :], in_=ident[:, :], compare_op=ALU.not_equal, fill=1.0,
                                             base=0, pattern=[[-1, P]], channel_multiplier=1))
            for tile, value in ((ones[:, :], 1.0), (epsT[:, :], EPS), (std[:, :], 1.0), (sso[:, :, :], 0.0),
                                (uT[:, :, 0:HIST], 0.0), (maskL[:, :], 0.0), (maskR[:, :, :], 0.0)):
                constant(nc.gpsimd.memset(tile, value))
            for half in (0, 64):
                constant(nc.gpsimd.memset(maskL[half:half + 1, 0:64], 1.0))
                constant(nc.gpsimd.memset(maskL[half + 32:half + 33, 64:128], 1.0))
                constant(nc.gpsimd.memset(maskR[half:half + 1, :, 192:256], BIG))
                constant(nc.gpsimd.memset(maskR[half + 32:half + 33, :, 0:64], BIG))

            gain = par[:, 6, P_NA0:P_NA0 + KT].unsqueeze(2).to_broadcast([P, KT, P])

            def even_gain(u):
                reached(pool, 0, f"in_raw{u % 2}", 16 * (u // 2 + 1))
                if u == 0:
                    pool.wait_ge(S("par_ev"), 1)
                w = wraw[:, u % 2]
                nc.gpsimd.tensor_tensor(w, w, gain, ALU.mult).then_inc(S("ei_gam"), 1)
                pool.wait_ge(S("ei_gam"), u + 1)

            chain = [0]

            def step(ins):
                chain[0] += 1
                ins.then_inc(S("pl"), 1)
                pool.wait_ge(S("pl"), chain[0])

            def window_mean(g):
                pool.wait_ge(S("ei_ue"), g + 1)
                u, bufs = uT[:, g, :], [sumA, sumB]
                cur = u
                for l in range(g + 1):
                    sh, st, dst = 1 << l, (2 << l) - 1, bufs[l % 2]
                    step(nc.gpsimd.tensor_tensor(dst[:, st:UEXT], cur[:, st:UEXT], cur[:, st - sh:UEXT - sh], ALU.add))
                    cur = dst
                if g == 0:
                    pool.wait_ge(S("bc_in"), 48)
                step(nc.gpsimd.tensor_tensor(fix[:, :], cur[:, HIST:2 * HIST], rct[:, g, :], ALU.mult))
                step(nc.gpsimd.tensor_scalar(cur[:, HIST:UEXT], cur[:, HIST:UEXT], 1.0 / WINDOWS[g], None, ALU.mult))
                step(nc.gpsimd.tensor_copy(cur[:, HIST:2 * HIST], fix[:, :]))
                nc.gpsimd.tensor_tensor(u[:, HIST:UEXT], cur[:, HIST:UEXT], u[:, HIST:UEXT], ALU.subtract).then_inc(S("pooled"), 1)
                pool.wait_ge(S("pooled"), g + 1)

            even_gain(0)
            even_gain(1)
            for u in range(2, 16):
                even_gain(u)
                if u % 4 == 3:
                    window_mean(u // 4)
            pool.wait_ge(S("pooled"), 4)
            for n, k in enumerate((5, 6, 7, 0, 1)):
                if k == 0:
                    reached(pool, 0, "in_rope", 8)
                nc.gpsimd.tensor_tensor(H[:, k, :], xn0[0][:, k, :].bitcast(F32), xn0[1][:, k, :].bitcast(F32),
                                        ALU.add).then_inc(S("h_pool"), 1)
                pool.wait_ge(S("h_pool"), n + 1)
            def ffn_squares(f):
                pool.wait_ge(S("n_stat"), f["n"])
                nc.gpsimd.memset(acc[:, :], 0.0).then_inc(S("acc_zero"), 1)
                pool.wait_ge(S("acc_zero"), f["n"] + 1)
                for k in range(KT - 1):
                    c = 8 * f["n"] + k
                    pool.wait_ge(S("fin_sq"), c + 1)
                    if k:
                        pool.wait_ge(S("acc_done"), c - f["n"])
                    nc.gpsimd.tensor_tensor(acc[:, :], acc[:, :], ffn_sq(f, k), ALU.add).then_inc(S("acc_done"), 1)

            pool.wait_ge(S("at_pv"), NP_)
            nc.gpsimd.memset(acc[:, :], 0.0).then_inc(S("acc_zero"), 1)
            ffn_squares(FFN[0])
            pool.wait_ge(S("n_stat"), 2)
            pool.wait_ge(S("kc2_tr"), 1)
            nc.gpsimd.memset(acc[:, :], 0.0).then_inc(S("acc_zero"), 1)
            ffn_squares(FFN[1])

        @block.scalar
        def _(act):
            def identity(dst, src, scale=1.0, bias=0.0):
                return nc.scalar.activation(dst, src, ACT.Identity, scale=scale, bias=bias)

            act.wait_ge(S("c_set"), C_SMALL)

            def even_hi(u):
                act.wait_ge(S("ei_gam"), u + 1)
                if u >= 2:
                    reached(act, 0, "in_mm", u - 1)
                nc.scalar.copy(whi[:, u % 2], wraw[:, u % 2]).then_inc(S("in_hi"), 1)

            def gains_out():
                act.wait_ge(S("par_tr"), 1)
                nc.scalar.copy(par[:, 6, 0:P_ROWS6], PS[:, 7, 176:176 + P_ROWS6]).then_inc(S("par_ev"), 1)
                nc.scalar.copy(uT[:, :, HIST + SEQ:U_S], PS[:, 7, 240:300].rearrange("p (g r) -> p g r", r=HIST)) \
                    .then_inc(S("par_ev"), 1)

            def params_out():
                act.wait_ge(S("par_tr"), 2)
                nc.scalar.copy(par[:, 0:4, :], PS[:, 6, 0:352].rearrange("p (a b) -> p a b", b=88)).then_inc(S("par_ev"), 1)
                act.wait_ge(S("par_tr"), 3)
                nc.scalar.copy(par[:, 4:6, :], PS[:, 7, 0:176].rearrange("p (a b) -> p a b", b=88)).then_inc(S("par_ev"), 1)

            for t in range(RT):
                nr = ROWS[t]
                for j in range(2):
                    f = 2 * t + j
                    act.wait_ge(S("x_tr"), f + 1)
                    nc.scalar.copy(xn0[0][:, 4 * j:4 * j + 4, P * t:P * t + nr],
                                   PS[:, 3 + f % 3, :].rearrange("p (k r) -> p k r", k=4)[:, :, 0:nr]).then_inc(S("x_hi"), 1)
                if t >= 1:
                    act.wait_ge(S("x_sq"), t)
                nc.scalar.activation(junk[0:nr, :], xnat[0:nr, t, :], ACT.Square,
                                     accum_out=ss[0:nr, t:t + 1]).then_inc(S("x_sq"), 1)
                if t == 2:
                    gains_out()
                    even_hi(0)
            even_hi(1)
            act.wait_ge(S("x_sq"), RT)
            norm_act(act, 0, ss[:, :])
            params_out()
            act.wait_ge(S("pw_in"), 16)
            nc.scalar.copy(pwhi[:, :, :], pwraw[:, :, :]).then_inc(S("pw_hi"), 1)

            def natural(f):
                g, is_v, a, n = row_fill(f)
                nr = ROWS[a]
                dst = vN[:, :, g * P:(g + 1) * P] if is_v else kNat
                if not is_v and a == 0 and g >= 1:
                    act.wait_ge(S("st_k"), 32 * g)
                act.wait_ge(S("ei_tr"), f + 1)
                nc.scalar.copy(dst[0:nr, a:a + n, :],
                               PS[0:nr, 6 + f % 2, 0:n * P].rearrange("p (t c) -> p t c", c=P)).then_inc(S("ei_tev"), 1)
                if not is_v and a == 8:
                    act.wait_ge(S("ei_tev"), f + 1)
                    act.dma_start(io["diff_k_prompt"][0, 0].rearrange("(t p) h m d -> p t h (m d)", p=P)[:, :, g, :],
                                  kNat[:, 0:8, :]).then_inc(S("st_k"), 16)
                    act.dma_start(io["diff_k_sample"][0, 0].rearrange("s h m d -> s h (m d)")[:, g, :],
                                  kNat[0:DEC, 8, :]).then_inc(S("st_k"), 16)

            ropes = 0
            for u in range(16):
                g, kind = u // 4, u % 4
                if u + 2 < 16:
                    even_hi(u + 2)
                reached(act, 0, "in_ev", u + 1)
                if kind in (1, 2):
                    if ropes:
                        reached(act, 0, "in_rope", ropes)
                    for c in range(4):
                        last = nc.scalar.copy(zs_e[32 * c:32 * c + 32, :], z_e[32 * (c ^ 1):32 * (c ^ 1) + 32, :])
                    last.then_inc(S("in_sw"), 1)
                    ropes += 1
                if kind == 0:
                    nc.scalar.copy(ue[:, g, 0, :], uT[:, g, SEQ:SEQ + HIST])
                    nc.scalar.copy(ue[:, g, 1, :], uT[:, g, UEXT - HIST:UEXT]).then_inc(S("ei_ue"), 1)
                for f in row_fills_after(u):
                    natural(f)

            def pooled_hi(n):
                g = POOL_ORDER[n]
                phi = xn0[0][:, 4 + g, :]
                if n == 0:
                    reached(act, 0, "in_mm", 16)
                    act.wait_ge(S("h_pool"), 5)
                    act.wait_ge(S("pooled"), 4)
                if g == 0:
                    act.wait_ge(S("h_dve"), 1)
                nc.scalar.copy(phi[:, 0:SEQ], uT[:, g, HIST:HIST + SEQ])
                nc.scalar.copy(phi[:, SEQ:R], uT[:, g, U_S:UEXT]).then_inc(S("pm_phi"), 1)

            pooled_hi(0)
            for f in range(20, 24):
                natural(f)
            pooled_hi(1)
            pooled_hi(2)
            pool_hi(act, identity, 0)
            pooled_hi(3)
            for n in range(1, 4):
                pool_hi(act, identity, n)
            act.wait_ge(S("lam"), 2)
            nc.scalar.activation(lam2[:, 2:4], lam2[:, 0:2], ACT.Exp).then_inc(S("lam_exp"), 1)
            act.wait_ge(S("ue_tr"), 1)
            for st in range(2):
                last = nc.scalar.copy(uout[:, st, :], PS[0:HIST, 6 + st, :])
            last.then_inc(S("ue_ev"), 1)
            act.wait_ge(S("ue_ev"), 1)
            act.dma_start(io["pool_prompt"][0, 0], uout[:, 0, :]).then_inc(S("st_u"), 16)
            act.dma_start(io["pool_sample"][0, 0], uout[:, 1, :]).then_inc(S("st_u"), 16)
            act.wait_ge(S("st_k"), 128)
            for b in range(2):
                act.wait_ge(S("kc_tr"), b + 1)
                nc.scalar.copy(kAll[:, :, b * P:(b + 1) * P],
                               PS[:, 4 + b, :].rearrange("p (h r) -> p h r", h=4)).then_inc(S("kc_ev"), 1)
            nc.scalar.copy(kAll[:, :, PAST:PAST + DEC], kT[:, :, SEQ:R]).then_inc(S("kc_ev"), 1)

            def op_first_hi(l, s):
                reached(act, l, f"op_raw{s}", 16)
                nc.scalar.copy(whi_op[l][:, s], wraw[:, s]).then_inc(S("op_hi"), 1)

            def exps(p):
                t, h = PAIRS[p]
                nq, L = ROWS[t], KEYS[t]
                if p >= 2:
                    act.wait_ge(S("at_comb"), p - 1)
                for m in range(2):
                    act.wait_ge(S(f"at_max{m}"), p + 1)
                    nc.scalar.activation(E[0:nq, p % 2, m, 0:L],
                                         score_banks(p, m),
                                         ACT.Exp, bias=nm[0:nq, p % 2, m:m + 1],
                                         accum_out=sums[0:nq, p % 2, m:m + 1]).then_inc(S(f"at_exp{m}"), 1)

            def probs_out(p):
                t, h = PAIRS[p]
                nq = ROWS[t]
                if p >= 2:
                    act.wait_ge(S("at_pv"), p - 1)
                for j, (f, n) in enumerate(FILLS[t]):
                    F = FIRST_FILL[p] + j
                    act.wait_ge(S("at_tr"), F + 1)
                    src = PS[:, 4 + F % 2, :].rearrange("p (b q) -> p b q", q=P)
                    dst = AT[:, p % 2, :].rearrange("p (b q) -> p b q", q=P)
                    if t < 8:
                        last = nc.scalar.copy(dst[:, f:f + n, :], src[:, 0:n, :])
                    else:
                        nc.scalar.copy(dst[:, 0:2, 0:nq], src[:, 0:2, 0:nq])
                        last = nc.scalar.copy(dst[0:DEC, 2, 0:nq], src[0:DEC, 2, 0:nq])
                    last.then_inc(S("at_tev"), 1)

            def head_out(p):
                t, h = PAIRS[p]
                nq = ROWS[t]
                act.wait_ge(S("at_pv"), p + 1)
                identity(oN[0:nq, t, h, :], PS[0:nq, 6 + p % 2, 0:P], scale=rsum[0:nq, p % 4, 0:1]).then_inc(S("at_o"), 1)
                act.wait_ge(S("at_o"), p + 1)
                if p >= 1:
                    act.wait_ge(S("at_ss"), p)
                nc.scalar.activation(ojunk[0:nq, :], oN[0:nq, t, h, :], ACT.Square,
                                     accum_out=sso[0:nq, t, h:h + 1]).then_inc(S("at_ss"), 1)

            for p in range(NP_ + 3):
                if p < NP_:
                    exps(p)
                if 1 <= p <= NP_:
                    probs_out(p - 1)
                if p >= 3:
                    head_out(p - 3)
                if p in (SAMPLE_DONE + 8, SAMPLE_DONE + 10):
                    op_first_hi(0, p // (SAMPLE_DONE + 10))
            act.wait_ge(S("at_ss"), NP_)
            nc.scalar.activation(rso[:, :, :], sso[:, :, :], ACT.Sqrt, scale=1.0 / P,
                                 bias=epsT[:, 0:1]).then_inc(S("so_sqrt"), 1)
            for t in range(RT):
                nr = ROWS[t]
                act.wait_ge(S("so_tr"), t + 1)
                identity(xn0[0][:, 0:4, P * t:P * t + nr],
                         PS[:, 4 + t % 2, :].rearrange("p (h r) -> p h r", h=4)[:, :, 0:nr],
                         scale=subg[:, 0:1]).then_inc(S("so_hi"), 1)

            def out_projection(o):
                t, l, x = o["tag"], o["l"], o["y"]

                def w_hi(u, s):
                    reached(act, l, f"{t}_raw{s}", (u - s) * 8 + 16)
                    nc.scalar.copy(whi[:, s], wraw[:, s]).then_inc(S(f"{t}_hi"), 1)

                def step(k, s, more):
                    c = 8 * (o["n"] - 1) + k
                    if more:
                        if not isinstance(k, int):
                            reached(act, l, f"{t}_mm", k + 1)
                        w_hi(k + 2, s)
                    act.wait_ge(S("fin_h"), c + 1)
                    if not isinstance(k, int) or k > 0:
                        act.wait_ge(S("acc_done"), c - (o["n"] - 1))
                    elif o["n"] > 1:
                        act.wait_ge(S("n_stat"), o["n"] - 1)
                    finish_tile(act, identity, k, x, o["gain"], sq[:, :])

                if l == 0:
                    act.wait_ge(S("so_tr"), RT)
                    act.wait_ge(S("st_v"), 32)
                    act.wait_ge(S("st_u"), 32)
                else:
                    act.wait_ge(S("st_v2"), 32)
                for s in range(2):
                    step(s, s, True)
                with act.Fori(1, 3) as j:
                    for s in range(2):
                        step(2 * j + s, s, True)
                step(6, 0, False)
                ffn_first_hi(FFN[l])
                step(7, 1, False)

            def odd_hi(u, s):
                reached(act, 1, f"in_raw{s}", (u - s) * 8 + 16)
                if isinstance(u, int) and u < 2:
                    act.wait_ge(S("ff_uplo"), 4 * NB)
                    act.wait_ge(S("ff_dlo"), NB)
                if not isinstance(u, int) or u >= 2:
                    reached(act, 1, "in_mm", u - 1)
                nc.scalar.copy(whi[:, s], wraw[:, s]).then_inc(S("in_hi"), 1)

            def ffn_first_hi(f):
                t, b, l = f["tag"], f["b"], f["l"]
                reached(act, l, f"{t}_graw", 16)
                reached(act, l, "op_mm", 8)
                nc.scalar.copy(b.uphi[:, 0], graw[:, :, 0:P]).then_inc(S(f"{t}_uphi"), 1)

            def ffn(f):
                t, b, l = f["tag"], f["b"], f["l"]

                def w_hi(s, half, raw, count, freed):
                    reached(act, l, f"{t}_{'gv'[s]}raw", count)
                    if freed is not None:
                        reached(act, l, f"{t}_upmm", freed)
                    nc.scalar.copy(b.uphi[:, s], raw[:, :, half * P:(half + 1) * P]).then_inc(S(f"{t}_uphi"), 1)

                def tap(s, T):
                    k = "gv"[s]
                    col = T + FT * s
                    reached(act, l, f"{t}_{k}ext", T + 1)
                    nc.scalar.copy(edge[:, :, :, bass.ds(col, 1)],
                                   b.ext[:, s, 960:EXT].rearrange("p (a c) -> p a c", c=66)[:, :, 64:66].unsqueeze(3))
                    identity(b.c[:, s, :], b.ext[:, s, 0:EXT - 2], scale=par[:, 3 * l, bass.ds(col, 1)],
                             bias=par[:, 3 * l + 1, bass.ds(col + 44, 1)]).then_inc(S(f"{t}_{k}tap"), 1)

                def silu(T):
                    reached(act, l, f"{t}_gconv", T + 1)
                    nc.scalar.activation(b.c[:, 0, :], b.c[:, 0, :], ACT.Silu).then_inc(S(f"{t}_silu"), 1)

                def h_hi(T, s):
                    reached(act, l, f"{t}_h", T + 1)
                    nc.scalar.copy(b.hhi[:, s, :], b.ext[:, 1, 4:EXT]).then_inc(S(f"{t}_hhi"), 1)

                def d_hi(i, first):
                    reached(act, l, f"{t}_draw", 16 * i + 16)
                    if not first:
                        reached(act, l, f"{t}_dnmm", 8 * i)
                    nc.scalar.copy(b.dhi[:, :, :], draw[:, :, :]).then_inc(S(f"{t}_dhi"), 1)

                def block_(i, first, last):
                    if not first:
                        tap(1, 2 * i - 1)
                        h_hi(2 * i - 1, 1)
                        w_hi(1, 0, vraw, 16 * i + 16, 4 * i)
                    tap(0, 2 * i)
                    silu(2 * i)
                    if not first:
                        w_hi(0, 1, graw, 16 * i + 16, 4 * i + 1)
                        d_hi(i, False)
                    tap(1, 2 * i)
                    w_hi(1, 1, vraw, 16 * i + 16, 4 * i + 2)
                    if first:
                        d_hi(i, True)
                    h_hi(2 * i, 0)
                    tap(0, 2 * i + 1)
                    silu(2 * i + 1)
                    if not last:
                        w_hi(0, 0, graw, 16 * i + 32, 4 * i + 3)

                w_hi(1, 0, vraw, 16, None)
                act.wait_ge(S("n_stat"), f["n"])
                norm_act(act, f["n"], PS[:, 6, 0:RT])
                w_hi(0, 1, graw, 16, 1)
                block_(0, True, False)
                with act.Fori(1, NB - 1) as i:
                    block_(i, False, False)
                block_(NB - 1, False, True)
                tap(1, 2 * NB - 1)
                h_hi(2 * NB - 1, 1)
                if l == 0:
                    for s in range(2):
                        odd_hi(s, s)
                for k in range(KT):
                    c = 8 * f["n"] + k
                    act.wait_ge(S("fin_h"), c + 1)
                    if k >= 2:
                        act.wait_ge(S("acc_done"), c - f["n"] - 1)
                    if k == 0 and f["y"]:
                        reached(act, l, f"{t}_upmm", 4 * NB)
                    finish_tile(act, identity, k, f["y"], f["gain"], ffn_sq(f, k))
                act.wait_ge(S("ed_tr"), l + 1)
                if l == 1:
                    act.wait_ge(S("st_k2"), 32)
                nc.scalar.copy(edgeN[:, :, :], PS[0:2 * 2 * FT, 7, 0:256].rearrange("p (a c) -> p a c", a=2)).then_inc(S("ed_ev"), 1)
                act.wait_ge(S("ed_ev"), l + 1)
                for a, name in enumerate(("ffn_conv_prompt", "ffn_conv_sample")):
                    act.dma_start(io[name][l, 0].rearrange("i (t c) -> (i t) c", c=P), edgeN[:, a, :]).then_inc(S("st_e"), 16)

            out_projection(OUTP[0])
            ffn(FFN[0])

            def swap_bias(u):
                reached(act, 1, "in_ev", u + 1)
                if not isinstance(u, int) or u >= 1:
                    reached(act, 1, "in_rope", u)
                for c in range(4):
                    a = 32 * (c ^ 1)
                    last = identity(zs_o[32 * c:32 * c + 32, :], z_o[a:a + 32, :], bias=par[a:a + 32, 6, bass.ds(u + P_BIN, 1)])
                last.then_inc(S("in_sw"), 1)

            act.wait_ge(S("n_stat"), 2)
            norm_act(act, 2, PS[:, 6, 0:RT])
            for s in range(2):
                odd_hi(s + 2, s)
                swap_bias(s)
            with act.Fori(1, 4) as j:
                for s in range(2):
                    odd_hi(2 * j + s + 2, s)
                    swap_bias(2 * j + s)
            swap_bias(8)
            reached(act, 1, "in_rope", 9)
            for g in range(C_KV):
                for half in (0, 64):
                    last = nc.scalar.copy(kd[half:half + 64, g, :], z_o[64 * g:64 * g + 64, :])
            last.then_inc(S("oi_kd"), 1)
            act.wait_ge(S("oi_ktr"), 1)
            act.wait_ge(S("st_e"), 32)
            nc.scalar.copy(kn2[:, 0, :], PS[:, 6, 0:P]).then_inc(S("oi_kn"), 1)
            nc.scalar.copy(kn2[0:DEC, 1, :], PS[0:DEC, 6, P:2 * P]).then_inc(S("oi_kn"), 1)
            act.wait_ge(S("kc2_tr"), 1)
            for g in range(C_KV):
                for half in (0, 64):
                    nc.scalar.copy(kds[half:half + 64, g, 0:P], PS[64 * g:64 * g + 64, 7, 0:P])
            act.wait_ge(S("oi_kd"), 1)
            nc.scalar.copy(kds[:, :, P:P + DEC], kd[:, :, SEQ:R]).then_inc(S("oi_kds"), 1)
            for j, (a, n, nr) in enumerate(((0, 4, P), (4, 4, P), (8, 1, DEC))):
                act.wait_ge(S("oi_vtr"), j + 1)
                nc.scalar.copy(v2N[0:nr, a:a + n, :], PS[0:nr, 3 + j, 0:n * P].rearrange("p (t c) -> p t c", c=P)) \
                    .then_inc(S("oi_vn"), 1)

            def odd_exps(q):
                t, b = BATCHES[q]
                nq, (c0, c1), v = ROWS[t], WIN[t], q % 2
                act.wait_ge(S("o_nm"), q + 1)
                if q >= 2:
                    act.wait_ge(S("o_tr"), OFILL[q - 1])
                for i in range(4):
                    last = nc.scalar.activation(E2[0:nq, v, i, c0:c1],
                                                PS[0:nq, 2 * v + i // 2, (i % 2) * 256 + c0:(i % 2) * 256 + c1],
                                                ACT.Exp, bias=nm2[0:nq, v, i:i + 1], scale=C_DH ** -0.5,
                                                accum_out=sum2[0:nq, v, i:i + 1])
                last.then_inc(S("o_exp"), 1)
                nc.scalar.activation(es2[0:nq, v, :], snk2[0:nq, v, :], ACT.Exp).then_inc(S("o_es"), 1)

            def odd_probs_first(q):
                t, b = BATCHES[q]
                nq, v = ROWS[t], q % 2
                if key_tiles(t)[0] == 0:
                    if q >= 2:
                        act.wait_ge(S("o_pv"), q - 1)
                    act.wait_ge(S("o_tr"), OFILL[q] + 1)
                    nc.scalar.copy(PT2[:, v, 0, :, 0:nq],
                                   PS[:, 4, :].rearrange("p (i q) -> p i q", i=4)[:, :, 0:nq]).then_inc(S("o_tev0"), 1)

            for q in range(STEPS):
                if rows_step(q) is not None:
                    odd_rows_hi(act, rows_step(q))
                if 1 <= q <= NQ:
                    odd_probs_first(q - 1)
                if q < NQ:
                    odd_exps(q)
                if q in (NQ - 4, NQ - 2):
                    op_first_hi(1, q // (NQ - 2))

            out_projection(OUTP[1])
            ffn(FFN[1])

            act.wait_ge(S("n_stat"), 4)
            norm_act(act, 4, PS[:, 6, 0:RT])
            act.wait_ge(S("n_rec"), 5)
            for t in range(RT):
                act.wait_ge(S("y_tr"), 2 * t + 1)
                identity(yN[0:ROWS[t], t, 0:512], PS[0:ROWS[t], 2 * t % 6, :], scale=rs[0:ROWS[t], t:t + 1]).then_inc(S("y_act"), 1)

        @block.vector
        def _(dve):
            tt = nc.vector.tensor_tensor

            def split_lo(dst, src, hi, scale=None):
                if scale is None:
                    return tt(dst, src, hi.bitcast(F32), ALU.subtract)
                return nc.vector.scalar_tensor_tensor(out=dst, in0=src, scalar=scale, in1=hi.bitcast(F32),
                                                      op0=ALU.mult, op1=ALU.subtract)

            def even_lo(u):
                reached(dve, 0, "in_hi", u + 1)
                split_lo(wlo[:, u % 2], wraw[:, u % 2], whi[:, u % 2]).then_inc(S("in_lo"), 1)

            for f in range(2 * RT):
                t, j = f // 2, f % 2
                nr = ROWS[t]
                dve.wait_ge(S("x_hi"), f + 1)
                cols = slice(P * t, P * t + nr)
                split_lo(xn0[1][:, 4 * j:4 * j + 4, cols], PS[:, 3 + f % 3, :].rearrange("p (k r) -> p k r", k=4)[:, :, 0:nr],
                         xn0[0][:, 4 * j:4 * j + 4, cols]).then_inc(S("x_lo"), 1)
                if f == 5:
                    even_lo(0)
            even_lo(1)
            dve.wait_ge(S("c_set"), C_IDENT)
            norm_dve_diag(dve, 0)
            dve.wait_ge(S("pw_hi"), 1)
            split_lo(pwlo[:, :, :], pwraw[:, :, :], pwhi[:, :, :]).then_inc(S("pw_lo"), 1)
            dve.wait_ge(S("bc_in"), 48)
            tt(lamp[:, 0:4:2, :], lamp[:, 0:4:2, :], lamp[:, 1:4:2, :], ALU.mult).then_inc(S("lam"), 1)
            dve.wait_ge(S("lam"), 1)
            nc.vector.tensor_reduce(lam2[:, 0:2], lamp[:, 0:4:2, :], AX_X, ALU.add).then_inc(S("lam"), 1)
            nc.vector.tensor_scalar(subg[:, :], param(6, P_SUB), 1.0 - LAM_INIT, None, ALU.mult).then_inc(S("lam"), 1)
            norm_dve_rb(dve, 0)

            def residual_again(ks):
                for k in ks:
                    last = tt(H[:, k, :], xn0[0][:, k, :].bitcast(F32), xn0[1][:, k, :].bitcast(F32), ALU.add)
                return last

            dve.wait_ge(S("n_rb"), 3)
            ropes = 0
            for u in range(16):
                g, kind, s = u // 4, u % 4, u % 2
                reached(dve, 0, "in_mm", u + 1)
                if kind in (1, 2):
                    if ropes:
                        reached(dve, 0, "in_rope", ropes)
                    last = scaled_by_row(s, z_e)
                elif kind == 3:
                    if g >= 1:
                        dve.wait_ge(S("ei_tr"), 6 * g)
                    last = scaled_by_row(s, vz_e)
                else:
                    tt(uT[:, g, HIST:HIST + 728].rearrange("p (c n) -> p c n", c=2), PS[:, 3 * s:3 * s + 2, 0:364],
                       rB[:, 0:728].rearrange("p (c n) -> p c n", c=2), ALU.mult)
                    tt(uT[:, g, HIST + 728:HIST + SEQ], PS[:, 3 * s + 2, 0:SEQ - 728], rB[:, 728:SEQ], ALU.mult)
                    last = tt(uT[:, g, U_S:UEXT], PS[:, 3 * s + 2, SEQ - 728:360], rB[:, SEQ:R], ALU.mult)
                last.then_inc(S("in_ev"), 1)
                if u + 2 < 16:
                    even_lo(u + 2)
                if kind in (1, 2):
                    if ropes == 0:
                        dve.wait_ge(S("tab_in"), 96)
                    ropes += 1
                    by = A_DH ** -0.5 if kind == 1 else 1.0
                    reached(dve, 0, "in_sw", ropes)
                    nc.vector.scalar_tensor_tensor(out=z_e[:, :], in0=z_e[:, :], scalar=by, in1=cos_e[:, :],
                                                   op0=ALU.mult, op1=ALU.mult)
                    nc.vector.scalar_tensor_tensor(out=zs_e[:, :], in0=zs_e[:, :], scalar=by, in1=sin_e[:, :],
                                                   op0=ALU.mult, op1=ALU.mult).then_inc(S("in_rz"), 1)
                    reached(dve, 0, "in_rz", ropes)
                    tt((qT if kind == 1 else kT)[:, g, :], z_e[:, :], zs_e[:, :], ALU.add).then_inc(S("in_rope"), 1)
                if u == 14:
                    reached(dve, 0, "in_rope", 8)
                    residual_again((2, 3))
            def pool_lo(n):
                g = POOL_ORDER[n]
                dve.wait_ge(S("pm_hi"), n + 1)
                for (src, dst), (_, hi) in zip(pieces(n % 2, xn0[1][:, 4 + g, :]), pieces(n % 2, xn0[0][:, 4 + g, :])):
                    last = split_lo(dst, src, hi, param(6, P_PS + g))
                last.then_inc(S("pm_ev"), 1)

            def pooled_lo(n):
                g = POOL_ORDER[n]
                dve.wait_ge(S("pm_phi"), n + 1)
                hi, lo = xn0[0][:, 4 + g, :], xn0[1][:, 4 + g, :]
                split_lo(lo[:, 0:SEQ], uT[:, g, HIST:HIST + SEQ], hi[:, 0:SEQ])
                split_lo(lo[:, SEQ:R], uT[:, g, U_S:UEXT], hi[:, SEQ:R]).then_inc(S("pm_plo"), 1)

            pooled_lo(0)
            dve.wait_ge(S("ei_tr"), 24)
            residual_again([4]).then_inc(S("h_dve"), 1)
            pooled_lo(1)
            pooled_lo(2)
            pool_lo(0)
            pooled_lo(3)
            for n in range(1, 4):
                pool_lo(n)
            dve.wait_ge(S("lam_exp"), 1)
            nc.vector.scalar_tensor_tensor(out=neglam[:, :], in0=lam2[:, 3:4], scalar=-LAM_INIT, in1=lam2[:, 2:3],
                                           op0=ALU.add, op1=ALU.subtract).then_inc(S("lam"), 1)

            def op_first_lo(l, s):
                reached(dve, l, "op_hi", s + 1)
                split_lo(wlo_op[l][:, s], wraw[:, s], whi_op[l][:, s]).then_inc(S("op_lo"), 1)

            def maxes(p, ms):
                t, h = PAIRS[p]
                nq = ROWS[t]
                for m in ms:
                    dve.wait_ge(S(f"at_s{m}"), p + 1)
                    nc.vector.tensor_reduce(nm[0:nq, p % 2, m:m + 1],
                                            score_banks(p, m),
                                            AX_X, ALU.max, negate=True).then_inc(S(f"at_max{m}"), 1)

            def combine(p):
                t, h = PAIRS[p]
                nq, L = ROWS[t], KEYS[t]
                for m in range(2):
                    dve.wait_ge(S(f"at_exp{m}"), p + 1)
                if p >= 4:
                    dve.wait_ge(S("at_o"), p - 3)
                nc.vector.reciprocal(rsum[0:nq, p % 4, :], sums[0:nq, p % 2, :]).then_inc(S("at_r"), 1)
                dve.wait_ge(S("at_r"), 2 * p + 1)
                nc.vector.tensor_scalar(cc[0:nq, p % 2:p % 2 + 1], sums[0:nq, p % 2, 0:1], rsum[0:nq, p % 4, 1:2],
                                        neglam[0:nq, :], ALU.mult, ALU.mult).then_inc(S("at_r"), 1)
                dve.wait_ge(S("at_r"), 2 * p + 2)
                if p >= 2:
                    dve.wait_ge(S("at_tr"), FIRST_FILL[p - 1])
                nc.vector.scalar_tensor_tensor(out=comb[0:nq, p % 2, 0:L], in0=E[0:nq, p % 2, 1, 0:L],
                                               scalar=cc[0:nq, p % 2:p % 2 + 1], in1=E[0:nq, p % 2, 0, 0:L],
                                               op0=ALU.mult, op1=ALU.add).then_inc(S("at_comb"), 1)

            dve.wait_ge(S("lam"), 4)
            for p in range(NP_ + 1):
                if p < NP_:
                    maxes(p, [0])
                if p >= 1:
                    combine(p - 1)
                if p < NP_:
                    maxes(p, [1])
                if p in (SAMPLE_DONE + 9, SAMPLE_DONE + 11):
                    op_first_lo(0, p // (SAMPLE_DONE + 11))
            dve.wait_ge(S("so_sqrt"), 1)
            nc.vector.reciprocal(rso[:, :, :], rso[:, :, :]).then_inc(S("so_rec"), 1)
            dve.wait_ge(S("so_rec"), 1)
            for t in range(RT + 1):
                if t < RT:
                    nr = ROWS[t]
                    tt(oN[0:nr, t], oN[0:nr, t], rso[0:nr, t, :].unsqueeze(2).to_broadcast([nr, A_H, P]), ALU.mult) \
                        .then_inc(S("so_n"), 1)
                if t >= 1:
                    nr, cols = ROWS[t - 1], slice(P * (t - 1), P * (t - 1) + ROWS[t - 1])
                    dve.wait_ge(S("so_hi"), t)
                    split_lo(xn0[1][:, 0:4, cols], PS[:, 4 + (t - 1) % 2, :].rearrange("p (h r) -> p h r", h=4)[:, :, 0:nr],
                             xn0[0][:, 0:4, cols], subg[:, 0:1]).then_inc(S("so_lo"), 1)

            def add_residual(s, k):
                for (src, dst) in pieces(s, H[:, bass.ds(k, 1), :].rearrange("p k r -> p (k r)")):
                    last = tt(dst, src, dst, ALU.add)
                last.then_inc(S("fin_h"), 1)

            def finish_lo(k, c, x, gain):
                if x:
                    dve.wait_ge(S("fin_hi"), c + 1)
                    split_lo(x[1][:, bass.ds(k, 1), :], H[:, bass.ds(k, 1), :], x[0][:, bass.ds(k, 1), :],
                             par[:, 6, bass.ds(k + gain, 1)]).then_inc(S("fin_lo"), 1)

            def add_squares(c, n):
                dve.wait_ge(S("fin_sq"), c + 1)
                if not isinstance(c, int) or c > 0:
                    dve.wait_ge(S("acc_done"), c - (n - 1))
                tt(acc[:, :], acc[:, :], sq[:, :], ALU.add).then_inc(S("acc_done"), 1)

            def out_projection(o):
                t, l = o["tag"], o["l"]

                def w_lo(u, s):
                    reached(dve, l, f"{t}_hi", u + 1)
                    split_lo(wlo[:, s], wraw[:, s], whi[:, s]).then_inc(S(f"{t}_lo"), 1)

                def step(k, s, more):
                    reached(dve, l, f"{t}_mm", k + 1)
                    add_residual(s, k)
                    if more:
                        w_lo(k + 2, s)
                    if isinstance(k, int) and k == 7:
                        ffn_first_lo(FFN[l])
                    finish_lo(k, 8 * (o["n"] - 1) + k, o["y"], o["gain"])
                    if not isinstance(k, int) or k < 7:
                        add_squares(8 * (o["n"] - 1) + k, o["n"])

                dve.wait_ge(S("acc_zero"), o["n"])
                for s in range(2):
                    step(s, s, True)
                with dve.Fori(1, 3) as j:
                    for s in range(2):
                        step(2 * j + s, s, True)
                for s in range(2):
                    step(6 + s, s, False)

            def odd_lo(u, s):
                reached(dve, 1, "in_hi", u + 1)
                split_lo(wlo[:, s], wraw[:, s], whi[:, s]).then_inc(S("in_lo"), 1)

            def ffn_first_lo(f):
                t, b, l = f["tag"], f["b"], f["l"]
                reached(dve, l, f"{t}_uphi", 1)
                split_lo(b.uplo[:, 0], graw[:, :, 0:P], b.uphi[:, 0]).then_inc(S(f"{t}_uplo"), 1)

            def ffn(f):
                t, b, l = f["tag"], f["b"], f["l"]

                def w_lo(s, half, raw, count):
                    reached(dve, l, f"{t}_uphi", count)
                    split_lo(b.uplo[:, s], raw[:, :, half * P:(half + 1) * P], b.uphi[:, s]).then_inc(S(f"{t}_uplo"), 1)

                def extend(s, T, count, ps):
                    e = b.ext[:, s, :]
                    reached(dve, l, f"{t}_upmm", count)
                    nc.vector.tensor_copy(e[:, 2 + SEQ:4 + SEQ].unsqueeze(2),
                                          par[:, 3 * l + 2, :].rearrange("p (i t) -> p i t", i=2)[:, :, bass.ds(T + FT * s, 1)])
                    tt(e[:, 2:730].rearrange("p (c n) -> p c n", c=2), PS[:, 3 * ps:3 * ps + 2, 0:364],
                       rB[:, 0:728].rearrange("p (c n) -> p c n", c=2), ALU.mult)
                    tt(e[:, 730:2 + SEQ], PS[:, 3 * ps + 2, 0:SEQ - 728], rB[:, 728:SEQ], ALU.mult)
                    tt(e[:, 4 + SEQ:EXT], PS[:, 3 * ps + 2, SEQ - 728:360], rB[:, SEQ:R], ALU.mult) \
                        .then_inc(S(f"{t}_{'gv'[s]}ext"), 1)

                def taps(s, T):
                    k, col = "gv"[s], T + FT * s
                    e, c = b.ext[:, s, :], b.c[:, s, :]
                    reached(dve, l, f"{t}_{k}tap", T + 1)
                    nc.vector.scalar_tensor_tensor(out=c, in0=e[:, 1:EXT - 1], scalar=par[:, 3 * l, bass.ds(col + 44, 1)],
                                                   in1=c, op0=ALU.mult, op1=ALU.add).then_inc(S(f"{t}_{k}mid"), 1)
                    reached(dve, l, f"{t}_{k}mid", T + 1)
                    nc.vector.scalar_tensor_tensor(out=c, in0=e[:, 2:EXT], scalar=par[:, 3 * l + 1, bass.ds(col, 1)],
                                                   in1=c, op0=ALU.mult, op1=ALU.add).then_inc(S(f"{t}_{k}conv"), 1)

                def gate(T, s):
                    reached(dve, l, f"{t}_silu", T + 1)
                    reached(dve, l, f"{t}_vconv", T + 1)
                    h = b.ext[:, 1, 4:EXT]
                    tt(h[:, 0:SEQ], b.c[:, 0, 0:SEQ], b.c[:, 1, 0:SEQ], ALU.mult)
                    tt(h[:, SEQ:R], b.c[:, 0, SEQ + 2:EXT - 2], b.c[:, 1, SEQ + 2:EXT - 2], ALU.mult).then_inc(S(f"{t}_h"), 1)
                    reached(dve, l, f"{t}_hhi", T + 1)
                    split_lo(b.hlo[:, s, :], h, b.hhi[:, s, :]).then_inc(S(f"{t}_hlo"), 1)

                def d_lo(i):
                    reached(dve, l, f"{t}_dhi", i + 1)
                    split_lo(b.dlo[:, :, :], draw[:, :, :], b.dhi[:, :, :]).then_inc(S(f"{t}_dlo"), 1)

                def down(i, ks):
                    for k in ks:
                        reached(dve, l, f"{t}_dnmm", 8 * i - 7 + k)
                        for src, dst in pieces((k + 1) % 2, H[:, k, :]):
                            last = tt(dst, src, dst, ALU.add)
                        last.then_inc(S(f"{t}_dnev"), 1)

                def block_(i, first, last):
                    if not first:
                        extend(1, 2 * i - 1, 4 * i, 1)
                        taps(1, 2 * i - 1)
                        gate(2 * i - 1, 1)
                    w_lo(1, 0, vraw, 4 * i + 2)
                    if first:
                        norm_dve_diag(dve, f["n"])
                        w_lo(0, 1, graw, 3)
                        norm_dve_rb(dve, f["n"])
                        dve.wait_ge(S("n_rb"), 3 * f["n"] + 3)
                    extend(0, 2 * i, 4 * i + 1, 0)
                    if not first:
                        down(i, [0])
                    taps(0, 2 * i)
                    if not first:
                        down(i, [1, 2])
                        w_lo(0, 1, graw, 4 * i + 3)
                        down(i, range(3, KT))
                        d_lo(i)
                    extend(1, 2 * i, 4 * i + 2, 1)
                    taps(1, 2 * i)
                    w_lo(1, 1, vraw, 4 * i + 4)
                    if first:
                        d_lo(i)
                    gate(2 * i, 0)
                    extend(0, 2 * i + 1, 4 * i + 3, 0)
                    taps(0, 2 * i + 1)
                    if not last:
                        w_lo(0, 0, graw, 4 * i + 5)

                for s in range(2):
                    nc.vector.memset(b.ext[:, s, 0:2], 0.0)
                block_(0, True, False)
                with dve.Fori(1, NB - 1) as i:
                    block_(i, False, False)
                block_(NB - 1, False, True)
                extend(1, 2 * NB - 1, 4 * NB, 1)
                taps(1, 2 * NB - 1)
                gate(2 * NB - 1, 1)
                if l == 0:
                    for s in range(2):
                        odd_lo(s, s)
                for k in range(KT + 1):
                    c = 8 * f["n"] + k
                    if k < KT:
                        reached(dve, l, f"{t}_dnmm", 8 * NB - 7 + k)
                        add_residual(k % 2, k)
                    if k >= 1:
                        finish_lo(k - 1, c - 1, f["y"], f["gain"])
                        if f["y"] is None:
                            dve.wait_ge(S("fin_sq"), c)
                            nc.vector.tensor_scalar(H[:, k - 1, :], H[:, k - 1, :], param(6, P_NFIN + k - 1), None,
                                                    ALU.mult).then_inc(S("fin_g"), 1)

            out_projection(OUTP[0])
            ffn(FFN[0])

            def odd_rope(u, out):
                b = par[:, 6, bass.ds(u + P_BIN, 1)]
                reached(dve, 1, "in_sw", u + 1)
                nc.vector.scalar_tensor_tensor(out=z_o[:, :], in0=z_o[:, :], scalar=b, in1=cos_o[:, :],
                                               op0=ALU.add, op1=ALU.mult)
                tt(zs_o[:, :], zs_o[:, :], sin_o[:, :], ALU.mult).then_inc(S("in_rz"), 1)
                reached(dve, 1, "in_rz", u + 1)
                tt(out, z_o[:, :].unsqueeze(1), zs_o[:, :].unsqueeze(1), ALU.add).then_inc(S("in_rope"), 1)

            def odd_unit(u, s, more, out):
                reached(dve, 1, "in_mm", u + 1)
                if not isinstance(u, int) or u:
                    reached(dve, 1, "in_rope", u)
                scaled_by_row(s, z_o).then_inc(S("in_ev"), 1)
                if more:
                    odd_lo(u + 2, s)
                odd_rope(u, out)

            norm_dve_diag(dve, 2)
            norm_dve_rb(dve, 2)
            dve.wait_ge(S("n_rb"), 9)
            dve.wait_ge(S("tab_in"), 192)
            for s in range(2):
                odd_unit(s, s, True, q2T[:, s:s + 1, :])
            with dve.Fori(1, 4) as j:
                for s in range(2):
                    odd_unit(2 * j + s, s, True, q2T[:, bass.ds(2 * j + s, 1), :])
            odd_unit(8, 0, False, z_o[:, :].unsqueeze(1))
            reached(dve, 1, "in_mm", 10)
            scaled_by_row(1, vz_o).then_inc(S("in_ev"), 1)
            reached(dve, 1, "in_ev", 10)
            nc.vector.tensor_scalar(vz_o[:, :], vz_o[:, :], param(6, P_BIN + 9), None, ALU.add).then_inc(S("oi_vz"), 1)

            def by_head(x):
                return x.rearrange("p (j a) -> p a j", a=2)

            def quad(x):
                return x.rearrange("p (a j) -> p a j", a=2)

            def odd_max(q):
                t, b = BATCHES[q]
                nq, (c0, c1), v = ROWS[t], WIN[t], q % 2
                dve.wait_ge(S("o_s"), q + 1)
                if q >= 2:
                    dve.wait_ge(S("o_es"), q - 1)
                nc.vector.tensor_reduce(m2[0:nq, v, :],
                                        PS[0:nq, 2 * v:2 * v + 2, :].rearrange("p b (j c) -> p (b j) c", j=2)[:, :, c0:c1],
                                        AX_X, ALU.max).then_inc(S("o_m"), 1)
                dve.wait_ge(S("o_m"), 2 * q + 1)
                sink = by_head(sinkb[0:nq, 4 * b:4 * b + 4])
                nc.vector.scalar_tensor_tensor(out=quad(m2[0:nq, v, :]), in0=quad(m2[0:nq, v, :]), scalar=C_DH ** -0.5,
                                               in1=sink, op0=ALU.mult, op1=ALU.max).then_inc(S("o_m"), 1)
                dve.wait_ge(S("o_m"), 2 * q + 2)
                tt(quad(snk2[0:nq, v, :]), sink, quad(m2[0:nq, v, :]), ALU.subtract)
                nc.vector.tensor_scalar(nm2[0:nq, v, :], m2[0:nq, v, :], -1.0, None, ALU.mult).then_inc(S("o_nm"), 1)

            def odd_den(q):
                nq, v = ROWS[BATCHES[q][0]], q % 2
                dve.wait_ge(S("o_es"), q + 1)
                dve.wait_ge(S("o_exp"), q + 1)
                tt(den2[0:nq, v, :], sum2[0:nq, v, :], es2[0:nq, v, :], ALU.add).then_inc(S("o_rd"), 1)
                dve.wait_ge(S("o_rd"), 2 * q + 1)
                nc.vector.reciprocal(rd2[0:nq, v, :], den2[0:nq, v, :]).then_inc(S("o_rd"), 1)

            def odd_out(q):
                t, b = BATCHES[q]
                nq, v = ROWS[t], q % 2
                dve.wait_ge(S("o_pv"), q + 1)
                dve.wait_ge(S("o_rd"), 2 * q + 2)
                if b % 2 == 0 and t >= 1:
                    dve.wait_ge(S("om_tr"), 2 * t - 1 + b // 2)
                tt(oN2[0:nq, 256 * b:256 * b + 256].rearrange("p (j a d) -> p a j d", j=2, a=2),
                   PS[0:nq, 6, 0:256].rearrange("p (a j d) -> p a j d", a=2, j=2),
                   quad(rd2[0:nq, v, :]).unsqueeze(3).to_broadcast([nq, 2, 2, C_DH]), ALU.mult).then_inc(S("o_o"), 1)

            def odd_probs_last(q):
                t, b = BATCHES[q]
                nq, v = ROWS[t], q % 2
                bs = DEC if t == 8 else P
                if q >= 2:
                    dve.wait_ge(S("o_pv"), q - 1)
                dve.wait_ge(S("o_tr"), OFILL[q + 1])
                nc.vector.tensor_copy(PT2[0:bs, v, 1, :, 0:nq],
                                      PS[0:bs, 5, :].rearrange("p (i q) -> p i q", i=4)[:, :, 0:nq]).then_inc(S("o_tev1"), 1)

            def odd_rows_lo(f):
                t, j = f // 2, f % 2
                nr = ROWS[t]
                dve.wait_ge(S("om_hi"), f + 1)
                split_lo(xn1[1][:, 4 * j:4 * j + 4, P * t:P * t + nr],
                         PS[:, 7, :].rearrange("p (k r) -> p k r", k=4)[:, :, 0:nr],
                         xn1[0][:, 4 * j:4 * j + 4, P * t:P * t + nr]).then_inc(S("om_lo"), 1)

            for q in range(STEPS):
                if q < NQ:
                    odd_max(q)
                if rows_step(q) is not None:
                    odd_rows_lo(rows_step(q))
                if 1 <= q <= NQ:
                    odd_probs_last(q - 1)
                    odd_den(q - 1)
                if 2 <= q <= NQ + 1:
                    odd_out(q - 2)
                if q in (NQ - 3, NQ - 1):
                    op_first_lo(1, q // (NQ - 1))

            out_projection(OUTP[1])
            ffn(FFN[1])

            norm_dve_diag(dve, 4)
            dve.wait_ge(S("n_rec"), 5)
            for t in range(RT):
                dve.wait_ge(S("y_tr"), 2 * t + 2)
                nc.vector.tensor_scalar(yN[0:ROWS[t], t, 512:1024], PS[0:ROWS[t], (2 * t + 1) % 6, :],
                                        rs[0:ROWS[t], t:t + 1], None, ALU.mult).then_inc(S("y_dve"), 1)

        @block.tensor
        def _(pe):
            pe.wait_ge(S("c_set"), C_IDENT)

            def gains_in():
                pe.wait_ge(S("gain_in"), 16 * 7)
                nc.tensor.transpose(PS[:, 7, 176:176 + P_ROWS6], pnat[0:P_ROWS6, 6, :], ident[0:P_ROWS6, 0:P_ROWS6])
                for g in range(4):
                    last = nc.tensor.transpose(PS[:, 7, 240 + HIST * g:240 + HIST * (g + 1)], hnat[:, g * P:(g + 1) * P],
                                               ident[0:HIST, 0:HIST])
                last.then_inc(S("par_tr"), 1)

            def params_in():
                pe.wait_ge(S("par_in"), 16 * 8)
                pe.wait_ge(S("par_ev"), 2)
                for n in range(6):
                    col = 88 * (n % 4)
                    last = nc.tensor.transpose(PS[:, 6 + n // 4, col:col + 88], pnat[0:88, n, :], ident[0:88, 0:88])
                    if n == 3:
                        last.then_inc(S("par_tr"), 1)
                last.then_inc(S("par_tr"), 1)

            def x_rows(t):
                nr = ROWS[t]
                pe.wait_ge(S(X_IN[t]), 16)
                for j in range(2):
                    f = 2 * t + j
                    if f >= 3:
                        pe.wait_ge(S("x_lo"), f - 2)
                    for i in range(4):
                        k = 4 * j + i
                        last = nc.tensor.transpose(PS[:, 3 + f % 3, i * P:i * P + nr], xnat[0:nr, t, k * P:(k + 1) * P],
                                                   ident[0:nr, 0:nr])
                    last.then_inc(S("x_tr"), 1)

            def to_rows(f):
                g, is_v, a, n = row_fill(f)
                if f >= 2:
                    pe.wait_ge(S("ei_tev"), f - 1)
                if is_v:
                    reached(pe, 0, "in_ev", 4 * g + 4)
                else:
                    reached(pe, 0, "in_rope", 2 * g + 2)
                src = vz_e if is_v else kT[:, g, :]
                for i in range(n):
                    t = a + i
                    last = nc.tensor.transpose(PS[0:ROWS[t], 6 + f % 2, i * P:(i + 1) * P], src[:, rows_of(t)], ident[:, :])
                last.then_inc(S("ei_tr"), 1)

            def first_unit():
                for c, (a, width) in enumerate(CHUNKS):
                    for t in range(3 * c, 3 * c + 3):
                        x_rows(t)
                    if c == 0:
                        gains_in()
                        reached(pe, 0, "in_lo", 1)
                    pe.wait_ge(S("x_lo"), 6 * (c + 1))
                    for k in range(KT):
                        hi, lo = xn0[0][:, k, a:a + width], xn0[1][:, k, a:a + width]
                        for n, (w, x) in enumerate(((whi, hi), (whi, lo), (wlo, hi))):
                            last = nc.tensor.matmul(PS[:, c, 0:width], w[:, 0, k, :], x,
                                                    start=(k == 0 and n == 0), stop=(k == KT - 1 and n == 2))
                last.then_inc(S("in_mm"), 1)

            def even_unit(u):
                s = u % 2
                reached(pe, 0, "in_lo", u + 1)
                if u >= 2:
                    reached(pe, 0, "in_ev", u - 1)
                after = norm_bcast_after(pe, 0) if u == 1 else None
                for k in range(KT):
                    last = products(s, k, KT, whi[:, s, k, :], wlo[:, s, k, :], xn0[0][:, k, :], xn0[1][:, k, :])
                    if after:
                        after(k)
                last.then_inc(S("in_mm"), 1)

            first_unit()
            for u in range(1, 16):
                if u == 1:
                    params_in()
                even_unit(u)
                for f in row_fills_after(u):
                    to_rows(f)

            def pool_product(n):
                g = POOL_ORDER[n]
                pe.wait_ge(S("pm_plo"), n + 1)
                if n >= 2:
                    pe.wait_ge(S("pm_ev"), n - 1)
                products(n % 2, 0, 1, pwhi[:, g, :], pwlo[:, g, :],
                         xn0[0][:, 4 + g, :], xn0[1][:, 4 + g, :]).then_inc(S("pm_mm"), 1)

            pe.wait_ge(S("pw_lo"), 1)
            for f in range(20, 24):
                to_rows(f)
            for n in range(4):
                pool_product(n)
            pe.wait_ge(S("ei_tev"), 24)
            pe.wait_ge(S("ei_ue"), 4)
            for st in range(2):
                for g in range(4):
                    last = nc.tensor.transpose(PS[0:HIST, 6 + st, g * P:(g + 1) * P], ue[:, g, st, :], ident[:, :])
            last.then_inc(S("ue_tr"), 1)
            pe.wait_ge(S("kc_in"), 16)
            pe.wait_ge(S("pm_ev"), 4)
            for b in range(2):
                for h in range(A_H):
                    last = nc.tensor.transpose(PS[:, 4 + b, h * P:(h + 1) * P], kcn[:, b, h * P:(h + 1) * P], ident[:, :])
                last.then_inc(S("kc_tr"), 1)

            def scores(p):
                t, h = PAIRS[p]
                nq, L = ROWS[t], KEYS[t]
                for m in range(2):
                    before = p if p and (two_banks(p) or two_banks(p - 1)) else p - 1
                    if before > 0:
                        pe.wait_ge(S(f"at_exp{m}"), before)
                    half = slice(64 * m, 64 * m + 64)
                    for a in range(0, L, 512):
                        w = min(512, L - a)
                        masked = t < 8 and a + w == L
                        out = PS[0:nq, 2 * m + (a // 512 if two_banks(p) else p % 2), 0:w]
                        keys = kT[half, h, a:a + w] if t < 8 else kAll[half, h, a:a + w]
                        last = nc.tensor.matmul(out, qT[half, h, rows_of(t)], keys, start=True, stop=not masked)
                        if masked:
                            last = nc.tensor.matmul(out[:, w - 64:w], maskL[half, :], maskR[half, 0, 192:256],
                                                    start=False, stop=True)
                    last.then_inc(S(f"at_s{m}"), 1)

            def probs(p):
                t, h = PAIRS[p]
                nq = ROWS[t]
                pe.wait_ge(S("at_comb"), p + 1)
                for j, (f, n) in enumerate(FILLS[t]):
                    F = FIRST_FILL[p] + j
                    if F >= 2:
                        pe.wait_ge(S("at_tev"), F - 1)
                    for i in range(n):
                        a, w = BLOCKS[t][f + i]
                        last = nc.tensor.transpose(PS[0:w, 4 + F % 2, i * P:i * P + nq], comb[0:nq, p % 2, a:a + w], ident[0:nq, 0:nq])
                    last.then_inc(S("at_tr"), 1)

            def values(p):
                t, h = PAIRS[p]
                nq = ROWS[t]
                pe.wait_ge(S("at_tev"), FIRST_FILL[p + 1])
                if p >= 2:
                    pe.wait_ge(S("at_o"), p - 1)
                n = len(BLOCKS[t])
                for b, (a, w) in enumerate(BLOCKS[t]):
                    if t < 8:
                        v = vN[0:w, b, h * P:(h + 1) * P]
                    else:
                        v = vcn[:, b, h * P:(h + 1) * P] if b < 2 else vN[0:DEC, 8, h * P:(h + 1) * P]
                    last = nc.tensor.matmul(PS[0:nq, 6 + p % 2, 0:P], AT[0:w, p % 2, b * P:b * P + nq], v,
                                            start=b == 0, stop=b == n - 1)
                last.then_inc(S("at_pv"), 1)

            pe.wait_ge(S("c_set"), C_ALL)
            for p in range(NP_ + 2):
                if p < NP_:
                    scores(p)
                if p >= 2:
                    if p == 2:
                        pe.wait_ge(S("ue_ev"), 1)
                        pe.wait_ge(S("vc_in"), 16)
                    values(p - 2)
                if 1 <= p <= NP_:
                    if p == 1:
                        pe.wait_ge(S("kc_ev"), 3)
                    probs(p - 1)
            for t in range(RT):
                nr = ROWS[t]
                pe.wait_ge(S("so_n"), t + 1)
                if t >= 2:
                    pe.wait_ge(S("so_lo"), t - 1)
                for h in range(A_H):
                    last = nc.tensor.transpose(PS[:, 4 + t % 2, h * P:h * P + nr], oN[0:nr, t, h, :], ident[0:nr, 0:nr])
                last.then_inc(S("so_tr"), 1)
                if t == 0:
                    pe.wait_ge(S("op_lo"), 1)
                if t < 4:
                    k = OUTP[0]["ks"][t]
                    products(0, t, KT, whi_op[0][:, 0, k, :], wlo_op[0][:, 0, k, :], xn0[0][:, k, :], xn0[1][:, k, :])
            pe.wait_ge(S("so_lo"), RT)

            def out_projection(o):
                t, l, x = o["tag"], o["l"], o["x"]
                c0 = 8 * (o["n"] - 1)

                def unit(u, s, hi, lo, free):
                    reached(pe, l, f"{t}_lo", u + 1)
                    if free is not None:
                        pe.wait_ge(S("fin_h"), free)
                    for n, k in enumerate(o["ks"]):
                        if l == 0 and isinstance(u, int) and u == 0 and n < 4:
                            continue
                        last = products(s, n, KT, hi[:, s, k, :], lo[:, s, k, :], x[0][:, k, :], x[1][:, k, :])
                    last.then_inc(S(f"{t}_mm"), 1)

                for s in range(2):
                    unit(s, s, whi_op[l], wlo_op[l], None)
                with pe.Fori(1, 4) as j:
                    for s in range(2):
                        unit(2 * j + s, s, whi, wlo, c0 + 2 * j + s - 1)

            def ffn(f):
                t, b, l, x = f["tag"], f["b"], f["l"], f["x"]

                def up(s, ps, count, after=None):
                    reached(pe, l, f"{t}_uplo", count)
                    for k in range(KT):
                        last = products(ps, k, KT, b.uphi[:, s, k, :], b.uplo[:, s, k, :], x[0][:, k, :], x[1][:, k, :])
                        if after:
                            after(k)
                    last.then_inc(S(f"{t}_upmm"), 1)

                def first_gate():
                    reached(pe, l, f"{t}_uplo", 1)
                    for k in range(KT):
                        pe.wait_ge(S("fin_lo"), 8 * f["l"] * 2 + k + 1)
                        last = products(0, k, KT, b.uphi[:, 0, k, :], b.uplo[:, 0, k, :], x[0][:, k, :], x[1][:, k, :])
                    last.then_inc(S(f"{t}_upmm"), 1)

                def down_products(k, ps, ns):
                    c = slice(k * P, (k + 1) * P)
                    for n in ns:
                        last = products(ps, n, 2, b.dhi[:, n, c], b.dlo[:, n, c], b.hhi[:, n, :], b.hlo[:, n, :])
                    return last

                def down(i):
                    reached(pe, l, f"{t}_dlo", i)
                    reached(pe, l, f"{t}_hlo", 2 * i)
                    for k in range(KT):
                        if k == 0:
                            reached(pe, l, f"{t}_vext", 2 * i)
                        elif k == 1:
                            reached(pe, l, f"{t}_gext", 2 * i + 1)
                        else:
                            reached(pe, l, f"{t}_dnev", 8 * i - 8 + k - 1)
                        down_products(k, (k + 1) % 2, (0, 1)).then_inc(S(f"{t}_dnmm"), 1)

                def down_last():
                    reached(pe, l, f"{t}_dlo", NB)
                    reached(pe, l, f"{t}_hlo", 2 * NB - 1)
                    for k in range(2):
                        reached(pe, l, f"{t}_{'gv'[k]}ext", 2 * NB)
                        down_products(k, k, (0,))
                    reached(pe, l, f"{t}_hlo", 2 * NB)
                    for k in range(2):
                        down_products(k, k, (1,)).then_inc(S(f"{t}_dnmm"), 1)
                    for k in range(2, KT):
                        pe.wait_ge(S("fin_h"), 8 * f["n"] + k - 1)
                        down_products(k, k % 2, (0, 1)).then_inc(S(f"{t}_dnmm"), 1)

                def rest(i, first):
                    if not first:
                        reached(pe, l, f"{t}_dnev", 8 * i - 1)
                    up(1, 1, 4 * i + 2, norm_bcast_after(pe, f["n"]) if first else None)
                    if first:
                        reached(pe, l, f"{t}_gext", 1)
                    else:
                        reached(pe, l, f"{t}_dnev", 8 * i)
                    up(0, 0, 4 * i + 3)
                    reached(pe, l, f"{t}_vext", 2 * i + 1)
                    up(1, 1, 4 * i + 4)

                c0 = 8 * f["n"]
                pe.wait_ge(S("fin_h"), c0 - 1)
                first_gate()
                norm_pe_stats(pe, f["n"])
                pe.wait_ge(S("fin_h"), c0)
                rest(0, True)
                with pe.Fori(1, NB) as i:
                    reached(pe, l, f"{t}_gext", 2 * i)
                    up(0, 0, 4 * i + 1)
                    down(i)
                    rest(i, False)
                down_last()
                reached(pe, l, f"{t}_vtap", FT)
                for a in range(2):
                    last = nc.tensor.transpose(PS[0:4 * FT, 7, a * P:(a + 1) * P],
                                               edge[:, a, :, :].rearrange("p i t -> p (i t)"), ident[:, :])
                last.then_inc(S("ed_tr"), 1)

            out_projection(OUTP[0])
            ffn(FFN[0])

            def odd_unit(u, s, free, after=None):
                reached(pe, 1, "in_lo", u + 1)
                if free is not None:
                    reached(pe, 1, "in_ev", free)
                for k in range(KT):
                    if free is None:
                        pe.wait_ge(S("fin_lo"), 8 + k + 1)
                    last = products(s, k, KT, whi[:, s, k, :], wlo[:, s, k, :], xn1[0][:, k, :], xn1[1][:, k, :])
                    if after:
                        after(k)
                last.then_inc(S("in_mm"), 1)

            pe.wait_ge(S("fin_h"), 15)
            odd_unit(0, 0, None)
            norm_pe_stats(pe, 2)
            pe.wait_ge(S("fin_h"), 16)
            pe.wait_ge(S("ed_ev"), 1)
            odd_unit(1, 1, None, norm_bcast_after(pe, 2))
            with pe.Fori(1, 5) as j:
                for s in range(2):
                    odd_unit(2 * j + s, s, 2 * j + s - 1)
            reached(pe, 1, "in_rope", 9)
            pe.wait_ge(S("ed_ev"), 1)
            nc.tensor.transpose(PS[:, 6, 0:P], z_o[:, 7 * P:8 * P], ident[:, :])
            nc.tensor.transpose(PS[0:DEC, 6, P:2 * P], z_o[:, SEQ:R], ident[:, :]).then_inc(S("oi_ktr"), 1)
            pe.wait_ge(S("kc_in"), 32)
            nc.tensor.transpose(PS[:, 7, 0:P], kc2n[:, :], ident[:, :]).then_inc(S("kc2_tr"), 1)
            pe.wait_ge(S("oi_vz"), 1)
            for j, (a, n) in enumerate(((0, 4), (4, 4), (8, 1))):
                for i in range(n):
                    t = a + i
                    last = nc.tensor.transpose(PS[0:ROWS[t], 3 + j, i * P:(i + 1) * P], vz_o[:, rows_of(t)], ident[:, :])
                last.then_inc(S("oi_vtr"), 1)

            def odd_scores(q):
                t, b = BATCHES[q]
                nq, (c0, c1), v = ROWS[t], WIN[t], q % 2
                if q >= 2:
                    pe.wait_ge(S("o_exp"), q - 1)
                for jj in range(2):
                    for par_ in range(2):
                        half = slice(64 * par_, 64 * par_ + 64)
                        if t < 8:
                            keys = kd[half, b // 2, (t - 1) * P + c0:(t - 1) * P + c1]
                        else:
                            keys = kds[half, b // 2, 0:c1]
                        last = nc.tensor.matmul(PS[0:nq, 2 * v + par_, jj * 256 + c0:jj * 256 + c1], q2T[half, 2 * b + jj, rows_of(t)],
                                                keys, start=jj == 0, stop=t == 8 and jj == 1, skip_group_check=True)
                if t < 8:
                    for par_ in range(2):
                        half = slice(64 * par_, 64 * par_ + 64)
                        last = nc.tensor.matmul(PS[0:nq, 2 * v + par_, :].rearrange("p (j c) -> p j c", j=2)[:, :, c0:c1],
                                                maskL[half, :], maskR[half, :, c0:c1], start=False, stop=True,
                                                skip_group_check=True)
                last.then_inc(S("o_s"), 1)

            def left(q):
                pe.wait_ge(S("o_tev1"), q + 1)
                if q >= 4:
                    pe.wait_ge(S("o_tev0"), q - 3)

            def odd_probs(q):
                t, b = BATCHES[q]
                nq, v = ROWS[t], q % 2
                pe.wait_ge(S("o_exp"), q + 1)
                if q >= 1:
                    left(q - 1)
                for kt in key_tiles(t):
                    bs = DEC if (t == 8 and kt == 1) else P
                    for i in range(4):
                        last = nc.tensor.transpose(PS[0:bs, 4 + kt, i * P:i * P + nq], E2[0:nq, v, i, kt * P:kt * P + bs], ident[0:nq, 0:nq])
                    last.then_inc(S("o_tr"), 1)

            def odd_values(q):
                t, b = BATCHES[q]
                nq, v, g = ROWS[t], q % 2, b // 2
                left(q)
                if q >= 1:
                    pe.wait_ge(S("o_o"), q)
                kts = key_tiles(t)
                for i in range(4):
                    for kt in kts:
                        bs = DEC if (t == 8 and kt == 1) else P
                        if t < 8:
                            vals = v2N[:, t - 1 + kt, g * C_DH:(g + 1) * C_DH]
                        else:
                            vals = (v2N[0:DEC, 8] if kt else vc2[:, :])[:, g * C_DH:(g + 1) * C_DH]
                        last = nc.tensor.matmul(PS[0:nq, 6, i * C_DH:(i + 1) * C_DH], PT2[0:bs, v, kt, i, 0:nq], vals,
                                                start=kt == kts[0], stop=kt == 1)
                last.then_inc(S("o_pv"), 1)

            def odd_rows(f):
                t, j = f // 2, f % 2
                nr = ROWS[t]
                pe.wait_ge(S("o_o"), 2 * f + 2)
                if f >= 1:
                    pe.wait_ge(S("om_lo"), f)
                for i in range(4):
                    k = 4 * j + i
                    last = nc.tensor.transpose(PS[:, 7, i * P:i * P + nr], oN2[0:nr, k * P:(k + 1) * P], ident[0:nr, 0:nr])
                last.then_inc(S("om_tr"), 1)

            pe.wait_ge(S("oi_kds"), 1)
            pe.wait_ge(S("oi_vn"), 3)
            pe.wait_ge(S("vc_in"), 32)
            for q in range(STEPS):
                if q < NQ:
                    odd_scores(q)
                if rows_step(q) is not None:
                    odd_rows(rows_step(q))
                if 1 <= q <= NQ:
                    odd_probs(q - 1)
                if 2 <= q <= NQ + 1:
                    odd_values(q - 2)

            pe.wait_ge(S("om_lo"), 2 * RT)
            out_projection(OUTP[1])
            ffn(FFN[1])

            norm_pe_stats(pe, 4)
            pe.wait_ge(S("fin_g"), KT)
            for t in range(RT):
                nr = ROWS[t]
                for j in range(2):
                    f = 2 * t + j
                    if f >= 6:
                        pe.wait_ge(S("y_dve") if j else S("y_act"), t - 2)
                    for i in range(4):
                        last = nc.tensor.transpose(PS[0:nr, f % 6, i * P:(i + 1) * P], H[:, 4 * j + i, rows_of(t)], ident[:, :])
                    last.then_inc(S("y_tr"), 1)


_INS = ["x_prompt", "x_sample", "cache_diff_k", "cache_diff_v", "state_pool", "cache_swa_k", "cache_swa_v",
        "state_ffn_conv", "norm_attn", "norm_ffn", "norm_final", "w_in_even", "w_out_even", "diff_lambda",
        "diff_subln", "pool_w", "pool_scale", "w_in_odd", "b_in_odd", "w_out_odd", "sinks", "w_up", "conv_w",
        "conv_b", "w_down"]
_OUTS = [("y_prompt", (1, SEQ, D)), ("y_sample", (1, DEC, D)),
         ("diff_k_prompt", (1, 1, SEQ, A_H, 2, A_DH)), ("diff_v_prompt", (1, 1, SEQ, A_H, 2 * A_DH)),
         ("pool_prompt", (1, 1, HIST, A_W)),
         ("swa_k_prompt", (1, 1, C_CACHE, C_KV, C_DH)), ("swa_v_prompt", (1, 1, C_CACHE, C_KV, C_DH)),
         ("ffn_conv_prompt", (2, 1, 2, 2 * FF)),
         ("diff_k_sample", (1, 1, DEC, A_H, 2, A_DH)), ("diff_v_sample", (1, 1, DEC, A_H, 2 * A_DH)),
         ("pool_sample", (1, 1, HIST, A_W)),
         ("swa_k_sample", (1, 1, C_CACHE, C_KV, C_DH)), ("swa_v_sample", (1, 1, C_CACHE, C_KV, C_DH)),
         ("ffn_conv_sample", (2, 1, 2, 2 * FF))]


def tables():
    inv = np.float32(10000.0) ** (-np.arange(0, A_DH, 2, dtype=np.float32) / np.float32(A_DH))
    pos = np.concatenate([np.arange(SEQ), PAST + np.arange(DEC)]).astype(np.float32)
    ang = inv[:, None] * pos[None, :]
    cos, sin = np.cos(ang).astype(np.float32), np.sin(ang).astype(np.float32)
    counts = [[1.0 / min(w, t + 1) for t in range(HIST)] for w in WINDOWS]
    return {"cos_t": cos, "sin_t": np.concatenate([-sin, sin]),
            "rcnt_t": np.array(counts, np.float32).reshape(-1)}


def kernel(**inputs):
    import concourse.bacc as bacc
    from concourse.bass_utils import run_bass_kernel_spmd

    nc = bacc.Bacc("TRN2", target_bir_lowering=False, num_devices=1, dynamic_dma_scratch_size=1024)
    arrays, io = {}, {}
    for name in _INS:
        arrays[f"in_{name}"] = np.ascontiguousarray(inputs[name])
    for name, table in tables().items():
        arrays[f"in_{name}"] = table
    for name, a in arrays.items():
        io[name[3:]] = nc.dram_tensor(name, a.shape, mybir.dt.from_np(a.dtype), kind="ExternalInput").ap()
    for name, shape in _OUTS:
        io[name] = nc.dram_tensor(f"out_{name}", shape, F32, kind="ExternalOutput").ap()
    build(nc, io)
    r = run_bass_kernel_spmd(nc, [arrays], core_ids=[0])
    return tuple(r.results[0][f"out_{name}"] for name, _ in _OUTS)
```

```python
import math
from contextlib import ExitStack

import numpy as np
import concourse.bass as bass
from concourse import mybir

F32 = mybir.dt.float32
F32R = mybir.dt.float32r
BF16 = mybir.dt.bfloat16
ALU = mybir.AluOpType
ACT = mybir.ActivationFunctionType
AX_X = mybir.AxisListType.X

P = 128
D = 1024
KT = D // P
SEQ, DEC = 1024, 64
R = SEQ + DEC
PAST = 256
A_H, A_DH = 4, 64
A_W = A_H * 2 * A_DH
WINDOWS = (2, 4, 8, 16)
HIST = 15
C_H, C_KV, C_DH, C_CACHE = 16, 2, 64, 128
FF = 2816
FT = FF // P
NB = FT // 2
EPS = 1e-5
LAM_INIT = 0.8 - 0.6 * math.exp(-0.3 * 0)
BIG = -1e30
RT = 9
ROWS = [P] * 8 + [DEC]
CHUNKS = [(0, 364), (364, 364), (728, 360)]
EXT = SEQ + DEC + 4
UEXT = HIST + SEQ + HIST + DEC
U_S = HIST + SEQ + HIST

P_TILES = 7
P_NA0, P_NA1, P_NF0, P_NF1, P_NFIN, P_BIN, P_PS, P_SUB, P_ROWS6 = 0, 8, 16, 24, 32, 40, 50, 54, 55


def build(nc, io):
    ctx = ExitStack()
    with ctx:

        base = (nc.sbuf_base + 31) // 32 * 32
        RA = base
        RSZ = 71936
        R0 = RA + KT * R * 4
        R1 = R0 + RSZ
        RW = R1 + RSZ
        RK = RW + 26624
        RM = RK + 5120

        def at(name, off, shape, dt=F32):
            return nc.alloc_sbuf_tensor_at(name, shape, dt, offset=off)

        H = at("resid", RA, [P, KT, R])
        cos_e = at("cos_e", RA, [P, R])
        sin_e = at("sin_e", RA + 4352, [P, R])
        z_e = at("z_e", RA + 2 * 4352, [P, R])
        zs_e = at("zs_e", RA + 3 * 4352, [P, R])
        vz_e = at("vz_e", RA + 4 * 4352, [P, R])
        sumB = at("sumB", RA + 5 * 4352, [P, UEXT])
        sumA = at("sumA", RA + 5 * 4352 + 4480, [P, UEXT])

        def region_x(tag, off):
            return at(f"xhi{tag}", off, [P, KT, R], F32R), at(f"xlo{tag}", off + KT * R * 4, [P, KT, R], F32R)

        xn0, xn1 = region_x("0", R0), region_x("1", R1)
        xnat = at("xnat", R1, [P, RT, D])
        junk = at("junk", R1 + 36864, [P, D])
        pnat = at("pnat", R1 + 36864 + 4096, [P, P_TILES, P])
        hnat = at("hnat", R1 + 36864 + 4096 + 3584, [HIST, A_W])
        qT = at("qT", R1, [P, A_H, R])
        kT = at("kT", R1 + 17408, [P, A_H, R])
        vN = at("vN", R1 + 34816, [P, RT, A_W])
        uT = at("uT", R1 + 53248, [P, 4, UEXT])
        E = at("E", R0, [P, 2, 2, 1024])
        comb = at("comb", R0 + 34816, [P, 2, 1024])
        AT = at("AT", R0 + 34816 + 8192, [P, 2, 1024])
        oN = at("oN", RW + 8192, [P, RT, A_H, P])
        kcn = at("kcn", RW, [P, 2, A_W])
        vcn = at("vcn", RW + 4096, [P, 2, A_W])
        kNat = at("kNat", RK, [P, RT, P])
        kAll = at("kAll", RK, [P, A_H, PAST + DEC])
        acc = at("acc", RK, [P, R])
        kc2n = at("kc2n", RK, [P, P])
        wraw = at("wraw", RW, [P, 2, KT, P])
        whi = at("whi", RW + 8192, [P, 2, KT, P], F32R)
        wlo = at("wlo", RW + 8192 + 8192, [P, 2, KT, P], F32R)
        whi_op = [at("whi_op0", R1 + 53248, [P, 2, KT, P], F32R), at("whi_op1", R0 + 48128, [P, 2, KT, P], F32R)]
        wlo_op = [at("wlo_op0", R1 + 61440, [P, 2, KT, P], F32R), at("wlo_op1", R0 + 56320, [P, 2, KT, P], F32R)]
        graw = at("graw", RW, [P, KT, 2 * P])
        vraw = at("vraw", RW + 8192, [P, KT, 2 * P])
        draw = at("draw", RW + 16384, [P, 2, D])

        class FfnBuffers:
            def __init__(self, tag, off):
                self.hhi = at(f"hhi{tag}", off, [P, 2, R], F32R)
                self.hlo = at(f"hlo{tag}", off + 8704, [P, 2, R], F32R)
                o = off + 17408
                self.uphi = at(f"uphi{tag}", o, [P, 2, KT, P], F32R)
                self.uplo = at(f"uplo{tag}", o + 8192, [P, 2, KT, P], F32R)
                o += 16384
                self.dhi = at(f"dhi{tag}", o, [P, 2, D], F32R)
                self.dlo = at(f"dlo{tag}", o + 8192, [P, 2, D], F32R)
                o += 16384
                self.ext = at(f"ext{tag}", o, [P, 2, EXT])
                o += 2 * EXT * 4
                self.c = at(f"c{tag}", o, [P, 2, EXT - 2])
        ffn_buf = [FfnBuffers("_f0", R0), FfnBuffers("_f1", R1)]
        q2T = at("q2T", R0, [P, KT, R])
        kd = at("kd", R0 + 34816, [P, C_KV, R])
        v2N = at("v2N", R0 + 43520, [P, RT, P])
        o = R0 + 48128
        cos_o, sin_o = at("cos_o", o, [P, R]), at("sin_o", o + 4352, [P, R])
        z_o, zs_o = at("z_o", o + 8704, [P, R]), at("zs_o", o + 13056, [P, R])
        vz_o = at("vz_o", o + 17408, [P, R])
        k_o = at("k_o", R0 + 7 * R * 4, [P, R])
        E2 = at("E2", RW + 8192, [P, 2, 4, 256])
        PT2 = at("PT2", RW + 16384, [P, 2, 2, 4, P])
        oN2 = at("oN2", o + 16384, [P, D])
        o += 21760
        kds = at("kds", o, [P, C_KV, C_CACHE + DEC])
        vc2 = at("vc2", o + 1536, [P, P])
        yN = at("yN", R0, [P, RT, D])

        o = RM
        def small(name, shape, dt=F32):
            nonlocal o
            size = int(np.prod(shape[1:])) * (2 if dt == BF16 else 4)
            t = at(name, o, shape, dt)
            o += (size + 31) // 32 * 32
            return t
        dg_off = o
        dg = small("dg", [P, RT, P])
        rB = at("rB", dg_off, [P, R])
        ident = small("ident", [P, P])
        ones = small("ones", [P, P])
        par = small("par", [P, P_TILES, 88])
        s_off = o
        pwraw = small("pwraw", [P, 4, P])
        pwhi = small("pwhi", [P, 4, P], F32R)
        pwlo = small("pwlo", [P, 4, P], F32R)
        sq = at("sq", s_off, [P, R])
        ojunk = at("ojunk", s_off + 4352, [P, P])
        kn2 = at("kn2", s_off + 4352, [P, 2, P])
        maskL = small("maskL", [P, P], BF16)
        maskR = small("maskR", [P, 2, 256], BF16)
        epsT = small("epsT", [P, 1])
        ss = small("ss", [P, RT])
        std = small("std", [P, RT])
        rs = small("rs", [P, RT])
        lamp = at("lamp", R1 + 48640, [P, 4, A_DH])
        lam2 = small("lam2", [P, 4])
        neglam = small("neglam", [P, 1])
        subg = small("subg", [P, 1])
        sinkb = small("sinkb", [P, C_H])
        e_off = o
        edge = at("edge", e_off, [P, 2, 2, 2 * FT])
        rct = small("rct", [P, 4, HIST])
        ue = small("ue", [P, 4, 2, HIST])
        fix = small("fix", [P, HIST])
        nm = small("nm", [P, 2, 2])
        sums = small("sums", [P, 2, 2])
        rsum = small("rsum", [P, 4, 2])
        cc = small("cc", [P, 2])
        sso = small("sso", [P, RT, A_H])
        rso = small("rso", [P, RT, A_H])
        m2 = small("m2", [P, 2, 4]); nm2 = small("nm2", [P, 2, 4]); snk2 = small("snk2", [P, 2, 4])
        es2 = small("es2", [P, 2, 4]); sum2 = small("sum2", [P, 2, 4]); den2 = small("den2", [P, 2, 4])
        rd2 = small("rd2", [P, 2, 4])
        uout = at("uout", s_off, [HIST, 2, A_W])
        edgeN = at("edgeN", s_off + 4352, [4 * FT, 2, P])
        assert o <= nc.sbuf_usable_end, (o, nc.sbuf_usable_end)

        PS = ctx.enter_context(nc.psum_tensor("PS", [P, 8, 512], F32))

        def pieces(s, t, off=0):
            a = CHUNKS[2][0]
            return [(PS[:, 3 * s:3 * s + 2, 0:364], t[:, off:off + a].rearrange("p (c n) -> p c n", c=2)),
                    (PS[:, 3 * s + 2, 0:360], t[:, off + a:off + R])]

        def rows_of(t):
            return slice(P * t, P * t + ROWS[t])

        def param(tile, row):
            return par[:, tile, row:row + 1]

        def products(s, k, nk, wh, wl, xh, xl):
            for n, (w, x) in enumerate(((wh, xh), (wh, xl), (wl, xh))):
                for c, (a, width) in enumerate(CHUNKS):
                    last = nc.tensor.matmul(PS[:, 3 * s + c, 0:width], w, x[:, a:a + width],
                                            start=(k == 0 and n == 0), stop=(k == nk - 1 and n == 2))
            return last

        made = {}

        def S(name):
            if name not in made:
                made[name] = ctx.enter_context(nc.semaphore(name))
            return made[name]

        LAYER_COUNT = {"in_raw0": 128, "in_raw1": 128, "in_hi": 16, "in_lo": 16, "in_mm": 16, "in_ev": 16,
                       "in_rope": 8, "in_rz": 8, "in_sw": 8, "op_raw0": 64, "op_raw1": 64, "op_hi": 8, "op_lo": 8, "op_mm": 8, "op_mid": 8,
                       "ff_graw": 16 * NB, "ff_vraw": 16 * NB, "ff_draw": 16 * NB,
                       "ff_uphi": 4 * NB, "ff_uplo": 4 * NB, "ff_upmm": 4 * NB + 1,
                       "ff_dhi": NB, "ff_dlo": NB, "ff_dnmm": KT * NB, "ff_dnev": KT * (NB - 1)}
        for name in ("aext", "atap", "amid", "aconv", "ah", "ahi"):
            LAYER_COUNT["ff_" + name] = 1
        for name in ("gext", "vext", "gtap", "vtap", "gmid", "vmid", "gconv", "vconv", "silu", "h", "hhi", "hlo"):
            LAYER_COUNT["ff_" + name] = FT

        C_IDENT, C_SMALL, C_ALL = 2, 7, 17
        X_IN = [f"x_in{n}" for n in (0, 2, 2, 4, 4, 6, 6, 7, 8)]

        def reached(eng, l, name, count):
            eng.wait_ge(S(name), count + l * LAYER_COUNT[name])

        def norm_pe_stats(pe, n):
            pe.wait_ge(S("acc_done"), 8 * n)
            for t in range(RT):
                last = nc.tensor.matmul(PS[0:ROWS[t], 6, t:t + 1], acc[:, rows_of(t)], ones[:, 0:1],
                                        start=True, stop=True)
            last.then_inc(S("n_stat"), 1)

        def final_pe_stats(pe, c):
            pe.wait_ge(S("acc_done"), C_SQ + 7 * c + 7)
            pe.wait_ge(S("fin_sq"), C_SQ + 8 * c + 8)
            if c:
                pe.wait_ge(S("n_sqrt"), 4 + c)
            for t in range(3 * c, 3 * c + 3):
                nc.tensor.matmul(PS[0:ROWS[t], 6, t:t + 1], acc[:, rows_of(t)], ones[:, 0:1], start=True, stop=False)
                last = nc.tensor.matmul(PS[0:ROWS[t], 6, t:t + 1], sq[:, rows_of(t)], ones[:, 0:1], start=False, stop=True)
            last.then_inc(S("n_stat"), 1)

        BC_BANK = (7, 6, 7)

        def norm_pe_bcast(pe, n, c):
            pe.wait_ge(S("n_diag"), n + 1)
            if n == 0:
                pe.wait_ge(S("par_ev"), 4)
            if c == 2:
                pe.wait_ge(S("n_rb"), 3 * n + 1)
            flat = dg[:, :, :].rearrange("p t c -> p (t c)")
            a, width = CHUNKS[c]
            nc.tensor.matmul(PS[:, BC_BANK[c], 0:width], ones[:, :], flat[:, a:a + width],
                             start=True, stop=True).then_inc(S("n_bc"), 1)

        def norm_bcast_after(pe, n):
            def after(k):
                if k == 3:
                    norm_pe_bcast(pe, n, 0)
                    norm_pe_bcast(pe, n, 1)
                if k == 5:
                    norm_pe_bcast(pe, n, 2)
            return after

        def norm_act(act, n, src):
            nc.scalar.activation(std[:, 0:8], src[:, 0:8], ACT.Sqrt, scale=1.0 / D, bias=epsT[:, 0:1])
            nc.scalar.activation(std[0:DEC, 8:9], src[0:DEC, 8:9], ACT.Sqrt, scale=1.0 / D,
                                 bias=epsT[0:DEC, 0:1]).then_inc(S("n_sqrt"), 1)

        def norm_dve_diag(dve, n):
            dve.wait_ge(S("n_sqrt"), n + 1)
            nc.vector.reciprocal(rs[:, :], std[:, :]).then_inc(S("n_rec"), 1)
            dve.wait_ge(S("n_rec"), n + 1)
            nc.vector.tensor_tensor(dg[:, :, :], ident[:, :].unsqueeze(1).to_broadcast([P, RT, P]),
                                    rs[:, :].unsqueeze(2).to_broadcast([P, RT, P]),
                                    ALU.mult).then_inc(S("n_diag"), 1)

        def norm_dve_rb(dve, n):
            for c, (a, width) in enumerate(CHUNKS):
                dve.wait_ge(S("n_bc"), 3 * n + c + 1)
                nc.vector.tensor_copy(rB[:, a:a + width], PS[:, BC_BANK[c], 0:width]).then_inc(S("n_rb"), 1)

        def scaled_by_row(s, dst, off=0):
            for (src, d), (_, r) in zip(pieces(s, dst, off), pieces(s, rB)):
                last = nc.vector.tensor_tensor(d, src, r, ALU.mult)
            return last

        PAIRS = [(t, h) for t in (7, 6, 5, 4, 8, 3, 2, 1, 0) for h in range(A_H)]
        SAMPLE_DONE = 20
        KEYS = [(t + 1) * P for t in range(8)] + [PAST + DEC]
        BLOCKS = [[(b * P, min(P, KEYS[t] - b * P)) for b in range((KEYS[t] + P - 1) // P)] for t in range(RT)]
        FILLS = [[(f, min(4, len(BLOCKS[t]) - f)) for f in range(0, len(BLOCKS[t]), 4)] for t in range(RT)]
        FIRST_FILL = [sum(len(FILLS[t]) for t, _ in PAIRS[:p]) for p in range(len(PAIRS) + 1)]
        NP_ = len(PAIRS)

        def two_banks(p):
            return KEYS[PAIRS[p][0]] > 512

        def score_banks(p, m):
            nq, L = ROWS[PAIRS[p][0]], KEYS[PAIRS[p][0]]
            if two_banks(p):
                return PS[0:nq, 2 * m:2 * m + 2, :].rearrange("p b n -> p (b n)")[:, 0:L]
            return PS[0:nq, 2 * m + p % 2, 0:L]

        BATCHES = [(t, b) for t in range(RT) for b in range(4)]
        WIN = [(P, 256)] + [(0, 256)] * 7 + [(0, C_CACHE + DEC)]
        NQ = len(BATCHES)

        def key_tiles(t):
            return [kt for kt in range(2) if WIN[t][0] < (kt + 1) * P]
        OFILL = [sum(len(key_tiles(t)) for t, _ in BATCHES[:q]) for q in range(NQ + 1)]

        OUTP = [dict(x=xn0, y=xn1, w=io["w_out_even"][0], gain=P_NF0, n=1, l=0, tag="op", ks=[4, 5, 6, 7, 0, 1, 2, 3]),
                dict(x=xn1, y=xn0, w=io["w_out_odd"][0], gain=P_NF1, n=3, l=1, tag="op", ks=[4, 5, 6, 7, 0, 1, 2, 3])]
        FFN = [dict(x=xn1, y=xn1, gain=P_NA1, n=1, tag="ff", b=ffn_buf[0], l=0),
               dict(x=xn0, y=None, gain=P_NFIN, n=3, tag="ff", b=ffn_buf[1], l=1)]

        POOL_ORDER = (1, 2, 3, 0)

        def pool_hi(act, identity, n):
            g = POOL_ORDER[n]
            act.wait_ge(S("pm_mm"), n + 1)
            for src, dst in pieces(n % 2, xn0[0][:, 4 + g, :]):
                last = identity(dst, src, scale=param(6, P_PS + g))
            last.then_inc(S("pm_hi"), 1)

        def row_fill(f):
            j = f % 3
            return f // 6, f % 6 >= 3, 4 * j, 1 if j == 2 else 4

        def row_fills_after(u):
            g, kind = u // 4, u % 4
            if kind == 3:
                return (6 * g, 6 * g + 1)
            return (6 * g - 4 + 2 * kind, 6 * g - 3 + 2 * kind) if g >= 1 and kind < 2 else ()

        PARTS = ((slice(0, 728), slice(0, 724)), (slice(728, EXT - 2), slice(724, R)))

        Y_CHUNKS = [(0, 384), (384, 384), (768, 320)]
        Y_STATS = {(1, 3): 0, (2, 3): 1}
        Y_FILLS = {(2, 2 + n): n for n in range(6)}
        Y_BANKS = (4, 5, 7)
        STEPS_Y = [(c, k) for c in range(3) for k in range(KT)]
        C_SQ = 24

        def y_bank(c, k):
            return k % 6 if c == 0 else k % 4

        def y_free(c, k):
            i = STEPS_Y.index((c, k))
            before = [n for n, ck in enumerate(STEPS_Y[:i]) if y_bank(*ck) == y_bank(c, k)]
            return before[-1] + 1 if before else 0

        def ffn_sq(f, k):
            return sq[:, :] if k % 2 else f["b"].c[:, 0, 0:R]

        def finish_tile(act, identity, k, x, gain, sq_at):
            h = H[:, bass.ds(k, 1), :]
            identity(x[0][:, bass.ds(k, 1), :], h, scale=par[:, 6, bass.ds(k + gain, 1)]).then_inc(S("fin_hi"), 1)
            nc.scalar.activation(sq_at.unsqueeze(1), h, ACT.Square).then_inc(S("fin_sq"), 1)

        def odd_rows_hi(act, f):
            t, j = f // 2, f % 2
            nr = ROWS[t]
            act.wait_ge(S("om_tr"), f + 1)
            nc.scalar.copy(xn1[0][:, 4 * j:4 * j + 4, P * t:P * t + nr],
                           PS[:, 7, :].rearrange("p (k r) -> p k r", k=4)[:, :, 0:nr]).then_inc(S("om_hi"), 1)

        STEPS = NQ + 4

        def rows_step(q):
            return (q - 4) // 2 if q >= 4 and q % 2 == 0 and (q - 4) // 2 < 2 * RT else None

        block = ctx.enter_context(nc.Block())


        @block.sync
        def _(sp):
            def x_tile(t):
                if t == 8:
                    sp.dma_start(xnat[0:DEC, t, :], io["x_sample"][0]).then_inc(S("x_in8"), 16)
                else:
                    t0 = max(t - 1, 0)
                    sp.dma_start(xnat[:, t0:t + 1, :], io["x_prompt"][0].rearrange("(t p) d -> p t d", p=P)[:, t0:t + 1, :]) \
                        .then_inc(S(f"x_in{t}"), 16)

            def par_rows(tile, row, src):
                n = src.shape[0]
                sp.dma_start(pnat[row:row + n, tile, :], src).then_inc(S("gain_in" if tile == 6 else "par_in"), 16)

            x_tile(0)
            x_tile(2)

            def even_in_weight(u):
                col = (u + 3) % 4 * A_W + (u // 4) * P
                if u >= 2:
                    reached(sp, 0, "in_lo", u - 1)
                sp.dma_start(wraw[:, u % 2], io["w_in_even"][0].rearrange("(k p) n -> p k n", p=P)[:, :, col:col + P]) \
                    .then_inc(S(f"in_raw{u % 2}"), 16)
            even_in_weight(0)
            par_rows(6, P_NA0, io["norm_attn"].rearrange("i (t c) -> (i t) c", c=P))
            par_rows(6, P_NF0, io["norm_ffn"].rearrange("i (t c) -> (i t) c", c=P))
            par_rows(6, P_NFIN, io["norm_final"].rearrange("(t c) -> t c", c=P))
            par_rows(6, P_BIN, io["b_in_odd"][0].rearrange("(t c) -> t c", c=P))
            par_rows(6, P_PS, io["pool_scale"][0].rearrange("(t c) -> t c", c=P))
            par_rows(6, P_SUB, io["diff_subln"])
            sp.dma_start(hnat[:, :], io["state_pool"][0, 0]).then_inc(S("gain_in"), 16)
            x_tile(4)
            x_tile(6)
            sp.dma_start(xnat[:, 7, :], io["x_prompt"][0, 7 * P:8 * P, :]).then_inc(S("x_in7"), 16)
            x_tile(8)
            even_in_weight(1)
            for l in range(2):
                par_rows(3 * l, 0, io["conv_w"][l, 0:2].rearrange("i (t c) -> (i t) c", c=P))
                par_rows(3 * l + 1, 0, io["conv_w"][l, 2:3].rearrange("i (t c) -> (i t) c", c=P))
                par_rows(3 * l + 1, 44, io["conv_b"][l:l + 1].rearrange("i (t c) -> (i t) c", c=P))
                par_rows(3 * l + 2, 0, io["state_ffn_conv"][l, 0].rearrange("i (t c) -> (i t) c", c=P))
            for c in range(4):
                sp.dma_start(cos_e[32 * c:32 * c + 32, :], io["cos_t"]).then_inc(S("tab_in"), 16)
            for c in range(2):
                sp.dma_start(sin_e[64 * c:64 * c + 64, :], io["sin_t"]).then_inc(S("tab_in"), 16)
            sp.dma_start(pwraw[:, :, :], io["pool_w"][0].rearrange("g c d -> c g d")).then_inc(S("pw_in"), 16)
            sp.dma_start(rct[:, :, :].rearrange("p g t -> p (g t)"), io["rcnt_t"].partition_broadcast(P)).then_inc(S("bc_in"), 16)
            sp.dma_start(lamp[:, :, :].rearrange("p a b -> p (a b)"),
                         io["diff_lambda"][0].rearrange("a b -> (a b)").partition_broadcast(P)).then_inc(S("bc_in"), 16)
            sp.dma_start(sinkb[:, :], io["sinks"][0].partition_broadcast(P)).then_inc(S("bc_in"), 16)
            for u in range(2, 16):
                even_in_weight(u)
            reached(sp, 0, "in_lo", 16)
            sp.dma_start(kcn[:, :, :], io["cache_diff_k"][0, 0].rearrange("(b p) h m d -> p b (h m d)", p=P)).then_inc(S("kc_in"), 16)
            sp.dma_start(vcn[:, :, :], io["cache_diff_v"][0, 0].rearrange("(b p) h e -> p b (h e)", p=P)).then_inc(S("vc_in"), 16)
            sp.wait_ge(S("ei_tev"), 24)
            sp.dma_start(io["diff_v_prompt"][0, 0].rearrange("(t p) h e -> p t (h e)", p=P), vN[:, 0:8, :]).then_inc(S("st_v"), 16)
            sp.dma_start(io["diff_v_sample"][0, 0].rearrange("s h e -> s (h e)"), vN[0:DEC, 8, :]).then_inc(S("st_v"), 16)
            sp.dma_start(io["swa_k_sample"][0, 0, 0:64], io["cache_swa_k"][0, 0, 64:128]).then_inc(S("st_y"), 16)
            sp.dma_start(io["swa_v_sample"][0, 0, 0:64], io["cache_swa_v"][0, 0, 64:128]).then_inc(S("st_y"), 16)

            def out_weights(o):
                t, l = o["tag"], o["l"]
                src = o["w"].rearrange("(k p) n -> p k n", p=P)
                for u in range(2):
                    if l == 0:
                        sp.wait_ge(S("kc_ev") if u == 0 else S("at_pv"), 3 if u == 0 else SAMPLE_DONE)
                    else:
                        reached(sp, 1, "in_lo", 9 + u)
                    sp.dma_start(wraw[:, u], src[:, :, u * P:(u + 1) * P]).then_inc(S(f"{t}_raw{u}"), 16)
                with sp.Fori(1, 4) as j:
                    for s in range(2):
                        col = sp.snap(j * 256 + s * P)
                        reached(sp, l, f"{t}_lo", 2 * j + s - 1)
                        sp.dma_start(wraw[:, s], src[:, :, bass.ds(col, P)]).then_inc(S(f"{t}_raw{s}"), 16)

            def ffn_weights(f):
                t, l, b = f["tag"], f["l"], f["b"]
                up = io["w_up"][l].rearrange("(k p) n -> p k n", p=P)
                down = io["w_down"][l].rearrange("(f p) n -> p f n", p=P)
                reached(sp, l, "op_lo", 8)
                sp.dma_start(graw[:, :, :], up[:, :, 0:256]).then_inc(S(f"{t}_graw"), 16)
                reached(sp, l, "op_mm", 8)
                sp.dma_start(vraw[:, :, :], up[:, :, FF:FF + 256]).then_inc(S(f"{t}_vraw"), 16)
                sp.dma_start(draw[:, :, :], down[:, 0:2, :]).then_inc(S(f"{t}_draw"), 16)
                with sp.Fori(1, NB) as i:
                    g_col = sp.snap(i * 256)
                    v_col = sp.snap(i * 256 + FF)
                    d_tile = sp.snap(i * 2)
                    reached(sp, l, f"{t}_uplo", 4 * i - 1)
                    sp.dma_start(graw[:, :, :], up[:, :, bass.ds(g_col, 256)]).then_inc(S(f"{t}_graw"), 16)
                    reached(sp, l, f"{t}_dlo", i)
                    sp.dma_start(draw[:, :, :], down[:, bass.ds(d_tile, 2), :]).then_inc(S(f"{t}_draw"), 16)
                    reached(sp, l, f"{t}_uplo", 4 * i)
                    sp.dma_start(vraw[:, :, :], up[:, :, bass.ds(v_col, 256)]).then_inc(S(f"{t}_vraw"), 16)

            out_weights(OUTP[0])
            ffn_weights(FFN[0])

            src = io["w_in_odd"][0].rearrange("(k p) n -> p k n", p=P)
            for u in range(2):
                sp.wait_ge(S("ff_uplo"), 4 * NB - 1)
                sp.dma_start(wraw[:, u], src[:, :, D + u * P:D + (u + 1) * P]).then_inc(S(f"in_raw{u}"), 16)
            sp.wait_ge(S("fin_h"), 16)
            sp.wait_ge(S("acc_done"), 16)
            for c in range(4):
                sp.dma_start(cos_o[32 * c:32 * c + 32, :], io["cos_t"]).then_inc(S("tab_in"), 16)
            for c in range(2):
                sp.dma_start(sin_o[64 * c:64 * c + 64, :], io["sin_t"]).then_inc(S("tab_in"), 16)
            sp.dma_start(vc2[:, :], io["cache_swa_v"][0, 0].rearrange("s g d -> s (g d)")).then_inc(S("vc_in"), 16)
            sp.wait_ge(S("n_stat"), 2)
            sp.dma_start(kc2n[:, :], io["cache_swa_k"][0, 0].rearrange("s g d -> s (g d)")).then_inc(S("kc_in"), 16)
            with sp.Fori(1, 5) as j:
                for s in range(2):
                    col = sp.snap(j * 256 + (s - 2) * P)
                    reached(sp, 1, "in_lo", 2 * j + s - 1)
                    sp.dma_start(wraw[:, s], src[:, :, bass.ds(col, P)]).then_inc(S(f"in_raw{s}"), 16)
            sp.wait_ge(S("oi_kn"), 2)
            sp.dma_start(io["swa_k_prompt"][0, 0].rearrange("s g d -> s (g d)"), kn2[:, 0, :]).then_inc(S("st_k2"), 16)
            sp.dma_start(io["swa_k_sample"][0, 0, 64:128].rearrange("s g d -> s (g d)"), kn2[0:DEC, 1, :]).then_inc(S("st_k2"), 16)
            sp.wait_ge(S("oi_vn"), 3)
            sp.dma_start(io["swa_v_prompt"][0, 0].rearrange("s g d -> s (g d)"), v2N[:, 7, :]).then_inc(S("st_v2"), 16)
            sp.dma_start(io["swa_v_sample"][0, 0, 64:128].rearrange("s g d -> s (g d)"), v2N[0:DEC, 8, :]).then_inc(S("st_v2"), 16)

            out_weights(OUTP[1])
            ffn_weights(FFN[1])

            for t in range(RT):
                sp.wait_ge(S("y_act"), t + 1)
                sp.wait_ge(S("y_dve"), t + 1)
                dst = io["y_prompt"][0, t * P:(t + 1) * P, :] if t < 8 else io["y_sample"][0]
                sp.dma_start(dst, yN[0:ROWS[t], t, :]).then_inc(S("st_y"), 16)
            for name, n in (("st_v", 2), ("st_k2", 2), ("st_v2", 2), ("st_y", RT + 2),
                            ("st_k", 8), ("st_u", 2), ("st_e", 4)):
                sp.wait_ge(S(name), 16 * n)

        @block.gpsimd
        def _(pool):
            made_ = [0]

            def constant(ins):
                made_[0] += 1
                ins.then_inc(S("c_set"), 1)
                pool.wait_ge(S("c_set"), made_[0])

            constant(nc.gpsimd.memset(ident[:, :], 0.0))
            constant(nc.gpsimd.affine_select(out=ident[:, :], in_=ident[:, :], compare_op=ALU.not_equal, fill=1.0,
                                             base=0, pattern=[[-1, P]], channel_multiplier=1))
            for tile, value in ((ones[:, :], 1.0), (epsT[:, :], EPS), (std[:, :], 1.0), (sso[:, :, :], 0.0),
                                (uT[:, :, 0:HIST], 0.0), (maskL[:, :], 0.0), (maskR[:, :, :], 0.0)):
                constant(nc.gpsimd.memset(tile, value))
            for half in (0, 64):
                constant(nc.gpsimd.memset(maskL[half:half + 1, 0:64], 1.0))
                constant(nc.gpsimd.memset(maskL[half + 32:half + 33, 64:128], 1.0))
                constant(nc.gpsimd.memset(maskR[half:half + 1, :, 192:256], BIG))
                constant(nc.gpsimd.memset(maskR[half + 32:half + 33, :, 0:64], BIG))

            gain = par[:, 6, P_NA0:P_NA0 + KT].unsqueeze(2).to_broadcast([P, KT, P])

            def even_gain(u):
                reached(pool, 0, f"in_raw{u % 2}", 16 * (u // 2 + 1))
                if u == 0:
                    pool.wait_ge(S("par_ev"), 1)
                w = wraw[:, u % 2]
                nc.gpsimd.tensor_tensor(w, w, gain, ALU.mult).then_inc(S("ei_gam"), 1)
                pool.wait_ge(S("ei_gam"), u + 1)

            chain = [0]

            def step(ins):
                chain[0] += 1
                ins.then_inc(S("pl"), 1)
                pool.wait_ge(S("pl"), chain[0])

            def window_mean(g):
                pool.wait_ge(S("ei_ue"), g + 1)
                u, bufs = uT[:, g, :], [sumA, sumB]
                cur = u
                for l in range(g + 1):
                    sh, st, dst = 1 << l, (2 << l) - 1, bufs[l % 2]
                    step(nc.gpsimd.tensor_tensor(dst[:, st:UEXT], cur[:, st:UEXT], cur[:, st - sh:UEXT - sh], ALU.add))
                    cur = dst
                if g == 0:
                    pool.wait_ge(S("bc_in"), 48)
                step(nc.gpsimd.tensor_tensor(fix[:, :], cur[:, HIST:2 * HIST], rct[:, g, :], ALU.mult))
                step(nc.gpsimd.tensor_scalar(cur[:, HIST:UEXT], cur[:, HIST:UEXT], 1.0 / WINDOWS[g], None, ALU.mult))
                step(nc.gpsimd.tensor_copy(cur[:, HIST:2 * HIST], fix[:, :]))
                nc.gpsimd.tensor_tensor(u[:, HIST:UEXT], cur[:, HIST:UEXT], u[:, HIST:UEXT], ALU.subtract).then_inc(S("pooled"), 1)
                pool.wait_ge(S("pooled"), g + 1)

            even_gain(0)
            even_gain(1)
            for u in range(2, 16):
                even_gain(u)
                if u % 4 == 3:
                    window_mean(u // 4)
            pool.wait_ge(S("pooled"), 4)
            for n, k in enumerate((5, 6, 7, 0, 1)):
                if k == 0:
                    reached(pool, 0, "in_rope", 8)
                nc.gpsimd.tensor_tensor(H[:, k, :], xn0[0][:, k, :].bitcast(F32), xn0[1][:, k, :].bitcast(F32),
                                        ALU.add).then_inc(S("h_pool"), 1)
                pool.wait_ge(S("h_pool"), n + 1)
            def clear_squares(n):
                pool.wait_ge(S("n_stat"), n)
                nc.gpsimd.memset(acc[:, :], 0.0).then_inc(S("acc_zero"), 1)
                pool.wait_ge(S("acc_zero"), n + 1)

            def ffn_squares(f):
                clear_squares(f["n"])
                for k in range(KT):
                    c = 8 * f["n"] + k
                    pool.wait_ge(S("fin_sq"), c + 1)
                    if k:
                        pool.wait_ge(S("acc_done"), c)
                    nc.gpsimd.tensor_tensor(acc[:, :], acc[:, :], ffn_sq(f, k), ALU.add).then_inc(S("acc_done"), 1)

            def final_squares():
                clear_squares(3)
                for c, (a, w) in enumerate(Y_CHUNKS):
                    for k in range(KT - 1):
                        pool.wait_ge(S("fin_sq"), C_SQ + 8 * c + k + 1)
                        if c or k:
                            pool.wait_ge(S("acc_done"), C_SQ + 7 * c + k)
                        nc.gpsimd.tensor_tensor(acc[:, a:a + w], acc[:, a:a + w], ffn_sq(FFN[1], k)[:, a:a + w],
                                                ALU.add).then_inc(S("acc_done"), 1)

            pool.wait_ge(S("so_rec"), 1)
            for t in range(RT):
                if t % 3:
                    nr = ROWS[t]
                    nc.gpsimd.tensor_tensor(oN[0:nr, t], oN[0:nr, t], rso[0:nr, t, :].unsqueeze(2).to_broadcast([nr, A_H, P]),
                                            ALU.mult).then_inc(S("so_n_pool"), 1)
            pool.wait_ge(S("at_pv"), NP_)
            nc.gpsimd.memset(acc[:, :], 0.0).then_inc(S("acc_zero"), 1)
            ffn_squares(FFN[0])
            pool.wait_ge(S("n_stat"), 2)
            pool.wait_ge(S("kc2_tr"), 1)
            nc.gpsimd.memset(acc[:, :], 0.0).then_inc(S("acc_zero"), 1)
            final_squares()

        @block.scalar
        def _(act):
            def identity(dst, src, scale=1.0, bias=0.0):
                return nc.scalar.activation(dst, src, ACT.Identity, scale=scale, bias=bias)

            act.wait_ge(S("c_set"), C_SMALL)

            def even_hi(u):
                act.wait_ge(S("ei_gam"), u + 1)
                if u >= 2:
                    reached(act, 0, "in_mm", u - 1)
                nc.scalar.copy(whi[:, u % 2], wraw[:, u % 2]).then_inc(S("in_hi"), 1)

            def gains_out():
                act.wait_ge(S("par_tr"), 1)
                nc.scalar.copy(par[:, 6, 0:P_ROWS6], PS[:, 7, 176:176 + P_ROWS6]).then_inc(S("par_ev"), 1)
                nc.scalar.copy(uT[:, :, HIST + SEQ:U_S], PS[:, 7, 240:300].rearrange("p (g r) -> p g r", r=HIST)) \
                    .then_inc(S("par_ev"), 1)

            def params_out():
                act.wait_ge(S("par_tr"), 2)
                nc.scalar.copy(par[:, 0:4, :], PS[:, 6, 0:352].rearrange("p (a b) -> p a b", b=88)).then_inc(S("par_ev"), 1)
                act.wait_ge(S("par_tr"), 3)
                nc.scalar.copy(par[:, 4:6, :], PS[:, 7, 0:176].rearrange("p (a b) -> p a b", b=88)).then_inc(S("par_ev"), 1)

            for t in range(RT):
                nr = ROWS[t]
                for j in range(2):
                    f = 2 * t + j
                    act.wait_ge(S("x_tr"), f + 1)
                    nc.scalar.copy(xn0[0][:, 4 * j:4 * j + 4, P * t:P * t + nr],
                                   PS[:, 3 + f % 3, :].rearrange("p (k r) -> p k r", k=4)[:, :, 0:nr]).then_inc(S("x_hi"), 1)
                if t >= 1:
                    act.wait_ge(S("x_sq"), t)
                nc.scalar.activation(junk[0:nr, :], xnat[0:nr, t, :], ACT.Square,
                                     accum_out=ss[0:nr, t:t + 1]).then_inc(S("x_sq"), 1)
                if t == 2:
                    gains_out()
                if t == 4:
                    even_hi(0)
            even_hi(1)
            act.wait_ge(S("x_sq"), RT)
            norm_act(act, 0, ss[:, :])
            params_out()
            act.wait_ge(S("pw_in"), 16)
            nc.scalar.copy(pwhi[:, :, :], pwraw[:, :, :]).then_inc(S("pw_hi"), 1)

            def natural(f):
                g, is_v, a, n = row_fill(f)
                nr = ROWS[a]
                dst = vN[:, :, g * P:(g + 1) * P] if is_v else kNat
                if not is_v and a == 0 and g >= 1:
                    act.wait_ge(S("st_k"), 32 * g)
                act.wait_ge(S("ei_tr"), f + 1)
                nc.scalar.copy(dst[0:nr, a:a + n, :],
                               PS[0:nr, 6 + f % 2, 0:n * P].rearrange("p (t c) -> p t c", c=P)).then_inc(S("ei_tev"), 1)
                if not is_v and a == 8:
                    act.wait_ge(S("ei_tev"), f + 1)
                    act.dma_start(io["diff_k_prompt"][0, 0].rearrange("(t p) h m d -> p t h (m d)", p=P)[:, :, g, :],
                                  kNat[:, 0:8, :]).then_inc(S("st_k"), 16)
                    act.dma_start(io["diff_k_sample"][0, 0].rearrange("s h m d -> s h (m d)")[:, g, :],
                                  kNat[0:DEC, 8, :]).then_inc(S("st_k"), 16)

            ropes = 0
            for u in range(16):
                g, kind = u // 4, u % 4
                if u + 2 < 16:
                    even_hi(u + 2)
                reached(act, 0, "in_ev", u + 1)
                if kind in (1, 2):
                    if ropes:
                        reached(act, 0, "in_rope", ropes)
                    for c in range(4):
                        last = nc.scalar.copy(zs_e[32 * c:32 * c + 32, :], z_e[32 * (c ^ 1):32 * (c ^ 1) + 32, :])
                    last.then_inc(S("in_sw"), 1)
                    ropes += 1
                if kind == 0:
                    nc.scalar.copy(ue[:, g, 0, :], uT[:, g, SEQ:SEQ + HIST])
                    nc.scalar.copy(ue[:, g, 1, :], uT[:, g, UEXT - HIST:UEXT]).then_inc(S("ei_ue"), 1)
                for f in row_fills_after(u):
                    natural(f)

            def pooled_hi(n):
                g = POOL_ORDER[n]
                phi = xn0[0][:, 4 + g, :]
                if n == 0:
                    reached(act, 0, "in_mm", 16)
                    act.wait_ge(S("h_pool"), 5)
                    act.wait_ge(S("pooled"), 4)
                if g == 0:
                    act.wait_ge(S("h_dve"), 1)
                nc.scalar.copy(phi[:, 0:SEQ], uT[:, g, HIST:HIST + SEQ])
                nc.scalar.copy(phi[:, SEQ:R], uT[:, g, U_S:UEXT]).then_inc(S("pm_phi"), 1)

            pooled_hi(0)
            for f in range(20, 24):
                natural(f)
            pooled_hi(1)
            pooled_hi(2)
            pool_hi(act, identity, 0)
            pooled_hi(3)
            for n in range(1, 4):
                pool_hi(act, identity, n)
            act.wait_ge(S("lam"), 2)
            nc.scalar.activation(lam2[:, 2:4], lam2[:, 0:2], ACT.Exp).then_inc(S("lam_exp"), 1)
            act.wait_ge(S("ue_tr"), 1)
            for st in range(2):
                last = nc.scalar.copy(uout[:, st, :], PS[0:HIST, 6 + st, :])
            last.then_inc(S("ue_ev"), 1)
            act.wait_ge(S("ue_ev"), 1)
            act.dma_start(io["pool_prompt"][0, 0], uout[:, 0, :]).then_inc(S("st_u"), 16)
            act.dma_start(io["pool_sample"][0, 0], uout[:, 1, :]).then_inc(S("st_u"), 16)
            act.wait_ge(S("st_k"), 128)
            for b in range(2):
                act.wait_ge(S("kc_tr"), b + 1)
                nc.scalar.copy(kAll[:, :, b * P:(b + 1) * P],
                               PS[:, 4 + b, :].rearrange("p (h r) -> p h r", h=4)).then_inc(S("kc_ev"), 1)
            nc.scalar.copy(kAll[:, :, PAST:PAST + DEC], kT[:, :, SEQ:R]).then_inc(S("kc_ev"), 1)

            def op_first_hi(l, s):
                reached(act, l, f"op_raw{s}", 16)
                nc.scalar.copy(whi_op[l][:, s], wraw[:, s]).then_inc(S("op_hi"), 1)

            def exps(p):
                t, h = PAIRS[p]
                nq, L = ROWS[t], KEYS[t]
                if p >= 2:
                    act.wait_ge(S("at_comb"), p - 1)
                for m in range(2):
                    act.wait_ge(S(f"at_max{m}"), p + 1)
                    nc.scalar.activation(E[0:nq, p % 2, m, 0:L],
                                         score_banks(p, m),
                                         ACT.Exp, bias=nm[0:nq, p % 2, m:m + 1],
                                         accum_out=sums[0:nq, p % 2, m:m + 1]).then_inc(S(f"at_exp{m}"), 1)

            def probs_out(p):
                t, h = PAIRS[p]
                nq = ROWS[t]
                if p >= 2:
                    act.wait_ge(S("at_pv"), p - 1)
                for j, (f, n) in enumerate(FILLS[t]):
                    F = FIRST_FILL[p] + j
                    act.wait_ge(S("at_tr"), F + 1)
                    src = PS[:, 4 + F % 2, :].rearrange("p (b q) -> p b q", q=P)
                    dst = AT[:, p % 2, :].rearrange("p (b q) -> p b q", q=P)
                    if t < 8:
                        last = nc.scalar.copy(dst[:, f:f + n, :], src[:, 0:n, :])
                    else:
                        nc.scalar.copy(dst[:, 0:2, 0:nq], src[:, 0:2, 0:nq])
                        last = nc.scalar.copy(dst[0:DEC, 2, 0:nq], src[0:DEC, 2, 0:nq])
                    last.then_inc(S("at_tev"), 1)

            def head_out(p):
                t, h = PAIRS[p]
                nq = ROWS[t]
                act.wait_ge(S("at_pv"), p + 1)
                identity(oN[0:nq, t, h, :], PS[0:nq, 6 + p % 2, 0:P], scale=rsum[0:nq, p % 4, 0:1]).then_inc(S("at_o"), 1)
                act.wait_ge(S("at_o"), p + 1)
                if p >= 1:
                    act.wait_ge(S("at_ss"), p)
                nc.scalar.activation(ojunk[0:nq, :], oN[0:nq, t, h, :], ACT.Square,
                                     accum_out=sso[0:nq, t, h:h + 1]).then_inc(S("at_ss"), 1)

            for p in range(NP_ + 3):
                if p < NP_:
                    exps(p)
                if 1 <= p <= NP_:
                    probs_out(p - 1)
                if p >= 3:
                    head_out(p - 3)
                if p in (SAMPLE_DONE + 8, SAMPLE_DONE + 10):
                    op_first_hi(0, p // (SAMPLE_DONE + 10))
            act.wait_ge(S("at_ss"), NP_)
            nc.scalar.activation(rso[:, :, :], sso[:, :, :], ACT.Sqrt, scale=1.0 / P,
                                 bias=epsT[:, 0:1]).then_inc(S("so_sqrt"), 1)
            for t in range(RT):
                nr = ROWS[t]
                act.wait_ge(S("so_tr"), t + 1)
                identity(xn0[0][:, 0:4, P * t:P * t + nr],
                         PS[:, 4 + t % 2, :].rearrange("p (h r) -> p h r", h=4)[:, :, 0:nr],
                         scale=subg[:, 0:1]).then_inc(S("so_hi"), 1)

            def out_projection(o):
                t, l, x = o["tag"], o["l"], o["y"]

                def w_hi(u, s):
                    reached(act, l, f"{t}_raw{s}", (u - s) * 8 + 16)
                    nc.scalar.copy(whi[:, s], wraw[:, s]).then_inc(S(f"{t}_hi"), 1)

                def step(k, s, more):
                    c = 8 * (o["n"] - 1) + k
                    if more:
                        if not isinstance(k, int):
                            reached(act, l, f"{t}_mm", k + 1)
                        w_hi(k + 2, s)
                    act.wait_ge(S("fin_h"), c + 1)
                    if not isinstance(k, int) or k > 0:
                        act.wait_ge(S("acc_done"), c)
                    finish_tile(act, identity, k, x, o["gain"], sq[:, :])

                if l == 0:
                    act.wait_ge(S("so_tr"), RT)
                    act.wait_ge(S("st_v"), 32)
                    act.wait_ge(S("st_u"), 32)
                else:
                    act.wait_ge(S("st_v2"), 32)
                for s in range(2):
                    step(s, s, True)
                with act.Fori(1, 3) as j:
                    for s in range(2):
                        step(2 * j + s, s, True)
                step(6, 0, False)
                ffn_first_hi(FFN[l])
                step(7, 1, False)

            def odd_hi(u, s):
                reached(act, 1, f"in_raw{s}", (u - s) * 8 + 16)
                if isinstance(u, int) and u < 2:
                    act.wait_ge(S("ff_uplo"), 4 * NB)
                    act.wait_ge(S("ff_dlo"), NB)
                if not isinstance(u, int) or u >= 2:
                    reached(act, 1, "in_mm", u - 1)
                nc.scalar.copy(whi[:, s], wraw[:, s]).then_inc(S("in_hi"), 1)

            def ffn_first_hi(f):
                t, b, l = f["tag"], f["b"], f["l"]
                reached(act, l, f"{t}_graw", 16)
                reached(act, l, "op_mid", 8)
                nc.scalar.copy(b.uphi[:, 0], graw[:, :, 0:P]).then_inc(S(f"{t}_uphi"), 1)

            def ffn(f):
                t, b, l = f["tag"], f["b"], f["l"]

                def w_hi(s, half, raw, count, freed):
                    reached(act, l, f"{t}_{'gv'[s]}raw", count)
                    if freed is not None:
                        reached(act, l, f"{t}_upmm", freed)
                    nc.scalar.copy(b.uphi[:, s], raw[:, :, half * P:(half + 1) * P]).then_inc(S(f"{t}_uphi"), 1)

                def tap(s, T):
                    k = "gv"[s]
                    col = T + FT * s
                    reached(act, l, f"{t}_{k}ext", T + 1)
                    nc.scalar.copy(edge[:, :, :, bass.ds(col, 1)],
                                   b.ext[:, s, 960:EXT].rearrange("p (a c) -> p a c", c=66)[:, :, 64:66].unsqueeze(3))
                    identity(b.c[:, s, :], b.ext[:, s, 0:EXT - 2], scale=par[:, 3 * l, bass.ds(col, 1)],
                             bias=par[:, 3 * l + 1, bass.ds(col + 44, 1)]).then_inc(S(f"{t}_{k}tap"), 1)

                def last_tap(part):
                    cols, col = PARTS[part][0], 2 * FT - 1
                    if part == 0:
                        reached(act, l, f"{t}_aext", 1)
                    else:
                        reached(act, l, f"{t}_vext", FT)
                        nc.scalar.copy(edge[:, :, :, col:col + 1],
                                       b.ext[:, 1, 960:EXT].rearrange("p (a c) -> p a c", c=66)[:, :, 64:66].unsqueeze(3))
                    identity(b.c[:, 1, cols], b.ext[:, 1, cols], scale=par[:, 3 * l, col:col + 1],
                             bias=par[:, 3 * l + 1, col + 44:col + 45]).then_inc(S(f"{t}_{'av'[part]}tap"), 1)

                def last_h_hi(part):
                    cols = PARTS[part][1]
                    reached(act, l, f"{t}_ah" if part == 0 else f"{t}_h", 1 if part == 0 else FT)
                    nc.scalar.copy(b.hhi[:, 1, cols], b.ext[:, 1, 4:EXT][:, cols]).then_inc(S(f"{t}_ahi" if part == 0 else f"{t}_hhi"), 1)

                def silu(T):
                    reached(act, l, f"{t}_gconv", T + 1)
                    nc.scalar.activation(b.c[:, 0, :], b.c[:, 0, :], ACT.Silu).then_inc(S(f"{t}_silu"), 1)

                def h_hi(T, s):
                    reached(act, l, f"{t}_h", T + 1)
                    nc.scalar.copy(b.hhi[:, s, :], b.ext[:, 1, 4:EXT]).then_inc(S(f"{t}_hhi"), 1)

                def d_hi(i, first):
                    reached(act, l, f"{t}_draw", 16 * i + 16)
                    if not first:
                        reached(act, l, f"{t}_dnmm", 8 * i)
                    nc.scalar.copy(b.dhi[:, :, :], draw[:, :, :]).then_inc(S(f"{t}_dhi"), 1)

                def block_(i, first, last):
                    if not first:
                        tap(1, 2 * i - 1)
                        h_hi(2 * i - 1, 1)
                        w_hi(1, 0, vraw, 16 * i + 16, 4 * i)
                    tap(0, 2 * i)
                    silu(2 * i)
                    if not first:
                        w_hi(0, 1, graw, 16 * i + 16, 4 * i + 1)
                        d_hi(i, False)
                    tap(1, 2 * i)
                    w_hi(1, 1, vraw, 16 * i + 16, 4 * i + 2)
                    h_hi(2 * i, 0)
                    tap(0, 2 * i + 1)
                    silu(2 * i + 1)
                    if not last:
                        w_hi(0, 0, graw, 16 * i + 32, 4 * i + 3)
                    if first:
                        d_hi(i, True)

                def edges_out():
                    act.wait_ge(S("ed_tr"), l + 1)
                    if l == 1:
                        act.wait_ge(S("st_k2"), 32)
                    nc.scalar.copy(edgeN[:, :, :], PS[0:2 * 2 * FT, 7, 0:256].rearrange("p (a c) -> p a c", a=2)).then_inc(S("ed_ev"), 1)
                    act.wait_ge(S("ed_ev"), l + 1)
                    for a, name in enumerate(("ffn_conv_prompt", "ffn_conv_sample")):
                        act.dma_start(io[name][l, 0].rearrange("i (t c) -> (i t) c", c=P), edgeN[:, a, :]).then_inc(S("st_e"), 16)

                reached(act, l, "op_mm", 8)
                w_hi(1, 0, vraw, 16, None)
                act.wait_ge(S("n_stat"), f["n"])
                norm_act(act, f["n"], PS[:, 6, 0:RT])
                w_hi(0, 1, graw, 16, 1)
                block_(0, True, False)
                with act.Fori(1, NB - 1) as i:
                    block_(i, False, False)
                block_(NB - 1, False, True)
                last_tap(0)
                last_tap(1)
                last_h_hi(0)
                last_h_hi(1)
                if l == 0:
                    for s in range(2):
                        odd_hi(s, s)
                if l == 1:
                    edges_out()
                    return
                for k in range(KT):
                    c = 8 * f["n"] + k
                    act.wait_ge(S("fin_h"), c + 1)
                    act.wait_ge(S("acc_done"), c - 1)
                    if k == 0:
                        reached(act, l, f"{t}_upmm", 4 * NB + 1)
                    finish_tile(act, identity, k, f["y"], f["gain"], ffn_sq(f, k))
                edges_out()

            out_projection(OUTP[0])
            ffn(FFN[0])

            def swap_bias(u):
                ropes = u - 1 if not isinstance(u, int) or u else 0
                row = u - 2 + P_BIN if not isinstance(u, int) or u else P_BIN + 8
                reached(act, 1, "in_ev", u + 1)
                if not isinstance(u, int) or u >= 2:
                    reached(act, 1, "in_rope", ropes)
                for c in range(4):
                    a = 32 * (c ^ 1)
                    last = identity(zs_o[32 * c:32 * c + 32, :], z_o[a:a + 32, :], bias=par[a:a + 32, 6, bass.ds(row, 1)])
                last.then_inc(S("in_sw"), 1)

            act.wait_ge(S("n_stat"), 2)
            norm_act(act, 2, PS[:, 6, 0:RT])
            def value_rows(j, a, n, nr):
                act.wait_ge(S("oi_vtr"), j + 1)
                nc.scalar.copy(v2N[0:nr, a:a + n, :], PS[0:nr, 6 + j % 2, 0:n * P].rearrange("p (t c) -> p t c", c=P)) \
                    .then_inc(S("oi_vn"), 1)

            odd_hi(2, 0)
            swap_bias(0)
            odd_hi(3, 1)
            reached(act, 1, "in_rope", 1)
            for g in range(C_KV):
                for half in (0, 64):
                    last = nc.scalar.copy(kd[half:half + 64, g, :], k_o[64 * g:64 * g + 64, :])
            last.then_inc(S("oi_kd"), 1)
            for s in range(2):
                if s == 1:
                    act.wait_ge(S("oi_ktr"), 1)
                    act.wait_ge(S("st_e"), 32)
                    nc.scalar.copy(kn2[:, 0, :], PS[:, 6, 0:P]).then_inc(S("oi_kn"), 1)
                    nc.scalar.copy(kn2[0:DEC, 1, :], PS[0:DEC, 6, P:2 * P]).then_inc(S("oi_kn"), 1)
                    act.wait_ge(S("kc2_tr"), 1)
                    for g in range(C_KV):
                        for half in (0, 64):
                            nc.scalar.copy(kds[half:half + 64, g, 0:P], PS[64 * g:64 * g + 64, 7, 0:P])
                    act.wait_ge(S("oi_kd"), 1)
                    nc.scalar.copy(kds[:, :, P:P + DEC], kd[:, :, SEQ:R]).then_inc(S("oi_kds"), 1)
                odd_hi(s + 4, s)
                if s == 1:
                    value_rows(0, 0, 4, P)
                    value_rows(1, 4, 4, P)
                swap_bias(s + 2)
            value_rows(2, 8, 1, DEC)
            with act.Fori(2, 4) as j:
                for s in range(2):
                    odd_hi(2 * j + s + 2, s)
                    swap_bias(2 * j + s)
            swap_bias(8)

            def odd_exps(q):
                t, b = BATCHES[q]
                nq, (c0, c1), v = ROWS[t], WIN[t], q % 2
                act.wait_ge(S("o_nm"), q + 1)
                if q >= 2:
                    act.wait_ge(S("o_tr"), OFILL[q - 1])
                for i in range(4):
                    last = nc.scalar.activation(E2[0:nq, v, i, c0:c1],
                                                PS[0:nq, 2 * v + i // 2, (i % 2) * 256 + c0:(i % 2) * 256 + c1],
                                                ACT.Exp, bias=nm2[0:nq, v, i:i + 1], scale=C_DH ** -0.5,
                                                accum_out=sum2[0:nq, v, i:i + 1])
                last.then_inc(S("o_exp"), 1)
                nc.scalar.activation(es2[0:nq, v, :], snk2[0:nq, v, :], ACT.Exp).then_inc(S("o_es"), 1)

            def odd_probs_first(q):
                t, b = BATCHES[q]
                nq, v = ROWS[t], q % 2
                if key_tiles(t)[0] == 0:
                    if q >= 2:
                        act.wait_ge(S("o_pv"), q - 1)
                    act.wait_ge(S("o_tr"), OFILL[q] + 1)
                    nc.scalar.copy(PT2[:, v, 0, :, 0:nq],
                                   PS[:, 4, :].rearrange("p (i q) -> p i q", i=4)[:, :, 0:nq]).then_inc(S("o_tev0"), 1)

            for q in range(STEPS):
                if rows_step(q) is not None:
                    odd_rows_hi(act, rows_step(q))
                if 1 <= q <= NQ:
                    odd_probs_first(q - 1)
                if q < NQ:
                    odd_exps(q)
                if q == 1:
                    swap_bias(9)
                if q in (NQ - 4, NQ - 2):
                    op_first_hi(1, q // (NQ - 2))

            out_projection(OUTP[1])
            ffn(FFN[1])

            def final_root(c):
                act.wait_ge(S("n_stat"), 4 + c)
                if c < 2:
                    nc.scalar.activation(std[:, 3 * c:3 * c + 3], PS[:, 6, 3 * c:3 * c + 3], ACT.Sqrt, scale=1.0 / D,
                                         bias=epsT[:, 0:1]).then_inc(S("n_sqrt"), 1)
                else:
                    nc.scalar.activation(std[:, 6:8], PS[:, 6, 6:8], ACT.Sqrt, scale=1.0 / D, bias=epsT[:, 0:1])
                    nc.scalar.activation(std[0:DEC, 8:9], PS[0:DEC, 6, 8:9], ACT.Sqrt, scale=1.0 / D,
                                         bias=epsT[0:DEC, 0:1]).then_inc(S("n_sqrt"), 1)

            def y_even(f):
                t = f // 2
                act.wait_ge(S("n_rec"), 5 + t // 3)
                act.wait_ge(S("y_tr"), f + 1)
                identity(yN[0:ROWS[t], t, 0:512], PS[0:ROWS[t], Y_BANKS[f % 3], :], scale=rs[0:ROWS[t], t:t + 1]).then_inc(S("y_act"), 1)

            for i, (c, k) in enumerate(STEPS_Y):
                a, w = Y_CHUNKS[c]
                act.wait_ge(S("fin_h"), C_SQ + i + 1)
                act.wait_ge(S("acc_done"), C_SQ + max(7 * c + k - 1, 0) if k >= 2 else C_SQ)
                nc.scalar.activation(ffn_sq(FFN[1], k)[:, a:a + w], H[:, k, a:a + w], ACT.Square).then_inc(S("fin_sq"), 1)
                if (c, k - 2) in Y_STATS:
                    final_root(Y_STATS[c, k - 2])
                f = Y_FILLS.get((c, k))
                if f is not None and f % 2 == 0:
                    y_even(f)
            for t in range(3, RT):
                y_even(2 * t)
                if t == 3:
                    final_root(2)

        @block.vector
        def _(dve):
            tt = nc.vector.tensor_tensor

            def split_lo(dst, src, hi, scale=None):
                if scale is None:
                    return tt(dst, src, hi.bitcast(F32), ALU.subtract)
                return nc.vector.scalar_tensor_tensor(out=dst, in0=src, scalar=scale, in1=hi.bitcast(F32),
                                                      op0=ALU.mult, op1=ALU.subtract)

            def even_lo(u):
                reached(dve, 0, "in_hi", u + 1)
                split_lo(wlo[:, u % 2], wraw[:, u % 2], whi[:, u % 2]).then_inc(S("in_lo"), 1)

            for f in range(2 * RT):
                t, j = f // 2, f % 2
                nr = ROWS[t]
                dve.wait_ge(S("x_hi"), f + 1)
                cols = slice(P * t, P * t + nr)
                split_lo(xn0[1][:, 4 * j:4 * j + 4, cols], PS[:, 3 + f % 3, :].rearrange("p (k r) -> p k r", k=4)[:, :, 0:nr],
                         xn0[0][:, 4 * j:4 * j + 4, cols]).then_inc(S("x_lo"), 1)
                if f == 9:
                    even_lo(0)
            even_lo(1)
            dve.wait_ge(S("c_set"), C_IDENT)
            norm_dve_diag(dve, 0)
            dve.wait_ge(S("pw_hi"), 1)
            split_lo(pwlo[:, :, :], pwraw[:, :, :], pwhi[:, :, :]).then_inc(S("pw_lo"), 1)
            dve.wait_ge(S("bc_in"), 48)
            tt(lamp[:, 0:4:2, :], lamp[:, 0:4:2, :], lamp[:, 1:4:2, :], ALU.mult).then_inc(S("lam"), 1)
            dve.wait_ge(S("lam"), 1)
            nc.vector.tensor_reduce(lam2[:, 0:2], lamp[:, 0:4:2, :], AX_X, ALU.add).then_inc(S("lam"), 1)
            nc.vector.tensor_scalar(subg[:, :], param(6, P_SUB), 1.0 - LAM_INIT, None, ALU.mult).then_inc(S("lam"), 1)
            norm_dve_rb(dve, 0)

            def residual_again(ks):
                for k in ks:
                    last = tt(H[:, k, :], xn0[0][:, k, :].bitcast(F32), xn0[1][:, k, :].bitcast(F32), ALU.add)
                return last

            dve.wait_ge(S("n_rb"), 3)
            ropes = 0
            for u in range(16):
                g, kind, s = u // 4, u % 4, u % 2
                reached(dve, 0, "in_mm", u + 1)
                if kind in (1, 2):
                    if ropes:
                        reached(dve, 0, "in_rope", ropes)
                    last = scaled_by_row(s, z_e)
                elif kind == 3:
                    if g >= 1:
                        dve.wait_ge(S("ei_tr"), 6 * g)
                    last = scaled_by_row(s, vz_e)
                else:
                    tt(uT[:, g, HIST:HIST + 728].rearrange("p (c n) -> p c n", c=2), PS[:, 3 * s:3 * s + 2, 0:364],
                       rB[:, 0:728].rearrange("p (c n) -> p c n", c=2), ALU.mult)
                    tt(uT[:, g, HIST + 728:HIST + SEQ], PS[:, 3 * s + 2, 0:SEQ - 728], rB[:, 728:SEQ], ALU.mult)
                    last = tt(uT[:, g, U_S:UEXT], PS[:, 3 * s + 2, SEQ - 728:360], rB[:, SEQ:R], ALU.mult)
                last.then_inc(S("in_ev"), 1)
                if u + 2 < 16:
                    even_lo(u + 2)
                if kind in (1, 2):
                    if ropes == 0:
                        dve.wait_ge(S("tab_in"), 96)
                    ropes += 1
                    by = A_DH ** -0.5 if kind == 1 else 1.0
                    reached(dve, 0, "in_sw", ropes)
                    nc.vector.scalar_tensor_tensor(out=z_e[:, :], in0=z_e[:, :], scalar=by, in1=cos_e[:, :],
                                                   op0=ALU.mult, op1=ALU.mult)
                    nc.vector.scalar_tensor_tensor(out=zs_e[:, :], in0=zs_e[:, :], scalar=by, in1=sin_e[:, :],
                                                   op0=ALU.mult, op1=ALU.mult).then_inc(S("in_rz"), 1)
                    reached(dve, 0, "in_rz", ropes)
                    tt((qT if kind == 1 else kT)[:, g, :], z_e[:, :], zs_e[:, :], ALU.add).then_inc(S("in_rope"), 1)
                if u == 14:
                    reached(dve, 0, "in_rope", 8)
                    residual_again((2, 3))
            def pool_lo(n):
                g = POOL_ORDER[n]
                dve.wait_ge(S("pm_hi"), n + 1)
                for (src, dst), (_, hi) in zip(pieces(n % 2, xn0[1][:, 4 + g, :]), pieces(n % 2, xn0[0][:, 4 + g, :])):
                    last = split_lo(dst, src, hi, param(6, P_PS + g))
                last.then_inc(S("pm_ev"), 1)

            def pooled_lo(n):
                g = POOL_ORDER[n]
                dve.wait_ge(S("pm_phi"), n + 1)
                hi, lo = xn0[0][:, 4 + g, :], xn0[1][:, 4 + g, :]
                split_lo(lo[:, 0:SEQ], uT[:, g, HIST:HIST + SEQ], hi[:, 0:SEQ])
                split_lo(lo[:, SEQ:R], uT[:, g, U_S:UEXT], hi[:, SEQ:R]).then_inc(S("pm_plo"), 1)

            pooled_lo(0)
            dve.wait_ge(S("ei_tr"), 24)
            residual_again([4]).then_inc(S("h_dve"), 1)
            pooled_lo(1)
            pooled_lo(2)
            pool_lo(0)
            pooled_lo(3)
            for n in range(1, 4):
                pool_lo(n)
            dve.wait_ge(S("lam_exp"), 1)
            nc.vector.scalar_tensor_tensor(out=neglam[:, :], in0=lam2[:, 3:4], scalar=-LAM_INIT, in1=lam2[:, 2:3],
                                           op0=ALU.add, op1=ALU.subtract).then_inc(S("lam"), 1)

            def op_first_lo(l, s):
                reached(dve, l, "op_hi", s + 1)
                split_lo(wlo_op[l][:, s], wraw[:, s], whi_op[l][:, s]).then_inc(S("op_lo"), 1)

            def maxes(p, ms):
                t, h = PAIRS[p]
                nq = ROWS[t]
                for m in ms:
                    dve.wait_ge(S(f"at_s{m}"), p + 1)
                    nc.vector.tensor_reduce(nm[0:nq, p % 2, m:m + 1],
                                            score_banks(p, m),
                                            AX_X, ALU.max, negate=True).then_inc(S(f"at_max{m}"), 1)

            def combine(p):
                t, h = PAIRS[p]
                nq, L = ROWS[t], KEYS[t]
                for m in range(2):
                    dve.wait_ge(S(f"at_exp{m}"), p + 1)
                if p >= 4:
                    dve.wait_ge(S("at_o"), p - 3)
                nc.vector.reciprocal(rsum[0:nq, p % 4, :], sums[0:nq, p % 2, :]).then_inc(S("at_r"), 1)
                dve.wait_ge(S("at_r"), 2 * p + 1)
                nc.vector.tensor_scalar(cc[0:nq, p % 2:p % 2 + 1], sums[0:nq, p % 2, 0:1], rsum[0:nq, p % 4, 1:2],
                                        neglam[0:nq, :], ALU.mult, ALU.mult).then_inc(S("at_r"), 1)
                dve.wait_ge(S("at_r"), 2 * p + 2)
                if p >= 2:
                    dve.wait_ge(S("at_tr"), FIRST_FILL[p - 1])
                nc.vector.scalar_tensor_tensor(out=comb[0:nq, p % 2, 0:L], in0=E[0:nq, p % 2, 1, 0:L],
                                               scalar=cc[0:nq, p % 2:p % 2 + 1], in1=E[0:nq, p % 2, 0, 0:L],
                                               op0=ALU.mult, op1=ALU.add).then_inc(S("at_comb"), 1)

            dve.wait_ge(S("lam"), 4)
            for p in range(NP_ + 1):
                if p < NP_:
                    maxes(p, [0])
                if p >= 1:
                    combine(p - 1)
                if p < NP_:
                    maxes(p, [1])
                if p in (SAMPLE_DONE + 9, SAMPLE_DONE + 11):
                    op_first_lo(0, p // (SAMPLE_DONE + 11))
            dve.wait_ge(S("so_sqrt"), 1)
            nc.vector.reciprocal(rso[:, :, :], rso[:, :, :]).then_inc(S("so_rec"), 1)
            dve.wait_ge(S("so_rec"), 1)
            for t in range(RT + 1):
                if t < RT and t % 3 == 0:
                    nr = ROWS[t]
                    tt(oN[0:nr, t], oN[0:nr, t], rso[0:nr, t, :].unsqueeze(2).to_broadcast([nr, A_H, P]), ALU.mult) \
                        .then_inc(S("so_n"), 1)
                if t >= 1:
                    nr, cols = ROWS[t - 1], slice(P * (t - 1), P * (t - 1) + ROWS[t - 1])
                    dve.wait_ge(S("so_hi"), t)
                    split_lo(xn0[1][:, 0:4, cols], PS[:, 4 + (t - 1) % 2, :].rearrange("p (h r) -> p h r", h=4)[:, :, 0:nr],
                             xn0[0][:, 0:4, cols], subg[:, 0:1]).then_inc(S("so_lo"), 1)

            def add_residual(s, k):
                for (src, dst) in pieces(s, H[:, bass.ds(k, 1), :].rearrange("p k r -> p (k r)")):
                    last = tt(dst, src, dst, ALU.add)
                last.then_inc(S("fin_h"), 1)

            def finish_lo(k, c, x, gain):
                dve.wait_ge(S("fin_hi"), c + 1)
                split_lo(x[1][:, bass.ds(k, 1), :], H[:, bass.ds(k, 1), :], x[0][:, bass.ds(k, 1), :],
                         par[:, 6, bass.ds(k + gain, 1)]).then_inc(S("fin_lo"), 1)

            def add_squares(c):
                dve.wait_ge(S("fin_sq"), c + 1)
                if not isinstance(c, int) or c > 0:
                    dve.wait_ge(S("acc_done"), c)
                tt(acc[:, :], acc[:, :], sq[:, :], ALU.add).then_inc(S("acc_done"), 1)

            def out_projection(o):
                t, l = o["tag"], o["l"]

                def w_lo(u, s):
                    reached(dve, l, f"{t}_hi", u + 1)
                    split_lo(wlo[:, s], wraw[:, s], whi[:, s]).then_inc(S(f"{t}_lo"), 1)

                def step(k, s, more):
                    if isinstance(k, int) and k == 7:
                        ffn_first_lo(FFN[l])
                    reached(dve, l, f"{t}_mm", k + 1)
                    add_residual(s, k)
                    if more:
                        w_lo(k + 2, s)
                    finish_lo(k, 8 * (o["n"] - 1) + k, o["y"], o["gain"])
                    add_squares(8 * (o["n"] - 1) + k)

                dve.wait_ge(S("acc_zero"), o["n"])
                for s in range(2):
                    step(s, s, True)
                with dve.Fori(1, 3) as j:
                    for s in range(2):
                        step(2 * j + s, s, True)
                for s in range(2):
                    step(6 + s, s, False)

            def odd_lo(u, s):
                reached(dve, 1, "in_hi", u + 1)
                split_lo(wlo[:, s], wraw[:, s], whi[:, s]).then_inc(S("in_lo"), 1)

            def ffn_first_lo(f):
                t, b, l = f["tag"], f["b"], f["l"]
                reached(dve, l, f"{t}_uphi", 1)
                split_lo(b.uplo[:, 0], graw[:, :, 0:P], b.uphi[:, 0]).then_inc(S(f"{t}_uplo"), 1)

            def ffn(f):
                t, b, l = f["tag"], f["b"], f["l"]

                def w_lo(s, half, raw, count):
                    reached(dve, l, f"{t}_uphi", count)
                    split_lo(b.uplo[:, s], raw[:, :, half * P:(half + 1) * P], b.uphi[:, s]).then_inc(S(f"{t}_uplo"), 1)

                def extend(s, T, count, ps):
                    e = b.ext[:, s, :]
                    reached(dve, l, f"{t}_upmm", count)
                    nc.vector.tensor_copy(e[:, 2 + SEQ:4 + SEQ].unsqueeze(2),
                                          par[:, 3 * l + 2, :].rearrange("p (i t) -> p i t", i=2)[:, :, bass.ds(T + FT * s, 1)])
                    tt(e[:, 2:730].rearrange("p (c n) -> p c n", c=2), PS[:, 3 * ps:3 * ps + 2, 0:364],
                       rB[:, 0:728].rearrange("p (c n) -> p c n", c=2), ALU.mult)
                    tt(e[:, 730:2 + SEQ], PS[:, 3 * ps + 2, 0:SEQ - 728], rB[:, 728:SEQ], ALU.mult)
                    tt(e[:, 4 + SEQ:EXT], PS[:, 3 * ps + 2, SEQ - 728:360], rB[:, SEQ:R], ALU.mult) \
                        .then_inc(S(f"{t}_{'gv'[s]}ext"), 1)

                def taps(s, T):
                    k, col = "gv"[s], T + FT * s
                    e, c = b.ext[:, s, :], b.c[:, s, :]
                    reached(dve, l, f"{t}_{k}tap", T + 1)
                    nc.vector.scalar_tensor_tensor(out=c, in0=e[:, 1:EXT - 1], scalar=par[:, 3 * l, bass.ds(col + 44, 1)],
                                                   in1=c, op0=ALU.mult, op1=ALU.add).then_inc(S(f"{t}_{k}mid"), 1)
                    reached(dve, l, f"{t}_{k}mid", T + 1)
                    nc.vector.scalar_tensor_tensor(out=c, in0=e[:, 2:EXT], scalar=par[:, 3 * l + 1, bass.ds(col, 1)],
                                                   in1=c, op0=ALU.mult, op1=ALU.add).then_inc(S(f"{t}_{k}conv"), 1)

                def gate(T, s):
                    reached(dve, l, f"{t}_silu", T + 1)
                    reached(dve, l, f"{t}_vconv", T + 1)
                    h = b.ext[:, 1, 4:EXT]
                    tt(h[:, 0:SEQ], b.c[:, 0, 0:SEQ], b.c[:, 1, 0:SEQ], ALU.mult)
                    tt(h[:, SEQ:R], b.c[:, 0, SEQ + 2:EXT - 2], b.c[:, 1, SEQ + 2:EXT - 2], ALU.mult).then_inc(S(f"{t}_h"), 1)
                    reached(dve, l, f"{t}_hhi", T + 1)
                    split_lo(b.hlo[:, s, :], h, b.hhi[:, s, :]).then_inc(S(f"{t}_hlo"), 1)

                def last_extend(part):
                    e = b.ext[:, 1, :]
                    reached(dve, l, f"{t}_upmm", 4 * NB + part)
                    if part == 0:
                        nc.vector.tensor_copy(e[:, 2 + SEQ:4 + SEQ].unsqueeze(2),
                                              par[:, 3 * l + 2, :].rearrange("p (i t) -> p i t", i=2)[:, :, 2 * FT - 1:2 * FT])
                        tt(e[:, 2:730].rearrange("p (c n) -> p c n", c=2), PS[:, 3:5, 0:364],
                           rB[:, 0:728].rearrange("p (c n) -> p c n", c=2), ALU.mult).then_inc(S(f"{t}_aext"), 1)
                    else:
                        tt(e[:, 730:2 + SEQ], PS[:, 5, 0:SEQ - 728], rB[:, 728:SEQ], ALU.mult)
                        tt(e[:, 4 + SEQ:EXT], PS[:, 5, SEQ - 728:360], rB[:, SEQ:R], ALU.mult).then_inc(S(f"{t}_vext"), 1)

                def last_taps(part):
                    cols, col, k, count = PARTS[part][0], 2 * FT - 1, "av"[part], FT if part else 1
                    e, c = b.ext[:, 1, :], b.c[:, 1, cols]
                    reached(dve, l, f"{t}_{k}tap", count)
                    if part:
                        reached(dve, l, f"{t}_vext", FT)
                    nc.vector.scalar_tensor_tensor(out=c, in0=e[:, 1:EXT - 1][:, cols], scalar=par[:, 3 * l, col + 44:col + 45],
                                                   in1=c, op0=ALU.mult, op1=ALU.add).then_inc(S(f"{t}_{k}mid"), 1)
                    reached(dve, l, f"{t}_{k}mid", count)
                    nc.vector.scalar_tensor_tensor(out=c, in0=e[:, 2:EXT][:, cols], scalar=par[:, 3 * l + 1, col:col + 1],
                                                   in1=c, op0=ALU.mult, op1=ALU.add).then_inc(S(f"{t}_{k}conv"), 1)

                def last_gate(part):
                    reached(dve, l, f"{t}_silu", FT)
                    reached(dve, l, f"{t}_aconv" if part == 0 else f"{t}_vconv", 1 if part == 0 else FT)
                    h = b.ext[:, 1, 4:EXT]
                    cols = slice(PARTS[part][1].start, min(PARTS[part][1].stop, SEQ))
                    last = tt(h[:, cols], b.c[:, 0, cols], b.c[:, 1, cols], ALU.mult)
                    if part:
                        last = tt(h[:, SEQ:R], b.c[:, 0, SEQ + 2:EXT - 2], b.c[:, 1, SEQ + 2:EXT - 2], ALU.mult)
                    last.then_inc(S(f"{t}_h" if part else f"{t}_ah"), 1)

                def last_h_lo(part):
                    cols = PARTS[part][1]
                    reached(dve, l, f"{t}_hhi" if part else f"{t}_ahi", FT if part else 1)
                    last = split_lo(b.hlo[:, 1, cols], b.ext[:, 1, 4:EXT][:, cols], b.hhi[:, 1, cols])
                    if part:
                        last.then_inc(S(f"{t}_hlo"), 1)

                def d_lo(i):
                    reached(dve, l, f"{t}_dhi", i + 1)
                    split_lo(b.dlo[:, :, :], draw[:, :, :], b.dhi[:, :, :]).then_inc(S(f"{t}_dlo"), 1)

                def down(i, ks):
                    for k in ks:
                        reached(dve, l, f"{t}_dnmm", 8 * i - 7 + k)
                        for src, dst in pieces((k + 1) % 2, H[:, k, :]):
                            last = tt(dst, src, dst, ALU.add)
                        last.then_inc(S(f"{t}_dnev"), 1)

                def block_(i, first, last):
                    if not first:
                        extend(1, 2 * i - 1, 4 * i, 1)
                        taps(1, 2 * i - 1)
                        gate(2 * i - 1, 1)
                    w_lo(1, 0, vraw, 4 * i + 2)
                    if first:
                        norm_dve_diag(dve, f["n"])
                        w_lo(0, 1, graw, 3)
                        norm_dve_rb(dve, f["n"])
                        dve.wait_ge(S("n_rb"), 3 * f["n"] + 3)
                    extend(0, 2 * i, 4 * i + 1, 0)
                    if not first:
                        down(i, [0])
                    taps(0, 2 * i)
                    if not first:
                        down(i, [1, 2])
                        w_lo(0, 1, graw, 4 * i + 3)
                        down(i, range(3, KT))
                        d_lo(i)
                    extend(1, 2 * i, 4 * i + 2, 1)
                    taps(1, 2 * i)
                    w_lo(1, 1, vraw, 4 * i + 4)
                    gate(2 * i, 0)
                    extend(0, 2 * i + 1, 4 * i + 3, 0)
                    taps(0, 2 * i + 1)
                    if not last:
                        w_lo(0, 0, graw, 4 * i + 5)
                    if first:
                        d_lo(i)

                for s in range(2):
                    nc.vector.memset(b.ext[:, s, 0:2], 0.0)
                block_(0, True, False)
                with dve.Fori(1, NB - 1) as i:
                    block_(i, False, False)
                block_(NB - 1, False, True)
                last_extend(0)
                last_taps(0)
                last_extend(1)
                last_gate(0)
                last_taps(1)
                last_h_lo(0)
                last_gate(1)
                last_h_lo(1)
                if l == 0:
                    for s in range(2):
                        odd_lo(s, s)
                if l == 1:
                    return
                for k in range(KT + 1):
                    c = 8 * f["n"] + k
                    if k < KT:
                        reached(dve, l, f"{t}_dnmm", 8 * NB - 7 + k)
                        add_residual(k % 2, k)
                    if k >= 1:
                        finish_lo(k - 1, c - 1, f["y"], f["gain"])

            out_projection(OUTP[0])
            ffn(FFN[0])

            def by_head(x):
                return x.rearrange("p (j a) -> p a j", a=2)

            def quad(x):
                return x.rearrange("p (a j) -> p a j", a=2)

            def odd_max(q):
                t, b = BATCHES[q]
                nq, (c0, c1), v = ROWS[t], WIN[t], q % 2
                dve.wait_ge(S("o_s"), q + 1)
                if q >= 2:
                    dve.wait_ge(S("o_es"), q - 1)
                nc.vector.tensor_reduce(m2[0:nq, v, :],
                                        PS[0:nq, 2 * v:2 * v + 2, :].rearrange("p b (j c) -> p (b j) c", j=2)[:, :, c0:c1],
                                        AX_X, ALU.max).then_inc(S("o_m"), 1)
                dve.wait_ge(S("o_m"), 2 * q + 1)
                sink = by_head(sinkb[0:nq, 4 * b:4 * b + 4])
                nc.vector.scalar_tensor_tensor(out=quad(m2[0:nq, v, :]), in0=quad(m2[0:nq, v, :]), scalar=C_DH ** -0.5,
                                               in1=sink, op0=ALU.mult, op1=ALU.max).then_inc(S("o_m"), 1)
                dve.wait_ge(S("o_m"), 2 * q + 2)
                tt(quad(snk2[0:nq, v, :]), sink, quad(m2[0:nq, v, :]), ALU.subtract)
                nc.vector.tensor_scalar(nm2[0:nq, v, :], m2[0:nq, v, :], -1.0, None, ALU.mult).then_inc(S("o_nm"), 1)

            def odd_rope(ropes, row, out):
                b = par[:, 6, bass.ds(row, 1)]
                reached(dve, 1, "in_sw", ropes + 1)
                nc.vector.scalar_tensor_tensor(out=z_o[:, :], in0=z_o[:, :], scalar=b, in1=cos_o[:, :],
                                               op0=ALU.add, op1=ALU.mult)
                tt(zs_o[:, :], zs_o[:, :], sin_o[:, :], ALU.mult).then_inc(S("in_rz"), 1)
                reached(dve, 1, "in_rz", ropes + 1)
                tt(out, z_o[:, :].unsqueeze(1), zs_o[:, :].unsqueeze(1), ALU.add).then_inc(S("in_rope"), 1)

            def odd_queries(u, s, more):
                reached(dve, 1, "in_mm", u + 1)
                reached(dve, 1, "in_rope", u - 1)
                scaled_by_row(s, z_o).then_inc(S("in_ev"), 1)
                if more:
                    odd_lo(u + 2, s)
                if not isinstance(u, int) or u < 9:
                    query_rope(u)

            def query_rope(u):
                odd_rope(u - 1, u - 2 + P_BIN, q2T[:, bass.ds(u - 2, 1), :])

            norm_dve_diag(dve, 2)
            norm_dve_rb(dve, 2)
            dve.wait_ge(S("n_rb"), 9)
            reached(dve, 1, "in_mm", 1)
            scaled_by_row(0, z_o).then_inc(S("in_ev"), 1)
            odd_lo(2, 0)
            dve.wait_ge(S("tab_in"), 192)
            odd_rope(0, P_BIN + 8, k_o[:, :].unsqueeze(1))
            reached(dve, 1, "in_mm", 2)
            scaled_by_row(1, vz_o).then_inc(S("in_ev"), 1)
            odd_lo(3, 1)
            reached(dve, 1, "in_ev", 2)
            nc.vector.tensor_scalar(vz_o[:, :], vz_o[:, :], param(6, P_BIN + 9), None, ALU.add).then_inc(S("oi_vz"), 1)
            with dve.Fori(1, 4) as j:
                for s in range(2):
                    odd_queries(2 * j + s, s, True)
            for s in range(2):
                odd_queries(8 + s, s, False)

            def odd_den(q):
                nq, v = ROWS[BATCHES[q][0]], q % 2
                dve.wait_ge(S("o_es"), q + 1)
                dve.wait_ge(S("o_exp"), q + 1)
                tt(den2[0:nq, v, :], sum2[0:nq, v, :], es2[0:nq, v, :], ALU.add).then_inc(S("o_rd"), 1)
                dve.wait_ge(S("o_rd"), 2 * q + 1)
                nc.vector.reciprocal(rd2[0:nq, v, :], den2[0:nq, v, :]).then_inc(S("o_rd"), 1)

            def odd_out(q):
                t, b = BATCHES[q]
                nq, v = ROWS[t], q % 2
                dve.wait_ge(S("o_pv"), q + 1)
                dve.wait_ge(S("o_rd"), 2 * q + 2)
                if q == 0:
                    reached(dve, 1, "in_rope", 9)
                if b % 2 == 0 and t >= 1:
                    dve.wait_ge(S("om_tr"), 2 * t - 1 + b // 2)
                tt(oN2[0:nq, 256 * b:256 * b + 256].rearrange("p (j a d) -> p a j d", j=2, a=2),
                   PS[0:nq, 6, 0:256].rearrange("p (a j d) -> p a j d", a=2, j=2),
                   quad(rd2[0:nq, v, :]).unsqueeze(3).to_broadcast([nq, 2, 2, C_DH]), ALU.mult).then_inc(S("o_o"), 1)

            def odd_probs_last(q):
                t, b = BATCHES[q]
                nq, v = ROWS[t], q % 2
                bs = DEC if t == 8 else P
                if q >= 2:
                    dve.wait_ge(S("o_pv"), q - 1)
                dve.wait_ge(S("o_tr"), OFILL[q + 1])
                nc.vector.tensor_copy(PT2[0:bs, v, 1, :, 0:nq],
                                      PS[0:bs, 5, :].rearrange("p (i q) -> p i q", i=4)[:, :, 0:nq]).then_inc(S("o_tev1"), 1)

            def odd_rows_lo(f):
                t, j = f // 2, f % 2
                nr = ROWS[t]
                dve.wait_ge(S("om_hi"), f + 1)
                split_lo(xn1[1][:, 4 * j:4 * j + 4, P * t:P * t + nr],
                         PS[:, 7, :].rearrange("p (k r) -> p k r", k=4)[:, :, 0:nr],
                         xn1[0][:, 4 * j:4 * j + 4, P * t:P * t + nr]).then_inc(S("om_lo"), 1)

            for q in range(STEPS):
                if q < NQ:
                    odd_max(q)
                if rows_step(q) is not None:
                    odd_rows_lo(rows_step(q))
                if 1 <= q <= NQ:
                    odd_probs_last(q - 1)
                    odd_den(q - 1)
                if 2 <= q <= NQ + 1:
                    odd_out(q - 2)
                if q == 1:
                    query_rope(9)
                if q in (NQ - 3, NQ - 1):
                    op_first_lo(1, q // (NQ - 1))

            out_projection(OUTP[1])
            ffn(FFN[1])

            def final_gain(i):
                c, k = STEPS_Y[i]
                a, w = Y_CHUNKS[c]
                dve.wait_ge(S("fin_sq"), C_SQ + i + 1)
                nc.vector.tensor_scalar(H[:, k, a:a + w], H[:, k, a:a + w], param(6, P_NFIN + k), None, ALU.mult).then_inc(S("fin_g"), 1)

            def final_rstd(c):
                dve.wait_ge(S("n_sqrt"), 5 + c)
                nc.vector.reciprocal(rs[:, 3 * c:3 * c + 3], std[:, 3 * c:3 * c + 3]).then_inc(S("n_rec"), 1)

            def y_odd(f):
                t = f // 2
                dve.wait_ge(S("n_rec"), 5 + t // 3)
                dve.wait_ge(S("y_tr"), f + 1)
                nc.vector.tensor_scalar(yN[0:ROWS[t], t, 512:1024], PS[0:ROWS[t], Y_BANKS[f % 3], :],
                                        rs[0:ROWS[t], t:t + 1], None, ALU.mult).then_inc(S("y_dve"), 1)

            for i, (c, k) in enumerate(STEPS_Y):
                a, w = Y_CHUNKS[c]
                reached(dve, 1, "ff_dnmm", 8 * NB - 7 + i)
                tt(H[:, k, a:a + w], PS[:, y_bank(c, k), 0:w], H[:, k, a:a + w], ALU.add).then_inc(S("fin_h"), 1)
                if i:
                    final_gain(i - 1)
                if (c, k - 3) in Y_STATS:
                    final_rstd(Y_STATS[c, k - 3])
                f = Y_FILLS.get((c, k))
                if f is not None and f % 2:
                    y_odd(f)
            final_gain(len(STEPS_Y) - 1)
            for t in range(3, RT):
                y_odd(2 * t + 1)
                if t == 3:
                    final_rstd(2)

        @block.tensor
        def _(pe):
            pe.wait_ge(S("c_set"), C_IDENT)

            def gains_in():
                pe.wait_ge(S("gain_in"), 16 * 7)
                nc.tensor.transpose(PS[:, 7, 176:176 + P_ROWS6], pnat[0:P_ROWS6, 6, :], ident[0:P_ROWS6, 0:P_ROWS6])
                for g in range(4):
                    last = nc.tensor.transpose(PS[:, 7, 240 + HIST * g:240 + HIST * (g + 1)], hnat[:, g * P:(g + 1) * P],
                                               ident[0:HIST, 0:HIST])
                last.then_inc(S("par_tr"), 1)

            def params_in():
                pe.wait_ge(S("par_in"), 16 * 8)
                pe.wait_ge(S("par_ev"), 2)
                for n in range(6):
                    col = 88 * (n % 4)
                    last = nc.tensor.transpose(PS[:, 6 + n // 4, col:col + 88], pnat[0:88, n, :], ident[0:88, 0:88])
                    if n == 3:
                        last.then_inc(S("par_tr"), 1)
                last.then_inc(S("par_tr"), 1)

            def x_rows(t):
                nr = ROWS[t]
                pe.wait_ge(S(X_IN[t]), 16)
                for j in range(2):
                    f = 2 * t + j
                    if f >= 3:
                        pe.wait_ge(S("x_lo"), f - 2)
                    for i in range(4):
                        k = 4 * j + i
                        last = nc.tensor.transpose(PS[:, 3 + f % 3, i * P:i * P + nr], xnat[0:nr, t, k * P:(k + 1) * P],
                                                   ident[0:nr, 0:nr])
                    last.then_inc(S("x_tr"), 1)

            def to_rows(f):
                g, is_v, a, n = row_fill(f)
                if f >= 2:
                    pe.wait_ge(S("ei_tev"), f - 1)
                if is_v:
                    reached(pe, 0, "in_ev", 4 * g + 4)
                else:
                    reached(pe, 0, "in_rope", 2 * g + 2)
                src = vz_e if is_v else kT[:, g, :]
                for i in range(n):
                    t = a + i
                    last = nc.tensor.transpose(PS[0:ROWS[t], 6 + f % 2, i * P:(i + 1) * P], src[:, rows_of(t)], ident[:, :])
                last.then_inc(S("ei_tr"), 1)

            def first_unit():
                for t in range(3):
                    x_rows(t)
                gains_in()
                for t in range(3, 7):
                    x_rows(t)
                reached(pe, 0, "in_lo", 1)
                for c, (a, width) in enumerate(CHUNKS):
                    if c:
                        x_rows(c + 6)
                    pe.wait_ge(S("x_lo"), 6 * (c + 1))
                    for k in range(KT):
                        hi, lo = xn0[0][:, k, a:a + width], xn0[1][:, k, a:a + width]
                        for n, (w, x) in enumerate(((whi, hi), (whi, lo), (wlo, hi))):
                            last = nc.tensor.matmul(PS[:, c, 0:width], w[:, 0, k, :], x,
                                                    start=(k == 0 and n == 0), stop=(k == KT - 1 and n == 2))
                last.then_inc(S("in_mm"), 1)

            def even_unit(u):
                s = u % 2
                reached(pe, 0, "in_lo", u + 1)
                if u >= 2:
                    reached(pe, 0, "in_ev", u - 1)
                after = norm_bcast_after(pe, 0) if u == 1 else None
                for k in range(KT):
                    last = products(s, k, KT, whi[:, s, k, :], wlo[:, s, k, :], xn0[0][:, k, :], xn0[1][:, k, :])
                    if after:
                        after(k)
                last.then_inc(S("in_mm"), 1)

            first_unit()
            for u in range(1, 16):
                if u == 1:
                    params_in()
                even_unit(u)
                for f in row_fills_after(u):
                    to_rows(f)

            def pool_product(n):
                g = POOL_ORDER[n]
                pe.wait_ge(S("pm_plo"), n + 1)
                if n >= 2:
                    pe.wait_ge(S("pm_ev"), n - 1)
                products(n % 2, 0, 1, pwhi[:, g, :], pwlo[:, g, :],
                         xn0[0][:, 4 + g, :], xn0[1][:, 4 + g, :]).then_inc(S("pm_mm"), 1)

            pe.wait_ge(S("pw_lo"), 1)
            for f in range(20, 24):
                to_rows(f)
            for n in range(4):
                pool_product(n)
            pe.wait_ge(S("ei_tev"), 24)
            pe.wait_ge(S("ei_ue"), 4)
            for st in range(2):
                for g in range(4):
                    last = nc.tensor.transpose(PS[0:HIST, 6 + st, g * P:(g + 1) * P], ue[:, g, st, :], ident[:, :])
            last.then_inc(S("ue_tr"), 1)
            pe.wait_ge(S("kc_in"), 16)
            pe.wait_ge(S("pm_ev"), 4)
            for b in range(2):
                for h in range(A_H):
                    last = nc.tensor.transpose(PS[:, 4 + b, h * P:(h + 1) * P], kcn[:, b, h * P:(h + 1) * P], ident[:, :])
                last.then_inc(S("kc_tr"), 1)

            def scores(p):
                t, h = PAIRS[p]
                nq, L = ROWS[t], KEYS[t]
                for m in range(2):
                    before = p if p and (two_banks(p) or two_banks(p - 1)) else p - 1
                    if before > 0:
                        pe.wait_ge(S(f"at_exp{m}"), before)
                    half = slice(64 * m, 64 * m + 64)
                    for a in range(0, L, 512):
                        w = min(512, L - a)
                        masked = t < 8 and a + w == L
                        out = PS[0:nq, 2 * m + (a // 512 if two_banks(p) else p % 2), 0:w]
                        keys = kT[half, h, a:a + w] if t < 8 else kAll[half, h, a:a + w]
                        last = nc.tensor.matmul(out, qT[half, h, rows_of(t)], keys, start=True, stop=not masked)
                        if masked:
                            last = nc.tensor.matmul(out[:, w - 64:w], maskL[half, :], maskR[half, 0, 192:256],
                                                    start=False, stop=True)
                    last.then_inc(S(f"at_s{m}"), 1)

            def probs(p):
                t, h = PAIRS[p]
                nq = ROWS[t]
                pe.wait_ge(S("at_comb"), p + 1)
                for j, (f, n) in enumerate(FILLS[t]):
                    F = FIRST_FILL[p] + j
                    if F >= 2:
                        pe.wait_ge(S("at_tev"), F - 1)
                    for i in range(n):
                        a, w = BLOCKS[t][f + i]
                        last = nc.tensor.transpose(PS[0:w, 4 + F % 2, i * P:i * P + nq], comb[0:nq, p % 2, a:a + w], ident[0:nq, 0:nq])
                    last.then_inc(S("at_tr"), 1)

            def values(p):
                t, h = PAIRS[p]
                nq = ROWS[t]
                pe.wait_ge(S("at_tev"), FIRST_FILL[p + 1])
                if p >= 2:
                    pe.wait_ge(S("at_o"), p - 1)
                n = len(BLOCKS[t])
                for b, (a, w) in enumerate(BLOCKS[t]):
                    if t < 8:
                        v = vN[0:w, b, h * P:(h + 1) * P]
                    else:
                        v = vcn[:, b, h * P:(h + 1) * P] if b < 2 else vN[0:DEC, 8, h * P:(h + 1) * P]
                    last = nc.tensor.matmul(PS[0:nq, 6 + p % 2, 0:P], AT[0:w, p % 2, b * P:b * P + nq], v,
                                            start=b == 0, stop=b == n - 1)
                last.then_inc(S("at_pv"), 1)

            pe.wait_ge(S("c_set"), C_ALL)
            for p in range(NP_ + 2):
                if p < NP_:
                    scores(p)
                if p >= 2:
                    if p == 2:
                        pe.wait_ge(S("ue_ev"), 1)
                        pe.wait_ge(S("vc_in"), 16)
                    values(p - 2)
                if 1 <= p <= NP_:
                    if p == 1:
                        pe.wait_ge(S("kc_ev"), 3)
                    probs(p - 1)
            for t in range(RT):
                nr = ROWS[t]
                if t % 3:
                    pe.wait_ge(S("so_n_pool"), t - t // 3)
                else:
                    pe.wait_ge(S("so_n"), t // 3 + 1)
                if t >= 2:
                    pe.wait_ge(S("so_lo"), t - 1)
                for h in range(A_H):
                    last = nc.tensor.transpose(PS[:, 4 + t % 2, h * P:h * P + nr], oN[0:nr, t, h, :], ident[0:nr, 0:nr])
                last.then_inc(S("so_tr"), 1)
                if t == 0:
                    pe.wait_ge(S("op_lo"), 1)
                if t < 4:
                    k = OUTP[0]["ks"][t]
                    last = products(0, t, KT, whi_op[0][:, 0, k, :], wlo_op[0][:, 0, k, :], xn0[0][:, k, :], xn0[1][:, k, :])
                    if t == 3:
                        last.then_inc(S("op_mid"), 1)
            pe.wait_ge(S("so_lo"), RT)

            def out_projection(o):
                t, l, x = o["tag"], o["l"], o["x"]
                c0 = 8 * (o["n"] - 1)

                def unit(u, s, hi, lo, free):
                    reached(pe, l, f"{t}_lo", u + 1)
                    if free is not None:
                        pe.wait_ge(S("fin_h"), free)
                    for n, k in enumerate(o["ks"]):
                        if l == 0 and isinstance(u, int) and u == 0 and n < 4:
                            continue
                        last = products(s, n, KT, hi[:, s, k, :], lo[:, s, k, :], x[0][:, k, :], x[1][:, k, :])
                        if n == 3:
                            last.then_inc(S(f"{t}_mid"), 1)
                    last.then_inc(S(f"{t}_mm"), 1)

                for s in range(2):
                    unit(s, s, whi_op[l], wlo_op[l], None)
                with pe.Fori(1, 4) as j:
                    for s in range(2):
                        unit(2 * j + s, s, whi, wlo, c0 + 2 * j + s - 1)

            def ffn(f):
                t, b, l, x = f["tag"], f["b"], f["l"], f["x"]

                def up(s, ps, count, after=None):
                    reached(pe, l, f"{t}_uplo", count)
                    for k in range(KT):
                        last = products(ps, k, KT, b.uphi[:, s, k, :], b.uplo[:, s, k, :], x[0][:, k, :], x[1][:, k, :])
                        if after:
                            after(k)
                    last.then_inc(S(f"{t}_upmm"), 1)

                def first_gate():
                    reached(pe, l, f"{t}_uplo", 1)
                    for k in range(KT):
                        pe.wait_ge(S("fin_lo"), 8 * f["l"] * 2 + k + 1)
                        last = products(0, k, KT, b.uphi[:, 0, k, :], b.uplo[:, 0, k, :], x[0][:, k, :], x[1][:, k, :])
                    last.then_inc(S(f"{t}_upmm"), 1)

                def down_products(k, ps, ns):
                    c = slice(k * P, (k + 1) * P)
                    for n in ns:
                        last = products(ps, n, 2, b.dhi[:, n, c], b.dlo[:, n, c], b.hhi[:, n, :], b.hlo[:, n, :])
                    return last

                def down(i):
                    reached(pe, l, f"{t}_dlo", i)
                    reached(pe, l, f"{t}_hlo", 2 * i)
                    for k in range(KT):
                        if k == 0:
                            reached(pe, l, f"{t}_vext", 2 * i)
                        elif k == 1:
                            reached(pe, l, f"{t}_gext", 2 * i + 1)
                        else:
                            reached(pe, l, f"{t}_dnev", 8 * i - 8 + k - 1)
                        down_products(k, (k + 1) % 2, (0, 1)).then_inc(S(f"{t}_dnmm"), 1)

                def down_last():
                    reached(pe, l, f"{t}_dlo", NB)
                    reached(pe, l, f"{t}_hlo", 2 * NB - 1)
                    for k in range(2):
                        reached(pe, l, f"{t}_{'gv'[k]}ext", 2 * NB)
                        down_products(k, k, (0,))
                    reached(pe, l, f"{t}_hlo", 2 * NB)
                    for k in range(2):
                        down_products(k, k, (1,)).then_inc(S(f"{t}_dnmm"), 1)
                    for k in range(2, KT):
                        pe.wait_ge(S("fin_h"), 8 * f["n"] + k - 1)
                        down_products(k, k % 2, (0, 1)).then_inc(S(f"{t}_dnmm"), 1)

                def edges_to_rows():
                    reached(pe, l, f"{t}_vtap", FT)
                    for a in range(2):
                        last = nc.tensor.transpose(PS[0:4 * FT, 7, a * P:(a + 1) * P],
                                                   edge[:, a, :, :].rearrange("p i t -> p (i t)"), ident[:, :])
                    last.then_inc(S("ed_tr"), 1)

                def chunk_products(c, k, n):
                    a, w = Y_CHUNKS[c]
                    col = slice(k * P, (k + 1) * P)
                    for m, (wt, h) in enumerate(((b.dhi, b.hhi), (b.dhi, b.hlo), (b.dlo, b.hhi))):
                        last = nc.tensor.matmul(PS[:, y_bank(c, k), 0:w], wt[:, n, col], h[:, n, a:a + w],
                                                start=(n == 0 and m == 0), stop=(n == 1 and m == 2))
                    return last

                def y_fill(f):
                    t, j = f // 2, f % 2
                    pe.wait_ge(S("fin_g"), 8 * (t // 3) + 8)
                    if f >= 3:
                        before = f - 3
                        pe.wait_ge(S("y_dve") if before % 2 else S("y_act"), before // 2 + 1)
                    for i in range(4):
                        last = nc.tensor.transpose(PS[0:ROWS[t], Y_BANKS[f % 3], i * P:(i + 1) * P], H[:, 4 * j + i, rows_of(t)],
                                                   ident[:, :])
                    last.then_inc(S("y_tr"), 1)

                def down_last_chunks():
                    reached(pe, l, f"{t}_dlo", NB)
                    reached(pe, l, f"{t}_hlo", 2 * NB - 1)
                    reached(pe, l, f"{t}_gext", 2 * NB)
                    for k in range(6):
                        if k == 3:
                            reached(pe, l, f"{t}_vext", 2 * NB)
                        chunk_products(0, k, 0)
                    edges_to_rows()
                    reached(pe, l, f"{t}_hlo", 2 * NB)
                    for c, k in STEPS_Y:
                        if y_free(c, k):
                            pe.wait_ge(S("fin_h"), C_SQ + y_free(c, k))
                        if c or k >= 6:
                            chunk_products(c, k, 0)
                        chunk_products(c, k, 1).then_inc(S(f"{t}_dnmm"), 1)
                        if (c, k) in Y_STATS:
                            final_pe_stats(pe, Y_STATS[c, k])
                        if (c, k) in Y_FILLS:
                            if Y_FILLS[c, k] == 2:
                                pe.wait_ge(S("ed_ev"), 2)
                            y_fill(Y_FILLS[c, k])
                    for f in range(6, 2 * RT):
                        if f == 9:
                            final_pe_stats(pe, 2)
                        y_fill(f)

                def last_value():
                    reached(pe, l, f"{t}_uplo", 4 * NB)
                    for c, (a, width) in enumerate(CHUNKS):
                        for k in range(KT):
                            hi, lo = x[0][:, k, a:a + width], x[1][:, k, a:a + width]
                            for n, (w, y) in enumerate(((b.uphi, hi), (b.uphi, lo), (b.uplo, hi))):
                                last = nc.tensor.matmul(PS[:, 3 + c, 0:width], w[:, 1, k, :], y,
                                                        start=(k == 0 and n == 0), stop=(k == KT - 1 and n == 2))
                        if c >= 1:
                            last.then_inc(S(f"{t}_upmm"), 1)

                def rest(i, first, last=False):
                    if not first:
                        reached(pe, l, f"{t}_dnev", 8 * i - 1)
                    up(1, 1, 4 * i + 2, norm_bcast_after(pe, f["n"]) if first else None)
                    if first:
                        reached(pe, l, f"{t}_gext", 1)
                    else:
                        reached(pe, l, f"{t}_dnev", 8 * i)
                    up(0, 0, 4 * i + 3)
                    reached(pe, l, f"{t}_vext", 2 * i + 1)
                    if last:
                        last_value()
                    else:
                        up(1, 1, 4 * i + 4)

                c0 = 8 * f["n"]
                pe.wait_ge(S("fin_h"), c0 - 1)
                first_gate()
                norm_pe_stats(pe, f["n"])
                pe.wait_ge(S("fin_h"), c0)
                rest(0, True)
                def block_(i, last):
                    reached(pe, l, f"{t}_gext", 2 * i)
                    up(0, 0, 4 * i + 1)
                    down(i)
                    rest(i, False, last)

                with pe.Fori(1, NB - 1) as i:
                    block_(i, False)
                block_(NB - 1, True)
                if l == 0:
                    down_last()
                    edges_to_rows()
                else:
                    down_last_chunks()

            out_projection(OUTP[0])
            ffn(FFN[0])

            def odd_unit(u, s, free, after=None):
                reached(pe, 1, "in_lo", u + 1)
                if free is not None:
                    reached(pe, 1, "in_ev", free)
                for k in range(KT):
                    if free is None:
                        pe.wait_ge(S("fin_lo"), 8 + k + 1)
                    last = products(s, k, KT, whi[:, s, k, :], wlo[:, s, k, :], xn1[0][:, k, :], xn1[1][:, k, :])
                    if after:
                        after(k)
                last.then_inc(S("in_mm"), 1)

            pe.wait_ge(S("fin_h"), 15)
            odd_unit(0, 0, None)
            norm_pe_stats(pe, 2)
            pe.wait_ge(S("fin_h"), 16)
            pe.wait_ge(S("ed_ev"), 1)
            odd_unit(1, 1, None, norm_bcast_after(pe, 2))
            odd_unit(2, 0, 1)
            reached(pe, 1, "in_rope", 1)
            pe.wait_ge(S("n_rb"), 9)
            nc.tensor.transpose(PS[:, 6, 0:P], k_o[:, 7 * P:8 * P], ident[:, :])
            nc.tensor.transpose(PS[0:DEC, 6, P:2 * P], k_o[:, SEQ:R], ident[:, :]).then_inc(S("oi_ktr"), 1)
            pe.wait_ge(S("kc_in"), 32)
            nc.tensor.transpose(PS[:, 7, 0:P], kc2n[:, :], ident[:, :]).then_inc(S("kc2_tr"), 1)
            odd_unit(3, 1, 2)
            pe.wait_ge(S("oi_vz"), 1)
            pe.wait_ge(S("oi_kds"), 1)
            for j, (a, n) in enumerate(((0, 4), (4, 4), (8, 1))):
                if j == 2:
                    pe.wait_ge(S("oi_vn"), 1)
                for i in range(n):
                    t = a + i
                    last = nc.tensor.transpose(PS[0:ROWS[t], 6 + j % 2, i * P:(i + 1) * P], vz_o[:, rows_of(t)], ident[:, :])
                last.then_inc(S("oi_vtr"), 1)
            with pe.Fori(2, 5) as j:
                for s in range(2):
                    odd_unit(2 * j + s, s, 2 * j + s - 1)

            def odd_scores(q):
                t, b = BATCHES[q]
                nq, (c0, c1), v = ROWS[t], WIN[t], q % 2
                if q < 4:
                    reached(pe, 1, "in_rope", 2 * b + 3)
                if q >= 2:
                    pe.wait_ge(S("o_exp"), q - 1)
                for jj in range(2):
                    for par_ in range(2):
                        half = slice(64 * par_, 64 * par_ + 64)
                        if t < 8:
                            keys = kd[half, b // 2, (t - 1) * P + c0:(t - 1) * P + c1]
                        else:
                            keys = kds[half, b // 2, 0:c1]
                        last = nc.tensor.matmul(PS[0:nq, 2 * v + par_, jj * 256 + c0:jj * 256 + c1], q2T[half, 2 * b + jj, rows_of(t)],
                                                keys, start=jj == 0, stop=t == 8 and jj == 1, skip_group_check=True)
                if t < 8:
                    for par_ in range(2):
                        half = slice(64 * par_, 64 * par_ + 64)
                        edges = [x.rearrange("p j (e c) -> p j e c", e=4)[:, :, (3 if c0 else 0):4:3, :]
                                 for x in (PS[0:nq, 2 * v + par_, :].rearrange("p (j c) -> p j c", j=2), maskR[half, :, :])]
                        last = nc.tensor.matmul(edges[0], maskL[half, :], edges[1], start=False, stop=True,
                                                skip_group_check=True)
                last.then_inc(S("o_s"), 1)

            def left(q):
                pe.wait_ge(S("o_tev1"), q + 1)
                if q >= 4:
                    pe.wait_ge(S("o_tev0"), q - 3)

            def odd_probs(q):
                t, b = BATCHES[q]
                nq, v = ROWS[t], q % 2
                pe.wait_ge(S("o_exp"), q + 1)
                if q >= 1:
                    left(q - 1)
                for kt in key_tiles(t):
                    bs = DEC if (t == 8 and kt == 1) else P
                    for i in range(4):
                        last = nc.tensor.transpose(PS[0:bs, 4 + kt, i * P:i * P + nq], E2[0:nq, v, i, kt * P:kt * P + bs], ident[0:nq, 0:nq])
                    last.then_inc(S("o_tr"), 1)

            def odd_values(q):
                t, b = BATCHES[q]
                nq, v, g = ROWS[t], q % 2, b // 2
                left(q)
                if q >= 1:
                    pe.wait_ge(S("o_o"), q)
                kts = key_tiles(t)
                for i in range(4):
                    for kt in kts:
                        bs = DEC if (t == 8 and kt == 1) else P
                        if t < 8:
                            vals = v2N[:, t - 1 + kt, g * C_DH:(g + 1) * C_DH]
                        else:
                            vals = (v2N[0:DEC, 8] if kt else vc2[:, :])[:, g * C_DH:(g + 1) * C_DH]
                        last = nc.tensor.matmul(PS[0:nq, 6, i * C_DH:(i + 1) * C_DH], PT2[0:bs, v, kt, i, 0:nq], vals,
                                                start=kt == kts[0], stop=kt == 1)
                last.then_inc(S("o_pv"), 1)

            def odd_rows(f):
                t, j = f // 2, f % 2
                nr = ROWS[t]
                pe.wait_ge(S("o_o"), 2 * f + 2)
                if f >= 1:
                    pe.wait_ge(S("om_lo"), f)
                for i in range(4):
                    k = 4 * j + i
                    last = nc.tensor.transpose(PS[:, 7, i * P:i * P + nr], oN2[0:nr, k * P:(k + 1) * P], ident[0:nr, 0:nr])
                last.then_inc(S("om_tr"), 1)

            pe.wait_ge(S("oi_vn"), 3)
            pe.wait_ge(S("vc_in"), 32)
            reached(pe, 1, "in_ev", 10)
            for q in range(STEPS):
                if q < NQ:
                    odd_scores(q)
                if rows_step(q) is not None:
                    odd_rows(rows_step(q))
                if 1 <= q <= NQ:
                    odd_probs(q - 1)
                if 2 <= q <= NQ + 1:
                    odd_values(q - 2)

            pe.wait_ge(S("om_lo"), 2 * RT)
            out_projection(OUTP[1])
            ffn(FFN[1])


_INS = ["x_prompt", "x_sample", "cache_diff_k", "cache_diff_v", "state_pool", "cache_swa_k", "cache_swa_v",
        "state_ffn_conv", "norm_attn", "norm_ffn", "norm_final", "w_in_even", "w_out_even", "diff_lambda",
        "diff_subln", "pool_w", "pool_scale", "w_in_odd", "b_in_odd", "w_out_odd", "sinks", "w_up", "conv_w",
        "conv_b", "w_down"]
_OUTS = [("y_prompt", (1, SEQ, D)), ("y_sample", (1, DEC, D)),
         ("diff_k_prompt", (1, 1, SEQ, A_H, 2, A_DH)), ("diff_v_prompt", (1, 1, SEQ, A_H, 2 * A_DH)),
         ("pool_prompt", (1, 1, HIST, A_W)),
         ("swa_k_prompt", (1, 1, C_CACHE, C_KV, C_DH)), ("swa_v_prompt", (1, 1, C_CACHE, C_KV, C_DH)),
         ("ffn_conv_prompt", (2, 1, 2, 2 * FF)),
         ("diff_k_sample", (1, 1, DEC, A_H, 2, A_DH)), ("diff_v_sample", (1, 1, DEC, A_H, 2 * A_DH)),
         ("pool_sample", (1, 1, HIST, A_W)),
         ("swa_k_sample", (1, 1, C_CACHE, C_KV, C_DH)), ("swa_v_sample", (1, 1, C_CACHE, C_KV, C_DH)),
         ("ffn_conv_sample", (2, 1, 2, 2 * FF))]


def tables():
    inv = np.float32(10000.0) ** (-np.arange(0, A_DH, 2, dtype=np.float32) / np.float32(A_DH))
    pos = np.concatenate([np.arange(SEQ), PAST + np.arange(DEC)]).astype(np.float32)
    ang = inv[:, None] * pos[None, :]
    cos, sin = np.cos(ang).astype(np.float32), np.sin(ang).astype(np.float32)
    counts = [[1.0 / min(w, t + 1) for t in range(HIST)] for w in WINDOWS]
    return {"cos_t": cos, "sin_t": np.concatenate([-sin, sin]),
            "rcnt_t": np.array(counts, np.float32).reshape(-1)}


def kernel(**inputs):
    import concourse.bacc as bacc
    from concourse.bass_utils import run_bass_kernel_spmd

    nc = bacc.Bacc("TRN2", target_bir_lowering=False, num_devices=1, dynamic_dma_scratch_size=1024)
    arrays, io = {}, {}
    for name in _INS:
        arrays[f"in_{name}"] = np.ascontiguousarray(inputs[name])
    for name, table in tables().items():
        arrays[f"in_{name}"] = table
    for name, a in arrays.items():
        io[name[3:]] = nc.dram_tensor(name, a.shape, mybir.dt.from_np(a.dtype), kind="ExternalInput").ap()
    for name, shape in _OUTS:
        io[name] = nc.dram_tensor(f"out_{name}", shape, F32, kind="ExternalOutput").ap()
    build(nc, io)
    r = run_bass_kernel_spmd(nc, [arrays], core_ids=[0])
    return tuple(r.results[0][f"out_{name}"] for name, _ in _OUTS)
```
